# Optimizing a Trainium2 kernel written in Bass

```python
import math
import jax, jax.numpy as jnp
from jax import lax
import numpy as np
import jax
import jax.numpy as jnp

D_MODEL = 1024
BATCH = 1
SEQ = 256
DEPTH = 2

GRID_W = 64
CTX_LEN = 256
N_MIXERS = 4
EPS = 1e-6
ROPE_THETA = 10000.0
Q_BLOCK = 128

FNET_GROUPS = 8
FNET_GROUP_DIM = D_MODEL // FNET_GROUPS
DIFF_HEAD_DIM = 64
DIFF_HEADS = D_MODEL // (2 * DIFF_HEAD_DIM)
HGRN_EXPAND = 128
HGRN_HEADS = D_MODEL // HGRN_EXPAND
HGRN_HEAD_V = D_MODEL // HGRN_HEADS
HGRN_FORGET_DIM = HGRN_HEADS * HGRN_EXPAND
HGRN_CHUNK = 64
GQA_HEAD_DIM = 128
GQA_Q_HEADS = D_MODEL // GQA_HEAD_DIM
GQA_KV_HEADS = 2
GQA_GROUP = GQA_Q_HEADS // GQA_KV_HEADS
D_FF = -(-8 * D_MODEL // (3 * 256)) * 256
N_FNET_LAYERS = len(range(0, DEPTH, N_MIXERS))
N_DIFF_LAYERS = len(range(1, DEPTH, N_MIXERS))
N_HGRN_LAYERS = len(range(2, DEPTH, N_MIXERS))
N_GQA_LAYERS = len(range(3, DEPTH, N_MIXERS))


def rms_norm(x, gain):
    xf = x.astype(jnp.float32)
    y = xf * lax.rsqrt(jnp.mean(xf * xf, axis=-1, keepdims=True) + EPS)
    return (y * gain.astype(jnp.float32)).astype(x.dtype)

def modulate(h, shift, scale):
    return h * (1.0 + scale) + shift

def swiglu(h, w_in, w_out):
    gate, up = jnp.split(h @ w_in, 2, axis=-1)
    return (jax.nn.silu(gate) * up) @ w_out

def axial_rope_tables(rows, head_dim):
    row = jnp.repeat(jnp.arange(rows, dtype=jnp.float32), GRID_W)
    col = jnp.tile(jnp.arange(GRID_W, dtype=jnp.float32), rows)
    n_freq = head_dim // 4
    inv_freq = ROPE_THETA ** (-jnp.arange(n_freq, dtype=jnp.float32) / n_freq)
    ang = jnp.concatenate([row[:, None] * inv_freq, col[:, None] * inv_freq], axis=-1)
    return jnp.cos(ang), jnp.sin(ang)

def apply_rope(x, cos, sin):
    shape = (cos.shape[0],) + (1,) * (x.ndim - 3) + (cos.shape[1],)
    cos = cos.reshape(shape)
    sin = sin.reshape(shape)
    x1, x2 = jnp.split(x.astype(jnp.float32), 2, axis=-1)
    return jnp.concatenate([x1 * cos - x2 * sin, x1 * sin + x2 * cos], axis=-1).astype(x.dtype)

def sweep_query_blocks(q, attend):
    b, l = q.shape[:2]
    nb = l // Q_BLOCK
    qb = jnp.moveaxis(q.reshape((b, nb, Q_BLOCK) + q.shape[2:]), 1, 0)
    out = lax.map(attend, qb)
    return jnp.moveaxis(out, 0, 1).reshape((b, l) + out.shape[3:])

def fnet_mixer(h_lat, h_ctx, w_out, b_out, need_ctx):
    def mix(h):
        b, l, _ = h.shape
        hg = h.astype(jnp.float32).reshape(b, l, FNET_GROUPS, FNET_GROUP_DIM)
        y = jnp.fft.fftn(hg, axes=(1, 3), norm='ortho').real
        return y.reshape(b, l, D_MODEL).astype(h.dtype) @ w_out + b_out
    return mix(h_lat), (mix(h_ctx) if need_ctx else None)

def diff_attn_core(q, k, v, lam):
    s = jnp.einsum('bqhcd,bkhcd->bhcqk', q.astype(jnp.float32), k.astype(jnp.float32)) * DIFF_HEAD_DIM ** -0.5
    p = jax.nn.softmax(s, axis=-1)
    w = p[:, :, 0] - lam * p[:, :, 1]
    return jnp.einsum('bhqk,bkhe->bqhe', w, v.astype(jnp.float32)).astype(v.dtype)

def diff_attention_mixer(h_lat, h_ctx, w_in, q_gain, k_gain, lam_par, subln_gain, w_out, layer_idx, rows, need_ctx):
    lam_init = 0.8 - 0.6 * math.exp(-0.3 * layer_idx)
    lp = lam_par.astype(jnp.float32)
    lam = jnp.exp(jnp.sum(lp[0] * lp[1])) - jnp.exp(jnp.sum(lp[2] * lp[3])) + lam_init
    cos, sin = axial_rope_tables(rows, DIFF_HEAD_DIM)

    def project(h, with_q):
        b, l, _ = h.shape
        if with_q:
            q, k, v = jnp.split(h @ w_in, 3, axis=-1)
            q = rms_norm(q.reshape(b, l, DIFF_HEADS, 2, DIFF_HEAD_DIM), q_gain)
        else:
            k, v = jnp.split(h @ w_in[:, D_MODEL:], 2, axis=-1)
            q = None
        k = rms_norm(k.reshape(b, l, DIFF_HEADS, 2, DIFF_HEAD_DIM), k_gain)
        return q, k, v.reshape(b, l, DIFF_HEADS, 2 * DIFF_HEAD_DIM)

    def finish(o):
        b, l = o.shape[:2]
        o = rms_norm(o, subln_gain) * (1.0 - lam_init)
        return o.reshape(b, l, D_MODEL) @ w_out

    q_c, k_c, v_c = project(h_ctx, need_ctx)
    q_l, k_l, v_l = project(h_lat, True)
    q_l = apply_rope(q_l, cos, sin)
    k_l = apply_rope(k_l, cos, sin)
    k_all = jnp.concatenate([k_c, k_l], axis=1)
    v_all = jnp.concatenate([v_c, v_l], axis=1)
    o_lat = finish(sweep_query_blocks(q_l, lambda qb: diff_attn_core(qb, k_all, v_all, lam)))
    o_ctx = finish(diff_attn_core(q_c, k_c, v_c, lam)) if need_ctx else None
    return o_lat, o_ctx

def gla_chunk_scan(q, k, v, log_f, s0):
    b, l, h, dk = q.shape
    dv = v.shape[-1]
    n = l // HGRN_CHUNK

    def chunks(t):
        return jnp.moveaxis(t.reshape((b, n, HGRN_CHUNK) + t.shape[2:]), 1, 0)

    lower = jnp.tril(jnp.ones((HGRN_CHUNK, HGRN_CHUNK), dtype=bool))[None, :, :, None, None]

    def step(s, inp):
        qc, kc, vc, gc = inp
        bc = jnp.cumsum(gc, axis=1)
        decay = jnp.exp(jnp.where(lower, bc[:, :, None] - bc[:, None, :], -jnp.inf))
        scores = jnp.einsum('bthk,bshk,btshk->bhts', qc, kc, decay)
        o = jnp.einsum('bhts,bshv->bthv', scores, vc) + jnp.einsum('bthk,bhkv->bthv', qc * jnp.exp(bc), s)
        b_last = bc[:, -1]
        s = jnp.exp(b_last)[..., None] * s + jnp.einsum('bshk,bshv->bhkv', kc * jnp.exp(b_last[:, None] - bc), vc)
        return s, o

    s_fin, o = lax.scan(step, s0, (chunks(q), chunks(k), chunks(v), chunks(log_f)))
    return jnp.moveaxis(o, 0, 1).reshape(b, l, h, dv), s_fin

def hgrn2_mixer(h_lat, h_ctx, w_in, lower_bound, norm_gain, w_out, layer_idx, need_ctx):
    lbs = jnp.cumsum(jax.nn.softmax(lower_bound.astype(jnp.float32), axis=1), axis=1)
    lb = (lbs[:, layer_idx] - lbs[:, 0]).reshape(2, HGRN_HEADS, HGRN_EXPAND)

    def project(h):
        b, l, _ = h.shape
        q, z_fwd, z_bwd, v, g = jnp.split(h @ w_in, 5, axis=-1)
        q = jax.nn.silu(q).reshape(b, l, HGRN_HEADS, HGRN_EXPAND).astype(jnp.float32)
        v = v.reshape(b, l, HGRN_HEADS, HGRN_HEAD_V).astype(jnp.float32)
        log_f = [jnp.log(lb[d] + (1.0 - lb[d]) * jax.nn.sigmoid(z.reshape(b, l, HGRN_HEADS, HGRN_EXPAND).astype(jnp.float32)))
                 for d, z in enumerate((z_fwd, z_bwd))]
        return q, v, log_f, g

    def run(q, v, lf, s0, reverse):
        if reverse:
            q, v, lf = jnp.flip(q, 1), jnp.flip(v, 1), jnp.flip(lf, 1)
        o, s = gla_chunk_scan(q, -jnp.expm1(lf), v, lf, s0)
        return (jnp.flip(o, 1) if reverse else o), s

    def finish(o, g):
        b, l = o.shape[:2]
        o = rms_norm(o, norm_gain) * jax.nn.silu(g.reshape(b, l, HGRN_HEADS, HGRN_HEAD_V).astype(jnp.float32))
        return o.reshape(b, l, D_MODEL).astype(g.dtype) @ w_out

    q_c, v_c, lf_c, g_c = project(h_ctx)
    q_l, v_l, lf_l, g_l = project(h_lat)
    s0 = jnp.zeros((h_ctx.shape[0], HGRN_HEADS, HGRN_EXPAND, HGRN_HEAD_V), jnp.float32)
    o_ctx_f, s_ctx_f = run(q_c, v_c, lf_c[0], s0, False)
    o_ctx_b, s_ctx_b = run(q_c, v_c, lf_c[1], s0, True)
    o_lat_f, _ = run(q_l, v_l, lf_l[0], s_ctx_f, False)
    o_lat_b, _ = run(q_l, v_l, lf_l[1], s_ctx_b, True)
    o_lat = finish(o_lat_f + o_lat_b, g_l)
    o_ctx = finish(o_ctx_f + o_ctx_b, g_c) if need_ctx else None
    return o_lat, o_ctx

def gqa_core(q, k, v):
    s = jnp.einsum('bqhgd,bkhd->bhgqk', q.astype(jnp.float32), k.astype(jnp.float32)) * GQA_HEAD_DIM ** -0.5
    p = jax.nn.softmax(s, axis=-1)
    return jnp.einsum('bhgqk,bkhd->bqhgd', p, v.astype(jnp.float32)).astype(v.dtype)

def gqa_mixer(h_lat, h_ctx, w_in, q_gain, k_gain, w_out, rows, need_ctx):
    qd = GQA_Q_HEADS * GQA_HEAD_DIM
    cos, sin = axial_rope_tables(rows, GQA_HEAD_DIM)

    def project(h, with_q):
        b, l, _ = h.shape
        if with_q:
            q, kv = jnp.split(h @ w_in, [qd], axis=-1)
            q = rms_norm(q.reshape(b, l, GQA_KV_HEADS, GQA_GROUP, GQA_HEAD_DIM), q_gain)
        else:
            kv = h @ w_in[:, qd:]
            q = None
        k, v = jnp.split(kv, 2, axis=-1)
        k = rms_norm(k.reshape(b, l, GQA_KV_HEADS, GQA_HEAD_DIM), k_gain)
        return q, k, v.reshape(b, l, GQA_KV_HEADS, GQA_HEAD_DIM)

    def finish(o):
        b, l = o.shape[:2]
        return o.reshape(b, l, D_MODEL) @ w_out

    q_c, k_c, v_c = project(h_ctx, need_ctx)
    q_l, k_l, v_l = project(h_lat, True)
    q_l = apply_rope(q_l, cos, sin)
    k_l = apply_rope(k_l, cos, sin)
    k_all = jnp.concatenate([k_c, k_l], axis=1)
    v_all = jnp.concatenate([v_c, v_l], axis=1)
    o_lat = finish(sweep_query_blocks(q_l, lambda qb: gqa_core(qb, k_all, v_all)))
    o_ctx = finish(gqa_core(q_c, k_c, v_c)) if need_ctx else None
    return o_lat, o_ctx

def first_inputs(seed: int = 0) -> dict:
    key = jax.random.key(seed)
    ks = iter(jax.random.split(key, 32))
    D = D_MODEL

    def nrm(shape, scale):
        return jax.random.normal(next(ks), shape, jnp.float32) * scale

    def gain(shape):
        return 1.0 + nrm(shape, 0.05)

    return {
        'x': nrm((BATCH, SEQ, D), 1.0),
        'c': nrm((BATCH, D), 1.0),
        'ctx': nrm((BATCH, CTX_LEN, D), 1.0),
        'c_ctx': nrm((D,), 1.0),
        'w_ada': nrm((DEPTH, D, 6 * D), 0.5 * D ** -0.5),
        'b_ada': nrm((DEPTH, 6 * D), 0.02),
        'norm_gain': gain((DEPTH, 2, D)),
        'ffn_w_in': nrm((DEPTH, D, 2 * D_FF), D ** -0.5),
        'ffn_w_out': nrm((DEPTH, D_FF, D), D_FF ** -0.5),
        'fnet_w_out': nrm((N_FNET_LAYERS, D, D), D ** -0.5),
        'fnet_b_out': nrm((N_FNET_LAYERS, D), 0.02),
        'diff_w_in': nrm((N_DIFF_LAYERS, D, 3 * D), D ** -0.5),
        'diff_q_gain': gain((N_DIFF_LAYERS, 2, DIFF_HEAD_DIM)),
        'diff_k_gain': gain((N_DIFF_LAYERS, 2, DIFF_HEAD_DIM)),
        'diff_lambda': nrm((N_DIFF_LAYERS, 4, DIFF_HEAD_DIM), 0.1),
        'diff_subln_gain': gain((N_DIFF_LAYERS, 2 * DIFF_HEAD_DIM)),
        'diff_w_out': nrm((N_DIFF_LAYERS, D, D), D ** -0.5),
        'hgrn_w_in': nrm((N_HGRN_LAYERS, D, 5 * D), D ** -0.5),
        'hgrn_lower_bound': nrm((2, DEPTH, HGRN_FORGET_DIM), 1.0),
        'hgrn_norm_gain': gain((N_HGRN_LAYERS, HGRN_HEAD_V)),
        'hgrn_w_out': nrm((N_HGRN_LAYERS, D, D), D ** -0.5),
        'gqa_w_in': nrm((N_GQA_LAYERS, D, (GQA_Q_HEADS + 2 * GQA_KV_HEADS) * GQA_HEAD_DIM), D ** -0.5),
        'gqa_q_gain': gain((N_GQA_LAYERS, GQA_HEAD_DIM)),
        'gqa_k_gain': gain((N_GQA_LAYERS, GQA_HEAD_DIM)),
        'gqa_w_out': nrm((N_GQA_LAYERS, D, D), D ** -0.5),
    }

def first_block(x, c, ctx, c_ctx, w_ada, b_ada, norm_gain, ffn_w_in, ffn_w_out, fnet_w_out, fnet_b_out,
              diff_w_in, diff_q_gain, diff_k_gain, diff_lambda, diff_subln_gain, diff_w_out,
              hgrn_w_in, hgrn_lower_bound, hgrn_norm_gain, hgrn_w_out,
              gqa_w_in, gqa_q_gain, gqa_k_gain, gqa_w_out):
    rows = x.shape[1] // GRID_W
    cond_lat = jax.nn.silu(c)[:, None, :]
    cond_ctx = jax.nn.silu(c_ctx)[None, None, :]
    for i in range(DEPTH):
        m, j = i % N_MIXERS, i // N_MIXERS
        need_ctx = i < DEPTH - 1
        sh1, sc1, g1, sh2, sc2, g2 = jnp.split(cond_lat @ w_ada[i] + b_ada[i], 6, axis=-1)
        csh1, csc1, cg1, csh2, csc2, cg2 = jnp.split(cond_ctx @ w_ada[i] + b_ada[i], 6, axis=-1)
        h_lat = modulate(rms_norm(x, norm_gain[i, 0]), sh1, sc1)
        h_ctx = modulate(rms_norm(ctx, norm_gain[i, 0]), csh1, csc1) if (need_ctx or m != 0) else None
        if m == 0:
            o_lat, o_ctx = fnet_mixer(h_lat, h_ctx, fnet_w_out[j], fnet_b_out[j], need_ctx)
        elif m == 1:
            o_lat, o_ctx = diff_attention_mixer(h_lat, h_ctx, diff_w_in[j], diff_q_gain[j], diff_k_gain[j], diff_lambda[j],
                                                diff_subln_gain[j], diff_w_out[j], i, rows, need_ctx)
        elif m == 2:
            o_lat, o_ctx = hgrn2_mixer(h_lat, h_ctx, hgrn_w_in[j], hgrn_lower_bound, hgrn_norm_gain[j], hgrn_w_out[j], i, need_ctx)
        else:
            o_lat, o_ctx = gqa_mixer(h_lat, h_ctx, gqa_w_in[j], gqa_q_gain[j], gqa_k_gain[j], gqa_w_out[j], rows, need_ctx)
        x = x + g1 * o_lat
        x = x + g2 * swiglu(modulate(rms_norm(x, norm_gain[i, 1]), sh2, sc2), ffn_w_in[i], ffn_w_out[i])
        if need_ctx:
            ctx = ctx + cg1 * o_ctx
            ctx = ctx + cg2 * swiglu(modulate(rms_norm(ctx, norm_gain[i, 1]), csh2, csc2), ffn_w_in[i], ffn_w_out[i])
    return x


DEPTH_2 = 1

N_META = 16

MLA_HEADS = 8
MLA_NOPE = 128
MLA_ROPE = 64
MLA_V = 128
MLA_Q_RANK = 256
MLA_KV_RANK = 256
MLA_WIDTH = MLA_HEADS * MLA_V
ROPE_BASE = 10000.0

NA_HEADS = 16
NA_HEAD_DIM = 64
NA_WIDTH = NA_HEADS * NA_HEAD_DIM
NA_WIN_R = 8
NA_WIN_C = 16

D_INNER = MLA_WIDTH + NA_WIDTH
IN_SIZES = (MLA_Q_RANK, MLA_KV_RANK, MLA_ROPE, MLA_WIDTH, NA_WIDTH, NA_WIDTH, NA_WIDTH, NA_WIDTH)
D_IN_PROJ = sum(IN_SIZES)


def _rmsnorm(x, w):
    xf = x.astype(jnp.float32)
    y = xf * lax.rsqrt(jnp.mean(xf * xf, axis=-1, keepdims=True) + EPS)
    return (y * w.astype(jnp.float32)).astype(x.dtype)

def _rope(x, cos, sin):
    x1, x2 = jnp.split(x.astype(jnp.float32), 2, axis=-1)
    return jnp.concatenate([x1 * cos - x2 * sin, x2 * cos + x1 * sin], axis=-1).astype(x.dtype)

def _mla(q_lat, kv_lat, k_pe, w_uq, w_ukv, q_lat_w, kv_lat_w, qn_w, qpe_w, kn_w, kpe_w):
    B, L, _ = q_lat.shape
    q = (_rmsnorm(q_lat, q_lat_w) @ w_uq).reshape(B, L, MLA_HEADS, MLA_NOPE + MLA_ROPE)
    kv = (_rmsnorm(kv_lat, kv_lat_w) @ w_ukv).reshape(B, L, MLA_HEADS, MLA_NOPE + MLA_V)
    q_nope, q_pe = q[..., :MLA_NOPE], q[..., MLA_NOPE:]
    k_nope, v = kv[..., :MLA_NOPE], kv[..., MLA_NOPE:]
    q_nope = _rmsnorm(q_nope, qn_w)
    k_nope = _rmsnorm(k_nope, kn_w)
    pos = jnp.arange(L, dtype=jnp.float32)
    inv_freq = ROPE_BASE ** (-(jnp.arange(0, MLA_ROPE, 2, dtype=jnp.float32) / MLA_ROPE))
    ang = pos[:, None] * inv_freq[None, :]
    cos, sin = jnp.cos(ang), jnp.sin(ang)
    q_pe = _rope(_rmsnorm(q_pe, qpe_w), cos[None, :, None, :], sin[None, :, None, :])
    k_pe = _rope(_rmsnorm(k_pe, kpe_w), cos[None], sin[None])
    scale = (MLA_NOPE + MLA_ROPE) ** -0.5

    n_blk = -(-L // Q_BLOCK)
    pad = n_blk * Q_BLOCK - L
    qn = jnp.pad(q_nope, ((0, 0), (0, pad), (0, 0), (0, 0)))
    qn = qn.reshape(B, n_blk, Q_BLOCK, MLA_HEADS, MLA_NOPE).transpose(1, 0, 2, 3, 4)
    qp = jnp.pad(q_pe, ((0, 0), (0, pad), (0, 0), (0, 0)))
    qp = qp.reshape(B, n_blk, Q_BLOCK, MLA_HEADS, MLA_ROPE).transpose(1, 0, 2, 3, 4)

    def block(args):
        qn_b, qp_b = args
        s = (jnp.einsum('bqhd,bkhd->bhqk', qn_b, k_nope)
             + jnp.einsum('bqhr,bkr->bhqk', qp_b, k_pe))
        p = jax.nn.softmax(s.astype(jnp.float32) * scale, axis=-1).astype(v.dtype)
        return jnp.einsum('bhqk,bkhd->bqhd', p, v)

    o = lax.map(block, (qn, qp))
    o = o.transpose(1, 0, 2, 3, 4).reshape(B, n_blk * Q_BLOCK, MLA_WIDTH)
    return o[:, :L]

def _na(q, k, v, q_w, k_w, rel_bias, meta_bias):
    B, L, _ = q.shape
    n_real = L - N_META
    rows = n_real // GRID_W
    win_r = min(NA_WIN_R, rows)
    n_win = win_r * NA_WIN_C
    scale = NA_HEAD_DIM ** -0.5
    q = _rmsnorm(q.reshape(B, L, NA_HEADS, NA_HEAD_DIM), q_w)
    k = _rmsnorm(k.reshape(B, L, NA_HEADS, NA_HEAD_DIM), k_w)
    v = v.reshape(B, L, NA_HEADS, NA_HEAD_DIM)
    q_meta, k_meta, v_meta = q[:, :N_META], k[:, :N_META], v[:, :N_META]
    q_grid = q[:, N_META:].reshape(B, rows, GRID_W, NA_HEADS, NA_HEAD_DIM)
    k_grid = k[:, N_META:].reshape(B, rows, GRID_W, NA_HEADS, NA_HEAD_DIM)
    v_grid = v[:, N_META:].reshape(B, rows, GRID_W, NA_HEADS, NA_HEAD_DIM)

    cols = np.arange(GRID_W)
    c0 = np.clip(cols - NA_WIN_C // 2, 0, GRID_W - NA_WIN_C)
    col_idx_np = c0[:, None] + np.arange(NA_WIN_C)[None, :]
    col_idx = jnp.asarray(col_idx_np, dtype=jnp.int32)
    dc_idx = jnp.asarray(col_idx_np - cols[:, None] + (NA_WIN_C - 1), dtype=jnp.int32)
    meta_b = meta_bias.astype(jnp.float32)[None, :, None, :]

    def row_block(args):
        r, q_row = args
        r0 = jnp.clip(r - win_r // 2, 0, rows - win_r)
        k_rows = lax.dynamic_slice_in_dim(k_grid, r0, win_r, axis=1)
        v_rows = lax.dynamic_slice_in_dim(v_grid, r0, win_r, axis=1)
        k_win = k_rows[:, :, col_idx]
        v_win = v_rows[:, :, col_idx]
        dr_idx = r0 + jnp.arange(win_r, dtype=jnp.int32) - r + (NA_WIN_R - 1)
        bias = rel_bias[:, dr_idx[None, :, None], dc_idx[:, None, :]]
        s_win = (jnp.einsum('bqhd,brqchd->bhqrc', q_row, k_win).astype(jnp.float32) * scale
                 + bias.astype(jnp.float32)[None])
        s_meta = jnp.einsum('bqhd,bmhd->bhqm', q_row, k_meta).astype(jnp.float32) * scale + meta_b
        s = jnp.concatenate([s_win.reshape(B, NA_HEADS, GRID_W, n_win), s_meta], axis=-1)
        p = jax.nn.softmax(s, axis=-1).astype(v.dtype)
        p_win = p[..., :n_win].reshape(B, NA_HEADS, GRID_W, win_r, NA_WIN_C)
        p_meta = p[..., n_win:]
        return (jnp.einsum('bhqrc,brqchd->bqhd', p_win, v_win)
                + jnp.einsum('bhqm,bmhd->bqhd', p_meta, v_meta))

    o_grid = lax.map(row_block, (jnp.arange(rows, dtype=jnp.int32), q_grid.transpose(1, 0, 2, 3, 4)))
    o_real = o_grid.transpose(1, 0, 2, 3, 4).reshape(B, n_real, NA_WIDTH)

    s_mm = jnp.einsum('bqhd,bmhd->bhqm', q_meta, k_meta).astype(jnp.float32) * scale + meta_b
    p_mm = jax.nn.softmax(s_mm, axis=-1).astype(v.dtype)
    o_meta = jnp.einsum('bhqm,bmhd->bqhd', p_mm, v_meta).reshape(B, N_META, NA_WIDTH)
    return jnp.concatenate([o_meta, o_real], axis=1)

def second_inputs(seed: int = 0) -> dict:
    key = jax.random.key(seed)
    ks = jax.random.split(key, 20)
    f32 = jnp.float32

    def nrm(k, shape, scale):
        return jax.random.normal(k, shape, f32) * scale

    def gain(k, shape):
        return 1.0 + 0.05 * jax.random.normal(k, shape, f32)

    return {
        "x": jax.random.normal(ks[0], (BATCH, SEQ, D_MODEL), f32),
        "meta_tokens": nrm(ks[1], (N_META, D_MODEL), 1.0),
        "norm_w": gain(ks[2], (DEPTH_2, D_MODEL)),
        "w_in": nrm(ks[3], (DEPTH_2, D_MODEL, D_IN_PROJ), D_MODEL ** -0.5),
        "q_lat_norm_w": gain(ks[4], (DEPTH_2, MLA_Q_RANK)),
        "kv_lat_norm_w": gain(ks[5], (DEPTH_2, MLA_KV_RANK)),
        "w_uq": nrm(ks[6], (DEPTH_2, MLA_Q_RANK, MLA_HEADS * (MLA_NOPE + MLA_ROPE)), MLA_Q_RANK ** -0.5),
        "w_ukv": nrm(ks[7], (DEPTH_2, MLA_KV_RANK, MLA_HEADS * (MLA_NOPE + MLA_V)), MLA_KV_RANK ** -0.5),
        "mla_qn_w": gain(ks[8], (DEPTH_2, MLA_NOPE)),
        "mla_qpe_w": gain(ks[9], (DEPTH_2, MLA_ROPE)),
        "mla_kn_w": gain(ks[10], (DEPTH_2, MLA_NOPE)),
        "mla_kpe_w": gain(ks[11], (DEPTH_2, MLA_ROPE)),
        "na_q_norm_w": gain(ks[12], (DEPTH_2, NA_HEAD_DIM)),
        "na_k_norm_w": gain(ks[13], (DEPTH_2, NA_HEAD_DIM)),
        "na_rel_bias": nrm(ks[14], (DEPTH_2, NA_HEADS, 2 * NA_WIN_R - 1, 2 * NA_WIN_C - 1), 0.5),
        "na_meta_bias": nrm(ks[15], (DEPTH_2, NA_HEADS, N_META), 0.5),
        "w_out": nrm(ks[16], (DEPTH_2, D_INNER, D_MODEL), D_INNER ** -0.5),
    }

def second_block(x, meta_tokens, norm_w, w_in, q_lat_norm_w, kv_lat_norm_w, w_uq, w_ukv,
              mla_qn_w, mla_qpe_w, mla_kn_w, mla_kpe_w, na_q_norm_w, na_k_norm_w,
              na_rel_bias, na_meta_bias, w_out):
    B = x.shape[0]
    meta = jnp.broadcast_to(meta_tokens.astype(x.dtype)[None], (B, N_META, D_MODEL))
    h_res = jnp.concatenate([meta, x], axis=1)
    split_at = [int(s) for s in np.cumsum(IN_SIZES)[:-1]]
    for l in range(DEPTH_2):
        h = _rmsnorm(h_res, norm_w[l])
        proj = h @ w_in[l]
        q_lat, kv_lat, k_pe, g_mla, na_q, na_k, na_v, g_na = jnp.split(proj, split_at, axis=-1)
        y_mla = _mla(q_lat, kv_lat, k_pe, w_uq[l], w_ukv[l], q_lat_norm_w[l], kv_lat_norm_w[l],
                     mla_qn_w[l], mla_qpe_w[l], mla_kn_w[l], mla_kpe_w[l]) * jax.nn.silu(g_mla)
        y_na = _na(na_q, na_k, na_v, na_q_norm_w[l], na_k_norm_w[l],
                   na_rel_bias[l], na_meta_bias[l]) * jax.nn.silu(g_na)
        h_res = h_res + jnp.concatenate([y_mla, y_na], axis=-1) @ w_out[l]
    return h_res[:, N_META:]


def setup_inputs(seed=0):
    out = dict(first_inputs(seed))
    for name, value in second_inputs(seed + 1).items():
        if name != "x":
            out[name + "_2"] = value
    return out


def reference(
    x, c, ctx, c_ctx, w_ada, b_ada, norm_gain, ffn_w_in, ffn_w_out, fnet_w_out, fnet_b_out,
    diff_w_in, diff_q_gain, diff_k_gain, diff_lambda, diff_subln_gain, diff_w_out, hgrn_w_in,
    hgrn_lower_bound, hgrn_norm_gain, hgrn_w_out, gqa_w_in, gqa_q_gain, gqa_k_gain, gqa_w_out,
    meta_tokens_2, norm_w_2, w_in_2, q_lat_norm_w_2, kv_lat_norm_w_2, w_uq_2, w_ukv_2,
    mla_qn_w_2, mla_qpe_w_2, mla_kn_w_2, mla_kpe_w_2, na_q_norm_w_2, na_k_norm_w_2,
    na_rel_bias_2, na_meta_bias_2, w_out_2,
):
    x = first_block(
        x, c, ctx, c_ctx, w_ada, b_ada, norm_gain, ffn_w_in, ffn_w_out, fnet_w_out, fnet_b_out,
        diff_w_in, diff_q_gain, diff_k_gain, diff_lambda, diff_subln_gain, diff_w_out,
        hgrn_w_in, hgrn_lower_bound, hgrn_norm_gain, hgrn_w_out, gqa_w_in, gqa_q_gain,
        gqa_k_gain, gqa_w_out,
    )
    return second_block(
        x, meta_tokens_2, norm_w_2, w_in_2, q_lat_norm_w_2, kv_lat_norm_w_2, w_uq_2, w_ukv_2,
        mla_qn_w_2, mla_qpe_w_2, mla_kn_w_2, mla_kpe_w_2, na_q_norm_w_2, na_k_norm_w_2,
        na_rel_bias_2, na_meta_bias_2, w_out_2,
    )


_drawn_inputs = setup_inputs


def setup_inputs(seed=0):
    import zlib

    import numpy as np

    out = dict(_drawn_inputs(seed))
    spreads = {}
    factors = {'fnet_b_out': 7.473,
     'diff_q_gain': 8.0,
     'diff_k_gain': 8.0,
     'diff_lambda': 2.975,
     'diff_subln_gain': 5.308,
     'norm_w_2': 5.962,
     'q_lat_norm_w_2': 8.0,
     'kv_lat_norm_w_2': 8.0,
     'mla_qn_w_2': 8.0,
     'mla_qpe_w_2': 8.0,
     'mla_kn_w_2': 8.0,
     'mla_kpe_w_2': 8.0,
     'na_q_norm_w_2': 8.0,
     'na_k_norm_w_2': 8.0,
     'na_meta_bias_2': 3.872}
    for name, (base, spread) in spreads.items():
        noise = np.random.default_rng([zlib.crc32(name.encode()), seed]).standard_normal(out[name].shape)
        drawn = base * np.exp(spread * noise) if base else spread * noise
        out[name] = jnp.asarray(drawn.astype(out[name].dtype))
    for name, factor in factors.items():
        out[name] = (out[name] * factor).astype(out[name].dtype)
    return out
```

```python
import math
from contextlib import ExitStack

import numpy as np
import concourse.bass as bass
from concourse import mybir

F32 = mybir.dt.float32
F32R = mybir.dt.float32r
ACT = mybir.ActivationFunctionType
ALU = mybir.AluOpType
AX_X = mybir.AxisListType.X

P = 128
D = 1024
KD = D // P
L = 256
LC = 256
NT = L + LC
GRID_W = 64
ROWS = L // GRID_W
EPS = 1e-6
D_FF = 2816
KF = D_FF // P
DIFF_HEADS = 8
DIFF_DIM = 64
LAM_INIT = 0.8 - 0.6 * math.exp(-0.3 * 1)
N_META = 16
L2 = L + N_META
MLA_HEADS, MLA_NOPE, MLA_ROPE, MLA_V, MLA_RANK = 8, 128, 64, 128, 256
NA_HEADS, NA_DIM, NA_WIN_R, NA_WIN_C = 16, 64, 8, 16
REL_R, REL_C = 2 * NA_WIN_R - 1, 2 * NA_WIN_C - 1
MASKED = -1e30

RAW_SLOTS = 4
SPLIT_SLOTS = 2
SLAB = 2048

IN_QLAT, IN_KVLAT, IN_KPE, IN_GMLA = 0, 256, 512, 576
IN_NAQ, IN_NAK, IN_NAV, IN_GNA = 1600, 2624, 3648, 4672

SLOTS_R = 2 * ROWS - 2
RUN = REL_C * (SLOTS_R - 1) + GRID_W
BIAS_W = N_META + SLOTS_R * GRID_W + N_META


def shape_tables():
    eye = np.eye(P)
    half = np.kron(np.eye(2), np.ones((64, 64)))
    rot = np.zeros((P, P))
    for m in range(P):
        if m % 64 < 32:
            rot[m + 32, m] = -1.0
        else:
            rot[m - 32, m] = 1.0
    g = np.arange(P)
    ang_g = 2 * np.pi * (np.outer(g, g) % P) / P
    t = np.arange(L)
    ang_l = 2 * np.pi * (np.outer(t, t) % L) / L
    norm = 1.0 / math.sqrt(L * P)
    dft_g = np.concatenate([np.cos(ang_g), np.sin(ang_g)], 1)
    cos_l = (np.cos(ang_l) * norm).reshape(2, P, L).transpose(1, 0, 2).reshape(P, 2 * L)
    nsin_l = (-np.sin(ang_l) * norm).reshape(2, P, L).transpose(1, 0, 2).reshape(P, 2 * L)

    f32 = np.float32
    inv = (f32(10000.0) ** (-np.arange(16, dtype=f32) / f32(16))).astype(f32)
    row = np.repeat(np.arange(ROWS, dtype=f32), GRID_W)
    col = np.tile(np.arange(GRID_W, dtype=f32), ROWS)
    ang = np.concatenate([row[:, None] * inv, col[:, None] * inv], -1).astype(f32).T
    ang_d = np.tile(ang, (4, 1))
    inv = (f32(10000.0) ** (-(np.arange(0, MLA_ROPE, 2, dtype=f32) / f32(MLA_ROPE)))).astype(f32)
    pos = np.concatenate([np.arange(N_META, L2), np.arange(N_META)]).astype(f32)
    ang = (pos[:, None] * inv).astype(f32).T
    ang_m = np.tile(ang, (4, 1))

    c = np.arange(P) % GRID_W
    c0 = np.clip(c - NA_WIN_C // 2, 0, GRID_W - NA_WIN_C)[:, None]
    kc = np.arange(GRID_W)[None, :]
    mask = np.where((kc >= c0) & (kc < c0 + NA_WIN_C), 0.0, MASKED)
    return {
        "ident": eye, "ones": np.ones((P, P)), "half": half, "rot": rot,
        "cos_d": np.cos(ang_d), "sin_d": np.sin(ang_d), "cos_m": np.cos(ang_m), "sin_m": np.sin(ang_m),
        "mask": mask, "dft_g": dft_g, "cos_l": cos_l, "nsin_l": nsin_l,
    }


TABLE_COLS = {"ident": P, "ones": P, "half": P, "rot": P, "cos_d": L, "sin_d": L, "cos_m": L2, "sin_m": L2,
              "mask": GRID_W, "dft_g": 2 * P, "cos_l": 2 * L, "nsin_l": 2 * L}
KEPT = 4 * P + 2 * L + 2 * L2 + GRID_W
FOURIER = 2 * P + 4 * L

PAR_ROWS = {"norm_gain": 4 * KD, "fnet_b": KD, "norm_w": KD, "q_lat": 2, "kv_lat": 2, "subln": 1, "dq": 1,
            "dk": 1, "qn": 1, "kn": 1, "qpe": 1, "kpe": 1, "naq": 1, "nak": 1, "lam_a": 1, "lam_b": 1,
            "c": KD, "c_ctx": KD}
PAR_AT = {}
for _name, _n in PAR_ROWS.items():
    PAR_AT[_name] = sum(PAR_ROWS[x] for x in list(PAR_ROWS)[:list(PAR_ROWS).index(_name)])
N_PAR = sum(PAR_ROWS.values())
N_ADA = 2 * 6 * KD


def slab_starts():
    stages = [("ada0", 24), ("fnet_out", 4), ("ffn0_in", 44), ("ffn0_out", 11), ("ada1_tail", 2),
              ("diff_k", 4), ("diff_q", 4), ("diff_v", 4), ("diff_out", 4), ("ffn1_in", 22), ("ffn1_out", 11),
              ("lat", 2), ("kpe", 1), ("uq", 2), ("ukv", 2), ("gmla", 4),
              ("naq", 4), ("nak", 4), ("nav", 4), ("gna", 4), ("out2", 8)]
    at, out = 0, {}
    for name, n in stages:
        out[name] = at
        at += n
    out["end"] = at
    return out


G = slab_starts()


def build(nc, d, out):
    with ExitStack() as ctx:
        def sb(name, shape, dt=F32):
            return ctx.enter_context(nc.sbuf_tensor(name, shape, dt))

        def sem(name):
            return ctx.enter_context(nc.semaphore(name))

        ps = ctx.enter_context(nc.psum_tensor("ps", [P, 8, 512], F32))
        x_lat = sb("x_lat", [P, KD, L])
        x_ctx = sb("x_ctx", [P, KD, LC])
        x_meta = sb("x_meta", [P, KD, N_META])
        HW = L2 + L
        hh = sb("hh", [P, KD, HW], F32R)
        hl = sb("hl", [P, KD, HW], F32R)
        ah = sb("ah", [P, 2, HW], F32R)
        al = sb("al", [P, 2, HW], F32R)
        raw = sb("raw", [P, RAW_SLOTS, SLAB])
        wh = sb("wh", [P, SPLIT_SLOTS, SLAB], F32R)
        wl = sb("wl", [P, SPLIT_SLOTS, SLAB], F32R)
        big = sb("big", [P, 13824])
        tab = sb("tab", [P, KEPT])
        ex = sb("ex", [P, 2, 2, 512])
        sq = sb("sq", [P, 2, 512])
        rstd = sb("rstd", [P, 2, 512])
        nrm = sb("nrm", [P, 2, 512])
        t1 = sb("t1", [P, L2])
        rows = big[:, 12000:12000 + 2 * P]
        par = sb("par", [P, N_ADA + N_PAR])
        ada = sb("ada", [P, 2, 6 * KD, 2])
        ada_lo = sb("ada_lo", [P, 4, 2])
        gsc = sb("gsc", [P, 2, 2, KD, 2])
        gb = sb("gb", [P, KD, 2])
        cond = sb("cond", [P, 2 * KD])
        condr = sb("condr", [P, KD, 4], F32R)
        eps_c = sb("eps_c", [P, 1])
        sml = sb("sml", [P, 16])
        mx = sb("mx", [P, 2, 2])
        nm = sb("nm", [P, 2, 2])
        sm = sb("sm", [P, 2, 2])
        rc = sb("rc", [P, 2, 2])
        meta_b = sb("meta_b", [P, NA_HEADS * N_META])
        subg = sb("subg", [P, 1])

        T, at = {}, 0
        for name in list(TABLE_COLS)[:9]:
            T[name] = tab[:, at:at + TABLE_COLS[name]]
            at += TABLE_COLS[name]

        def view(at, n, pattern=None, **kw):
            v = big[:, at:at + n]
            return v.rearrange(pattern, **kw) if pattern else v

        xin = view(0, 4096, "p (t d) -> p t d", t=4)
        h32 = view(4096, 4096, "p (k n) -> p k n", k=KD)
        uv = view(8192, 2048, "p (s t c) -> p s t c", s=2, t=4)
        dft_g = view(10240, 2 * P)
        cos_l = view(10240 + 2 * P, 2 * L, "p (t n) -> p t n", t=2)
        nsin_l = view(10240 + 2 * P + 2 * L, 2 * L, "p (t n) -> p t n", t=2)
        dq = view(0, 2048, "p (h n) -> p h n", h=8)
        dk = view(2048, 4096, "p (h n) -> p h n", h=8)
        dv = view(6144, 4096, "p (t e) -> p t e", t=4)
        qn = view(0, 2048, "p (h n) -> p h n", h=8)
        qp = view(2048, 2048, "p (h n) -> p h n", h=8)
        kn = view(4096, 8 * L2, "p (h n) -> p h n", h=8)
        kp = view(6272, L2)
        mv = view(6544, 3072, "p (t e) -> p t e", t=3)
        mg = view(9616, 2048, "p (h n) -> p h n", h=8)
        lat32 = ex[:].rearrange("p a b c -> p (a b c)")[:, 0:2 * HW].rearrange("p (k n) -> p k n", k=2)
        nq = view(0, 2048, "p (h n) -> p h n", h=8)
        nkx = view(2048, 8 * (L2 + N_META), "p (h n) -> p h n", h=8)
        nv = view(4352, 3072, "p (t e) -> p t e", t=3)
        ng = view(7424, 2048, "p (h n) -> p h n", h=8)
        runs = view(9472, NA_HEADS * RUN, "p (h n) -> p h n", h=NA_HEADS)
        bias = view(12976, 2 * BIAS_W, "p (s n) -> p s n", s=2)
        wT = x_ctx[:].rearrange("p k n -> p (k n)").rearrange("p (s c n) -> p s c n", s=2, c=4)

        def par_of(name, k=0, n=1):
            at = N_ADA + PAR_AT[name] + k
            return par[:, at:at + n]

        s_rows = sem("rows_landed")
        s_tab = sem("tables_landed")
        s_xin = sem("x_landed")
        landed = [sem(f"slab_landed_{i}") for i in range(RAW_SLOTS)]
        rounded = sem("slab_rounded")
        split = sem("slab_split")
        used = sem("slab_used")
        s_turn = sem("turned")
        s_turn_a = sem("turned_out_act")
        s_turn_v = sem("turned_out_dve")
        s_cond = sem("cond_ready")
        s_ada = sem("ada_pair_done")
        s_adav = sem("ada_pair_out")
        s_mod = sem("modulation_ready")
        a_ch = sem("act_chain")
        v_ch = sem("dve_chain")
        s_sq = sem("norm_squared")
        s_sum = sem("norm_summed")
        s_rstd = sem("norm_rstd")
        s_mul = sem("norm_scaled")
        s_hh = sem("norm_rounded")
        s_h = sem("norm_out")
        s_f1 = sem("fnet_inner")
        s_f1a = sem("fnet_inner_out_act")
        s_f1v = sem("fnet_inner_out_dve")
        s_f2 = sem("fnet_outer")
        s_f2a = sem("fnet_rounded")
        s_f2v = sem("fnet_split")
        s_op = sem("outproj_done")
        s_opa = sem("outproj_biased")
        s_x = sem("x_updated")
        s_gate = sem("gate_done")
        s_silu = sem("gate_silu")
        s_up = sem("up_done")
        s_act = sem("act_written")
        s_ar = sem("act_rounded")
        s_as = sem("act_split")
        s_au = sem("act_used")
        s_ffn = sem("ffn_out_done")
        s_unit = sem("unit_done")
        s_usq = sem("unit_squared")
        s_usum = sem("unit_summed")
        s_urs = sem("unit_rstd")
        s_unrm = sem("unit_normed")
        s_urot = sem("unit_rotated")
        s_ucp = sem("unit_copied")
        s_urdy = sem("unit_ready")
        s_sc = sem("scores_done")
        s_sb = sem("scores_biased")
        s_mx = sem("row_max")
        s_ex = sem("exp_done")
        s_w = sem("weights_ready")
        s_tr = sem("weights_turned")
        s_trc = sem("weights_copied")
        s_pv = sem("pv_done")
        s_osq = sem("o_squared")
        s_osum = sem("o_summed")
        s_ors = sem("o_rstd")
        s_on = sem("o_scaled")
        s_or = sem("o_rounded")
        s_os = sem("o_split")
        s_bias = sem("bias_ready")
        s_runs = sem("bias_runs_landed")
        s_metab = sem("meta_bias_landed")
        s_fin = sem("final_done")
        s_fo = sem("final_copied")
        s_out = sem("out_stored")
        s_eps = sem("eps_written")

        def positive(eng, s, value):
            if type(value) is int and value <= 0:
                return
            eng.wait_ge(s, value)

        def round_slab(act, g, at, n=SLAB):
            turn = g - at
            act.wait_ge(landed[at % RAW_SLOTS], 4 * turn + 16 * (at // RAW_SLOTS + 1))
            positive(act, used, g - SPLIT_SLOTS + 1)
            nc.scalar.activation(wh[:, at % SPLIT_SLOTS, 0:n], raw[:, at % RAW_SLOTS, 0:n],
                                 ACT.Copy).then_inc(rounded, 1)

        def split_slab(dve, g, at, n=SLAB):
            dve.wait_ge(rounded, g + 1)
            s = at % SPLIT_SLOTS
            nc.vector.tensor_tensor(wl[:, s, 0:n], raw[:, at % RAW_SLOTS, 0:n], wh[:, s, 0:n].bitcast(F32),
                                    ALU.subtract).then_inc(split, 1)

        def load_slab(sp, g, at, src, k, n):
            positive(sp, split, g - RAW_SLOTS + 1)
            sp.dma_start(raw[:, at % RAW_SLOTS, 0:k * n].rearrange("p (k n) -> p k n", k=k),
                         src.rearrange("(k p) n -> p k n", p=P)).then_inc(landed[at % RAW_SLOTS], 16)

        def slab_view(which, at, k, n):
            return which[:, at % SPLIT_SLOTS, 0:k * n].rearrange("p (k n) -> p k n", k=k)

        def product(o, w_hi, w_lo, m_hi, m_lo, first, last, **kw):
            nc.tensor.matmul(o, w_hi, m_hi, start=first, stop=False, **kw)
            nc.tensor.matmul(o, w_hi, m_lo, start=False, stop=False, **kw)
            return nc.tensor.matmul(o, w_lo, m_hi, start=False, stop=last, **kw)

        SMALL = {G["kpe"]: KD * MLA_ROPE, G["uq"]: 2 * 768, G["uq"] + 1: 2 * 768}

        def slab_len(g):
            return SMALL.get(g, SLAB)

        def round_next(act, g):
            if g + 2 < G["end"]:
                round_slab(act, g + 2, g + 2, slab_len(g + 2))

        def split_next(dve, g):
            if g + 2 < G["end"]:
                split_slab(dve, g + 2, g + 2, slab_len(g + 2))

        def mod_parts(layer, n, ctx_too):
            sec = 0 if n == 0 else 3
            parts = [(lambda k: x_lat[:, k, :], 0, L, lambda k: gsc[:, layer, n, k, 0:1],
                      lambda k: ada[:, layer, sec * KD + k, 0:1])]
            if ctx_too:
                parts.append((lambda k: x_ctx[:, k, :], L, LC, lambda k: gsc[:, layer, n, k, 1:2],
                              lambda k: ada[:, layer, sec * KD + k, 1:2]))
            return parts

        NORMS = {
            "fnet": (KD, D, mod_parts(0, 0, True), None, None),
            "ffn0": (KD, D, mod_parts(0, 1, True), hh, hl),
            "diff": (KD, D, mod_parts(1, 0, True), hh, hl),
            "ffn1": (KD, D, mod_parts(1, 1, False), hh, hl),
            "second": (KD, D, [(lambda k: x_lat[:, k, :], 0, L, lambda k: par_of("norm_w", k), None),
                               (lambda k: x_meta[:, k, :], L, N_META, lambda k: par_of("norm_w", k), None)],
                       hh, hl),
            "q_lat": (2, MLA_RANK, [(lambda k: lat32[:, k, 0:L], 0, L, lambda k: par_of("q_lat", k), None)],
                      ah, al),
            "kv_lat": (2, MLA_RANK, [(lambda k: lat32[:, k, L:HW], L, L2, lambda k: par_of("kv_lat", k), None)],
                       ah, al),
        }
        BASE, SPLIT_BASE, at = {}, {}, 0
        at_s = 0
        for name, (tiles, *_rest) in NORMS.items():
            BASE[name], SPLIT_BASE[name] = at, at_s
            at += tiles
            at_s += tiles if _rest[2] is not None else 0
        ORDER = list(NORMS)
        NORM_BANK = 7

        def norm_act(act, link, name):
            tiles, dim, parts, hi, _ = NORMS[name]
            b = BASE[name]
            n = sum(p[2] for p in parts)
            for k in range(tiles):
                positive(act, s_sum, b + k - 1 if k >= 2 else 0)
                if k < 2 and b:
                    act.wait_ge(s_h, b)
                at = 0
                for src, _, w, _, _ in parts:
                    ins = nc.scalar.activation(sq[:, k % 2, at:at + w], src(k), ACT.Square)
                    at += w
                ins.then_inc(s_sq, 1)
            act.wait_ge(s_sum, b + tiles)
            link(nc.scalar.activation(rstd[:, 1, 0:n], ps[:, NORM_BANK, 0:n], ACT.Ln, bias=eps_c[:, 0:1],
                                      scale=1.0 / dim))
            nc.scalar.activation(rstd[:, 0, 0:n], rstd[:, 1, 0:n], ACT.Exp, scale=-0.5).then_inc(s_rstd, 1)
            if hi is None:
                return
            for k in range(tiles):
                act.wait_ge(s_mul, b + k + 1)
                at = 0
                for _, off, w, scale, shift in parts:
                    ins = nc.scalar.activation(hi[:, k, off:off + w], nrm[:, k % 2, at:at + w], ACT.Identity,
                                               scale=scale(k), bias=shift(k) if shift else 0.0)
                    at += w
                ins.then_inc(s_hh, 1)

        def norm_dve(dve, name):
            tiles, _, parts, hi, lo = NORMS[name]
            b, sb_ = BASE[name], SPLIT_BASE[name]
            dve.wait_ge(s_rstd, ORDER.index(name) + 1)
            for k in range(tiles):
                at = 0
                if hi is not None:
                    positive(dve, s_hh, sb_ + k - 1 if k >= 2 else 0)
                for src, _, w, _, _ in parts:
                    ins = nc.vector.tensor_tensor(nrm[:, k % 2, at:at + w], src(k), rstd[:, 0, at:at + w],
                                                  ALU.mult)
                    at += w
                ins.then_inc(s_mul, 1)
                dve.wait_ge(s_mul, b + k + 1)
                at = 0
                for _, off, w, scale, shift in parts:
                    dst = h32[:, k, off:off + w] if hi is None else sq[:, k % 2, at:at + w]
                    if shift:
                        ins = nc.vector.tensor_scalar(dst, nrm[:, k % 2, at:at + w], scale(k), shift(k),
                                                      ALU.mult, ALU.add)
                    else:
                        ins = nc.vector.tensor_scalar(dst, nrm[:, k % 2, at:at + w], scale(k), None, ALU.mult)
                    at += w
                if hi is None:
                    ins.then_inc(s_h, 1)
                    continue
                ins.then_inc(v_ch, 1)
                v_count[0] += 1
                dve.wait_ge(v_ch, v_count[0])
                dve.wait_ge(s_hh, sb_ + k + 1)
                at = 0
                for _, off, w, _, _ in parts:
                    ins = nc.vector.tensor_tensor(lo[:, k, off:off + w], sq[:, k % 2, at:at + w],
                                                  hi[:, k, off:off + w].bitcast(F32), ALU.subtract)
                    at += w
                ins.then_inc(s_h, 1)

        def norm_pe(pe, name):
            tiles, _, parts, _, _ = NORMS[name]
            b = BASE[name]
            n = sum(p[2] for p in parts)
            for k in range(tiles):
                pe.wait_ge(s_sq, b + k + 1)
                nc.tensor.matmul(ps[:, NORM_BANK, 0:n], T["ones"], sq[:, k % 2, 0:n], start=(k == 0),
                                 stop=(k == tiles - 1)).then_inc(s_sum, 1)

        def unit(kind, g, k, n, col, cols, width, ends, **kw):
            return dict(kind=kind, g=g, k=k, n=n, col=col, cols=cols, w=width, ends=ends, **kw)

        def seg(dst, a, b):
            return (dst, a, b)

        DIFF_UNITS, LAT_UNITS, MLA_UNITS, NA_UNITS = [], [], [], []
        for h in range(8):
            DIFF_UNITS.append(unit("head", G["diff_k"] + h // 2, KD, 256, h % 2 * P, P, NT, h % 2 == 1,
                                   red="half", dim=64, gain="dk", rope=("cos_d", "sin_d", L),
                                   out=[seg(dk[:, h, L:NT], L, NT)], dst=dk[:, h, 0:L]))
        for h in range(8):
            DIFF_UNITS.append(unit("head", G["diff_q"] + h // 2, KD, 256, h % 2 * P, P, L, h % 2 == 1,
                                   red="half", dim=64, gain="dq", rope=("cos_d", "sin_d", L), out=[],
                                   dst=dq[:, h, :]))
        for s in range(4):
            for t in range(4):
                DIFF_UNITS.append(unit("token", G["diff_v"] + s, KD, 256, 0, 256, P, t == 3, tok=t * P,
                                       dst=dv[:, t, s * 256:(s + 1) * 256]))
        for m in range(2):
            LAT_UNITS.append(unit("copy", G["lat"], KD, 256, m * P, P, L, m == 1, dst=lat32[:, m, 0:L]))
        for m in range(2):
            LAT_UNITS.append(unit("copy", G["lat"] + 1, KD, 256, m * P, P, L2, m == 1, dst=lat32[:, m, L:HW]))
        LAT_UNITS.append(unit("head", G["kpe"], KD, MLA_ROPE, 0, MLA_ROPE, L2, True, red="ones", dim=64,
                              gain="kpe", rope=("cos_m", "sin_m", L2), out=[], dst=kp[0:MLA_ROPE, :]))
        for h in range(8):
            hd = MLA_NOPE + MLA_ROPE
            MLA_UNITS.append(unit("head", G["uq"] + h // 4, 2, 768, h % 4 * hd, P, L, False, red="ones",
                                  dim=128, gain="qn", rope=None, out=[seg(qn[:, h, :], 0, L)], src=0))
            MLA_UNITS.append(unit("head", G["uq"] + h // 4, 2, 768, h % 4 * hd + P, MLA_ROPE, L, h % 4 == 3,
                                  red="ones", dim=64, gain="qpe", rope=("cos_m", "sin_m", L), out=[],
                                  dst=qp[0:MLA_ROPE, h, :], src=0))
        for s in range(2):
            for j in range(4):
                h = 4 * s + j
                MLA_UNITS.append(unit("head", G["ukv"] + s, 2, 1024, j * 256, P, L2, False, red="ones",
                                      dim=128, gain="kn", rope=None, out=[seg(kn[:, h, :], 0, L2)], src=L))
            for t in range(3):
                MLA_UNITS.append(unit("token", G["ukv"] + s, 2, 1024, None, 512, P if t < 2 else N_META,
                                      t == 2, tok=L + t * P, src=L,
                                      dst=mv[0:(P if t < 2 else N_META), t, s * 512:(s + 1) * 512]))
        for m in range(8):
            MLA_UNITS.append(unit("silu", G["gmla"] + m // 2, KD, 256, m % 2 * P, P, L, m % 2 == 1,
                                  dst=mg[:, m, :]))
        for m in range(8):
            NA_UNITS.append(unit("head", G["naq"] + m // 2, KD, 256, m % 2 * P, P, L, m % 2 == 1, red="half",
                                 dim=64, gain="naq", rope=None, out=[seg(nq[:, m, :], 0, L)]))
        for m in range(8):
            NA_UNITS.append(unit("head", G["nak"] + m // 2, KD, 256, m % 2 * P, P, L2, m % 2 == 1, red="half",
                                 dim=64, gain="nak", rope=None,
                                 out=[seg(nkx[:, m, 0:N_META], L, L2),
                                      seg(nkx[:, m, N_META:N_META + L2], 0, L2)]))
        for s in range(4):
            for t in range(3):
                NA_UNITS.append(unit("token", G["nav"] + s, KD, 256, 0, 256, P if t < 2 else N_META, t == 2,
                                     tok=t * P, dst=nv[0:(P if t < 2 else N_META), t, s * 256:(s + 1) * 256]))
        for m in range(8):
            NA_UNITS.append(unit("silu", G["gna"] + m // 2, KD, 256, m % 2 * P, P, L, m % 2 == 1,
                                 dst=ng[:, m, :]))
        PHASES = [DIFF_UNITS, LAT_UNITS, MLA_UNITS, NA_UNITS]
        n_unit = n_head = n_rope = n_copy = 0
        for phase in PHASES:
            for u in phase:
                u["u"] = n_unit
                n_unit += 1
                if u["kind"] == "head":
                    u["h"] = n_head
                    n_head += 1
                    if u["rope"]:
                        u["r"] = n_rope
                        n_rope += 1
                else:
                    u["c"] = n_copy
                    n_copy += 1
        ALL_UNITS = [u for phase in PHASES for u in phase]
        ROPED = [u for u in ALL_UNITS if u.get("rope")]

        def unit_out(u):
            bank = u["u"] % 3
            if u["kind"] == "token":
                return ps[0:u["w"], bank, 0:u["cols"]]
            return ps[0:u["cols"], bank, 0:u["w"]]

        def unit_pe(pe, u, first_of_slab):
            if first_of_slab:
                pe.wait_ge(split, u["g"] + 1)
            if u["u"] >= 3:
                v = ALL_UNITS[u["u"] - 3]
                if v["kind"] == "head":
                    pe.wait_ge(s_unrm, v["h"] + 1)
                else:
                    pe.wait_ge(s_ucp, v["c"] + 1)
            whv, wlv = slab_view(wh, u["g"], u["k"], u["n"]), slab_view(wl, u["g"], u["k"], u["n"])
            mh, ml = (ah, al) if "src" in u else (hh, hl)
            off = u.get("src", 0)
            o = unit_out(u)
            for k in range(u["k"]):
                first, last = k == 0, k == u["k"] - 1
                if u["kind"] == "token":
                    tok = slice(u["tok"], u["tok"] + u["w"])
                    if u["col"] is None:
                        def cols(w):
                            return w[:, k, :].rearrange("p (h two e) -> p h two e", h=4, two=2)[:, :, 1, :]
                        oo = o.rearrange("p (h e) -> p h e", h=4)
                    else:
                        def cols(w):
                            return w[:, k, 0:u["cols"]]
                        oo = o
                    nc.tensor.matmul(oo, mh[:, k, tok], cols(whv), start=first, stop=False)
                    nc.tensor.matmul(oo, mh[:, k, tok], cols(wlv), start=False, stop=False)
                    ins = nc.tensor.matmul(oo, ml[:, k, tok], cols(whv), start=False, stop=last)
                else:
                    c = slice(u["col"], u["col"] + u["cols"])
                    m = slice(off, off + u["w"])
                    ins = product(o, whv[:, k, c], wlv[:, k, c], mh[:, k, m], ml[:, k, m], first, last)
            if u["ends"]:
                ins.then_inc(used, 1)
                pe.wait_ge(used, u["g"] + 1)
                pe.sem_inc(s_unit, 1)
            else:
                ins.then_inc(s_unit, 1)

        def units_pe(pe, phase):
            seen = set()
            for i in range(len(phase) + 2):
                if i < len(phase):
                    unit_pe(pe, phase[i], phase[i]["g"] not in seen)
                    seen.add(phase[i]["g"])
                if 1 <= i <= len(phase) and phase[i - 1]["kind"] == "head":
                    u = phase[i - 1]
                    h, m = u["h"], u["cols"]
                    pe.wait_ge(s_usq, h + 1)
                    positive(pe, s_urs, h - 1)
                    nc.tensor.matmul(ps[0:m, 3 + h % 2, 0:u["w"]], T[u["red"]][0:m, 0:m],
                                     sq[0:m, h % 2, 0:u["w"]], start=True, stop=True).then_inc(s_usum, 1)
                if 2 <= i and phase[i - 2].get("rope"):
                    u = phase[i - 2]
                    m, w = u["cols"], u["rope"][2]
                    pe.wait_ge(s_unrm, u["h"] + 1)
                    positive(pe, s_urdy, u["r"] - 1)
                    nc.tensor.matmul(ps[0:m, 5 + u["r"] % 2, 0:w], T["rot"][0:m, 0:m],
                                     nrm[0:m, u["h"] % 2, 0:w], start=True, stop=True).then_inc(s_urot, 1)

        def units_act(act, link, phase):
            for i in range(len(phase) + 1):
                if i < len(phase):
                    u = phase[i]
                    act.wait_ge(s_unit, u["u"] + 1)
                    if u["kind"] == "head":
                        positive(act, s_usum, u["h"] - 1)
                        nc.scalar.activation(sq[0:u["cols"], u["h"] % 2, 0:u["w"]], unit_out(u),
                                             ACT.Square).then_inc(s_usq, 1)
                    else:
                        f = ACT.Silu if u["kind"] == "silu" else ACT.Copy
                        nc.scalar.activation(u["dst"], unit_out(u), f).then_inc(s_ucp, 1)
                    if u["ends"]:
                        round_next(act, u["g"])
                if i >= 1 and phase[i - 1]["kind"] == "head":
                    u = phase[i - 1]
                    m, w = u["cols"], u["w"]
                    act.wait_ge(s_usum, u["h"] + 1)
                    positive(act, s_unrm, u["h"])
                    link(nc.scalar.activation(rstd[0:m, 1, 0:w], ps[0:m, 3 + u["h"] % 2, 0:w], ACT.Ln,
                                              bias=eps_c[0:m, 0:1], scale=1.0 / u["dim"]))
                    nc.scalar.activation(rstd[0:m, 0, 0:w], rstd[0:m, 1, 0:w], ACT.Exp,
                                         scale=-0.5).then_inc(s_urs, 1)

        def units_dve(dve, link, phase):
            for i in range(len(phase) + 2):
                if i < len(phase) and phase[i]["ends"]:
                    split_next(dve, phase[i]["g"])
                if 1 <= i <= len(phase) and phase[i - 1]["kind"] == "head":
                    u = phase[i - 1]
                    m = u["cols"]
                    o = unit_out(u)
                    dve.wait_ge(s_urs, u["h"] + 1)
                    outs = list(u["out"])
                    if u["rope"]:
                        w = u["rope"][2]
                        old = [v for v in ROPED if v["h"] == u["h"] - 2]
                        if old:
                            dve.wait_ge(s_urdy, old[0]["r"] + 1)
                        outs.append((nrm[0:m, u["h"] % 2, 0:w], 0, w))
                    for dst, a, b in outs:
                        ins = nc.vector.scalar_tensor_tensor(
                            out=dst, in0=o[:, a:b], scalar=par_of(u["gain"])[0:m, :], in1=rstd[0:m, 0, a:b],
                            op0=ALU.mult, op1=ALU.mult)
                    ins.then_inc(s_unrm, 1)
                if i >= 2 and phase[i - 2].get("rope"):
                    u = phase[i - 2]
                    m = u["cols"]
                    cos, sin, w = u["rope"]
                    dve.wait_ge(s_unrm, u["h"] + 1)
                    positive(dve, s_urdy, u["r"])
                    tile = nrm[0:m, u["h"] % 2, 0:w]
                    link(nc.vector.tensor_tensor(t1[0:m, 0:w], tile, T[cos][0:m, 0:w], ALU.mult))
                    dve.wait_ge(s_urot, u["r"] + 1)
                    link(nc.vector.tensor_tensor(tile, ps[0:m, 5 + u["r"] % 2, 0:w], T[sin][0:m, 0:w],
                                                 ALU.mult))
                    nc.vector.tensor_tensor(u["dst"], t1[0:m, 0:w], tile, ALU.add).then_inc(s_urdy, 1)
            done = [u for u in phase if u.get("rope")]
            if done:
                dve.wait_ge(s_urdy, done[-1]["r"] + 1)

        def chunk_plan(keys):
            return [(a, min(P, keys - a)) for a in range(0, keys, P)]

        ATT = {
            "diff": dict(heads=8, maps=2, keys=NT, scale=DIFF_DIM ** -0.5, pair=1),
            "mla": dict(heads=8, maps=1, keys=L2, scale=(MLA_NOPE + MLA_ROPE) ** -0.5, pair=1),
            "na": dict(heads=16, maps=1, keys=L2, scale=NA_DIM ** -0.5, pair=2),
        }
        step_base = head_base = group_base = map_base = 0
        for name, a in ATT.items():
            a.update(name=name, steps=2 * a["heads"], s0=step_base, h0=head_base, g0=group_base, m0=map_base)
            a["groups"] = a["heads"] // a["pair"]
            step_base += a["steps"]
            head_base += a["heads"]
            group_base += a["groups"]
            map_base += a["maps"] * a["steps"]

        def scores_of(a, h, t, c):
            q = slice(t * P, (t + 1) * P)
            if a["name"] == "diff":
                r = slice(64 * c, 64 * c + 64)
                return [(dq[r, h, q], dk[r, h, :])]
            if a["name"] == "mla":
                return [(qn[:, h, q], kn[:, h, :]), (qp[0:MLA_ROPE, h, q], kp[0:MLA_ROPE, :])]
            r = slice(64 * (h % 2), 64 * (h % 2) + 64)
            off = N_META if t == 0 else 0
            return [(nq[r, h // 2, q], nkx[r, h // 2, off:off + L2])]

        def chunks_of(a, t):
            if a["name"] == "na" and t == 1:
                return [(N_META, P), (N_META + P, P), (0, N_META)]
            return chunk_plan(a["keys"])

        def values_of(a, h, j, n):
            v = {"diff": dv, "mla": mv, "na": nv}[a["name"]]
            w = P // a["pair"]
            return v[0:n, j, h * w:(h + 1) * w]

        def score_bank(a, i, c):
            return (i % 2) * a["maps"] + c

        def o_psum(a, f):
            return ps[:, 6 + f % 2, 0:L]

        def att_pe(pe, a):
            for i in range(a["steps"] + 3):
                if i < a["steps"]:
                    h, t = divmod(i, 2)
                    if i >= 2:
                        pe.wait_ge(s_ex, a["m0"] + (i - 1) * a["maps"])
                    for c in range(a["maps"]):
                        pairs = scores_of(a, h, t, c)
                        for j, (w, m) in enumerate(pairs):
                            ins = nc.tensor.matmul(ps[:, score_bank(a, i, c), 0:a["keys"]], w, m,
                                                   start=(j == 0), stop=(j == len(pairs) - 1))
                    ins.then_inc(s_sc, 1)
                if 1 <= i <= a["steps"]:
                    j0 = i - 1
                    pe.wait_ge(s_w, a["s0"] + j0 + 1)
                    positive(pe, s_trc, a["s0"] + j0 - 1)
                    for j, (at, n) in enumerate(chunks_of(a, j0 % 2)):
                        ins = nc.tensor.transpose(ps[0:n, 4 + j0 % 2, j * P:(j + 1) * P],
                                                  ex[:, j0 % 2, 0, at:at + n], T["ident"])
                    ins.then_inc(s_tr, 1)
                if i >= 3 and i % 2 == 1 and (i - 3) // 2 < a["heads"]:
                    h = (i - 3) // 2
                    f = h // a["pair"]
                    pe.wait_ge(s_trc, a["s0"] + 2 * h + 2)
                    if h % a["pair"] == 0:
                        positive(pe, s_on, a["g0"] + f - 1)
                    part = P // a["pair"]
                    row = h % a["pair"] * part
                    plan = chunk_plan(a["keys"])
                    for j, (_, n) in enumerate(plan):
                        ins = nc.tensor.matmul(o_psum(a, f)[row:row + part, :], values_of(a, h, j, n),
                                               wT[0:n, h % 2, j, :], start=(j == 0), stop=(j == len(plan) - 1))
                    ins.then_inc(s_pv, 1)
                if a["name"] == "diff" and i >= 4 and i % 2 == 0 and (i - 4) // 2 < a["heads"]:
                    sub_sum(pe, a, (i - 4) // 2)

        def sub_sum(pe, a, h):
            pe.wait_ge(s_osq, h + 1)
            nc.tensor.matmul(ps[:, 6 + h % 2, L:2 * L], T["ones"], sq[:, h % 2, 0:L], start=True,
                             stop=True).then_inc(s_osum, 1)

        def att_act(act, link, a):
            diff = a["name"] == "diff"
            for i in range(a["steps"] + 8):
                if i < a["steps"]:
                    for c in range(a["maps"]):
                        act.wait_ge(s_mx, a["m0"] + i * a["maps"] + c + 1)
                        src = ex[:, i % 2, 1, 0:a["keys"]] if a["name"] == "na" else \
                            ps[:, score_bank(a, i, c), 0:a["keys"]]
                        positive(act, s_tr, a["s0"] + i - 1)
                        nc.scalar.activation(ex[:, i % 2, c, 0:a["keys"]], src, ACT.Exp,
                                             bias=nm[:, i % 2, c:c + 1],
                                             scale=1.0 if a["name"] == "na" else a["scale"],
                                             accum_out=sm[:, i % 2, c:c + 1]).then_inc(s_ex, 1)
                if 1 <= i <= a["steps"]:
                    j0 = i - 1
                    h, t = divmod(j0, 2)
                    act.wait_ge(s_tr, a["s0"] + j0 + 1)
                    if h >= 2:
                        act.wait_ge(s_pv, a["h0"] + h - 1)
                    full = [c for c in chunk_plan(a["keys"]) if c[1] == P]
                    ins = nc.scalar.activation(
                        wT[:, h % 2, 0:len(full), t * P:(t + 1) * P],
                        ps[:, 4 + j0 % 2, 0:len(full) * P].rearrange("p (c n) -> p c n", c=len(full)), ACT.Copy)
                    if len(full) < len(chunk_plan(a["keys"])):
                        ins = nc.scalar.activation(wT[0:N_META, h % 2, len(full), t * P:(t + 1) * P],
                                                   ps[0:N_META, 4 + j0 % 2, len(full) * P:(len(full) + 1) * P],
                                                   ACT.Copy)
                    ins.then_inc(s_trc, 1)
                if diff and i % 2 == 0 and 0 <= (i - 4) // 2 < a["heads"]:
                    h = (i - 4) // 2
                    act.wait_ge(s_pv, a["h0"] + h + 1)
                    positive(act, s_osum, h - 1)
                    nc.scalar.activation(sq[:, h % 2, 0:L], o_psum(a, h), ACT.Square).then_inc(s_osq, 1)
                if diff and i % 2 == 1 and 0 <= (i - 5) // 2 < a["heads"]:
                    h = (i - 5) // 2
                    act.wait_ge(s_osum, h + 1)
                    positive(act, s_on, h)
                    link(nc.scalar.activation(rstd[:, 1, 0:L], ps[:, 6 + h % 2, L:2 * L], ACT.Ln, bias=eps_c[:, 0:1],
                                              scale=1.0 / P))
                    nc.scalar.activation(rstd[:, 0, 0:L], rstd[:, 1, 0:L], ACT.Exp, scale=-0.5)\
                        .then_inc(s_ors, 1)
                f = i // (2 * a["pair"]) - {"diff": 3, "mla": 2, "na": 1}[a["name"]]
                if i % (2 * a["pair"]) == (0 if a["pair"] == 1 else 2) and 0 <= f < a["groups"]:
                    o_round(act, a, f)

        def o_out(a, f, which):
            return which[:, f, L2:L2 + L] if a["name"] == "mla" else which[:, f, 0:L]

        def o_round(act, a, f):
            act.wait_ge(s_on, a["g0"] + f + 1)
            nc.scalar.activation(o_out(a, f, hh), nrm[:, f % 2, 0:L], ACT.Copy).then_inc(s_or, 1)

        def o_split(dve, a, f):
            dve.wait_ge(s_or, a["g0"] + f + 1)
            nc.vector.tensor_tensor(o_out(a, f, hl), nrm[:, f % 2, 0:L], o_out(a, f, hh).bitcast(F32),
                                    ALU.subtract).then_inc(s_os, 1)

        def att_dve(dve, link, a):
            diff, na = a["name"] == "diff", a["name"] == "na"
            n = a["keys"]
            for i in range(a["steps"] + 8):
                if i < a["steps"]:
                    dve.wait_ge(s_sc, a["s0"] + i + 1)
                    if na:
                        h, t = divmod(i, 2)
                        off = N_META + 2 * GRID_W if t == 0 else 0
                        dve.wait_ge(s_bias, h + 1)
                        ins = nc.vector.scalar_tensor_tensor(
                            out=ex[:, i % 2, 1, 0:n], in0=ps[:, score_bank(a, i, 0), 0:n], scalar=a["scale"],
                            in1=bias[:, h % 2, off:off + n], op0=ALU.mult, op1=ALU.add)
                        ins.then_inc(s_sb, 1)
                        dve.wait_ge(s_sb, i + 1)
                        nc.vector.tensor_reduce(nm[:, i % 2, 0:1], ex[:, i % 2, 1, 0:n], AX_X, ALU.max,
                                                negate=True).then_inc(s_mx, 1)
                    else:
                        for c in range(a["maps"]):
                            link(nc.vector.tensor_reduce(mx[:, i % 2, c:c + 1],
                                                         ps[:, score_bank(a, i, c), 0:n], AX_X, ALU.max))
                            nc.vector.tensor_scalar(nm[:, i % 2, c:c + 1], mx[:, i % 2, c:c + 1], -a["scale"],
                                                    None, ALU.mult).then_inc(s_mx, 1)
                if 1 <= i <= a["steps"]:
                    j = (i - 1) % 2
                    dve.wait_ge(s_ex, a["m0"] + i * a["maps"])
                    link(nc.vector.reciprocal(rc[:, j, 0:a["maps"]], sm[:, j, 0:a["maps"]]))
                    if diff:
                        link(nc.vector.tensor_scalar(rc[:, j, 1:2], rc[:, j, 1:2], sml[:, 5:6], None,
                                                     ALU.mult))
                        link(nc.vector.tensor_scalar(ex[:, j, 0, 0:n], ex[:, j, 0, 0:n], rc[:, j, 0:1], None,
                                                     ALU.mult))
                        nc.vector.scalar_tensor_tensor(out=ex[:, j, 0, 0:n], in0=ex[:, j, 1, 0:n],
                                                       scalar=rc[:, j, 1:2], in1=ex[:, j, 0, 0:n],
                                                       op0=ALU.mult, op1=ALU.add).then_inc(s_w, 1)
                    else:
                        nc.vector.tensor_scalar(ex[:, j, 0, 0:n], ex[:, j, 0, 0:n], rc[:, j, 0:1], None,
                                                ALU.mult).then_inc(s_w, 1)
                if diff:
                    if i % 2 == 1 and 0 <= (i - 5) // 2 < a["groups"]:
                        f = (i - 5) // 2
                        dve.wait_ge(s_ors, f + 1)
                        positive(dve, s_os, a["g0"] + f - 1)
                        nc.vector.scalar_tensor_tensor(out=nrm[:, f % 2, 0:L], in0=o_psum(a, f),
                                                       scalar=subg[:, 0:1], in1=rstd[:, 0, 0:L],
                                                       op0=ALU.mult, op1=ALU.mult).then_inc(s_on, 1)
                    if i % 2 == 0 and 0 <= (i - 6) // 2 < a["groups"]:
                        o_split(dve, a, (i - 6) // 2)
                else:
                    per = 2 * a["pair"]
                    if i % per == 2 % per and 0 <= (i - per - 2) // per < a["groups"]:
                        f = (i - per - 2) // per
                        dve.wait_ge(s_pv, a["h0"] + a["pair"] * (f + 1))
                        positive(dve, s_os, a["g0"] + f - 1)
                        gate = mg if a["name"] == "mla" else ng
                        nc.vector.tensor_tensor(nrm[:, f % 2, 0:L], o_psum(a, f), gate[:, f, :],
                                                ALU.mult).then_inc(s_on, 1)
                    if i % per == 3 % per and 0 <= (i - per - 3) // per < a["groups"]:
                        o_split(dve, a, (i - per - 3) // per)

        def outproj_pe(pe, g0, n, base):
            for m in range(KD):
                g = g0 + m // 2
                if m % 2 == 0:
                    pe.wait_ge(split, g + 1)
                if m >= 4:
                    pe.wait_ge(s_x, base + m - 3)
                whv, wlv = slab_view(wh, g, KD, 256), slab_view(wl, g, KD, 256)
                c = slice(m % 2 * P, m % 2 * P + P)
                for k in range(KD):
                    ins = product(ps[:, m % 4, 0:n], whv[:, k, c], wlv[:, k, c], hh[:, k, 0:n], hl[:, k, 0:n],
                                  k == 0, k == KD - 1)
                ins.then_inc(s_op, 1)
                if m % 2:
                    pe.wait_ge(s_op, (0 if base == 0 else KD) + m + 1)
                    pe.sem_inc(used, 1)

        X_FNET, X_FFN0, X_DIFF, X_FFN1 = 0, 8, 16, 24

        def ffn_in_steps(layer):
            return G["ffn0_in"] if layer == 0 else G["ffn1_in"]

        block = ctx.enter_context(nc.Block())
        v_count = [0]
        a_count = [0]

        @block.sync
        def _(sp):
            def load(g, src, k, n):
                load_slab(sp, g, g, src, k, n)

            for s in range(24):
                load(G["ada0"] + s, d["w_ada"][0, :, s * 256:(s + 1) * 256], KD, 256)
            for s in range(4):
                load(G["fnet_out"] + s, d["fnet_w_out"][0, :, s * 256:(s + 1) * 256], KD, 256)

            def ffn0_turn(i):
                g = G["ffn0_in"]
                for j, (w, col) in enumerate(((d["ffn_w_in"], i * 256), (d["ffn_w_in"], i * 256 + D_FF),
                                              (d["w_ada"], i * 512), (d["w_ada"], i * 512 + 256))):
                    lay = 0 if j < 2 else 1
                    load_slab(sp, g + 4 * i + j, g + j, w[lay, :, bass.ds(col, 256)], KD, 256)

            with sp.Fori(0, 11) as i:
                ffn0_turn(i)

            def ffn_out(layer, g, s, at):
                load_slab(sp, g, at, d["ffn_w_out"][layer, bass.ds(s * 256, 256), :], 2, D)

            def ffn_out_all(layer, g0):
                for s in range(3):
                    ffn_out(layer, g0 + s, s, g0 + s)
                with sp.Fori(0, 2) as i:
                    for j in range(4):
                        ffn_out(layer, g0 + 3 + j + i * 4, i * 4 + 3 + j, g0 + 3 + j)

            ffn_out_all(0, G["ffn0_out"])
            for s in range(2):
                load(G["ada1_tail"] + s, d["w_ada"][1, :, (22 + s) * 256:(23 + s) * 256], KD, 256)
            for g, col in ((G["diff_k"], D), (G["diff_q"], 0), (G["diff_v"], 2 * D)):
                for s in range(4):
                    load(g + s, d["diff_w_in"][0, :, col + s * 256:col + (s + 1) * 256], KD, 256)
            for s in range(4):
                load(G["diff_out"] + s, d["diff_w_out"][0, :, s * 256:(s + 1) * 256], KD, 256)

            def ffn1(i, t, at):
                for j in range(2):
                    load_slab(sp, G["ffn1_in"] + 2 * t + j, at + j,
                              d["ffn_w_in"][1, :, bass.ds(t * 256 + j * D_FF, 256)], KD, 256)

            ffn1(0, 0, G["ffn1_in"])
            with sp.Fori(0, 5) as i:
                for t in range(2):
                    ffn1(i, 2 * i + 1 + t, G["ffn1_in"] + 2 + 2 * t)
            ffn_out_all(1, G["ffn1_out"])

            w_in = d["w_in_2"]
            load(G["lat"], w_in[0, :, IN_QLAT:IN_QLAT + 256], KD, 256)
            load(G["lat"] + 1, w_in[0, :, IN_KVLAT:IN_KVLAT + 256], KD, 256)
            load(G["kpe"], w_in[0, :, IN_KPE:IN_KPE + MLA_ROPE], KD, MLA_ROPE)
            for s in range(2):
                load(G["uq"] + s, d["w_uq_2"][0, :, s * 768:(s + 1) * 768], 2, 768)
            for s in range(2):
                load(G["ukv"] + s, d["w_ukv_2"][0, :, s * 1024:(s + 1) * 1024], 2, 1024)
            for g, col in ((G["gmla"], IN_GMLA), (G["naq"], IN_NAQ), (G["nak"], IN_NAK), (G["nav"], IN_NAV),
                           (G["gna"], IN_GNA)):
                for s in range(4):
                    load(g + s, w_in[0, :, col + s * 256:col + (s + 1) * 256], KD, 256)
            for s in range(8):
                load(G["out2"] + s, d["w_out_2"][0, s * 256:(s + 1) * 256, :], 2, D)

        @block.gpsimd
        def _(pool):
            pool.dma_start(big[:, 10240:10240 + FOURIER], d["fourier"]).then_inc(s_tab, 16)
            pool.dma_start(meta_b[:, :], d["meta_bias"].to_broadcast([P, NA_HEADS * N_META])
                           if False else bass.AP(tensor=d["meta_bias"].tensor, offset=0,
                                                 ap=[[0, P], [1, NA_HEADS * N_META]])).then_inc(s_metab, 16)
            pool.wait_ge(s_metab, 16)
            pool.wait_ge(s_on, ATT["mla"]["g0"] + ATT["mla"]["groups"])
            flat = NA_HEADS * REL_R * REL_C
            for half in range(2):
                first = flat - 1 - (NA_HEADS - 1) * REL_R * REL_C - (NA_WIN_R - 1 - 2 - half) * REL_C \
                    - (NA_WIN_C - 1) - (RUN - 1)
                pool.dma_start(runs[64 * half:64 * half + 64, :, :],
                               bass.AP(tensor=d["rel_bias_rev"].tensor, offset=first,
                                       ap=[[1, 64], [REL_R * REL_C, NA_HEADS], [1, RUN]])).then_inc(s_runs, 16)
            pool.wait_ge(s_runs, 32)
            for h in range(NA_HEADS):
                s = h % 2
                if h >= 2:
                    pool.wait_ge(s_sb, 2 * (h - 1))
                at = 9472 + (NA_HEADS - 1 - h) * RUN + RUN - 1
                run = bass.AP(tensor=big, offset=at, ap=[[13824, P], [-REL_C, SLOTS_R], [-1, GRID_W]])
                mask = bass.AP(tensor=tab, offset=KEPT - GRID_W, ap=[[KEPT, P], [0, SLOTS_R], [1, GRID_W]])
                for c in (0, N_META + SLOTS_R * GRID_W):
                    nc.gpsimd.tensor_copy(bias[:, s, c:c + N_META], meta_b[:, h * N_META:(h + 1) * N_META])
                nc.gpsimd.tensor_tensor(
                    bias[:, s, N_META:N_META + SLOTS_R * GRID_W].rearrange("p (j c) -> p j c", j=SLOTS_R),
                    run, mask, ALU.add).then_inc(s_bias, 1)

        @block.scalar
        def _(act):
            def link(ins):
                a_count[0] += 1
                ins.then_inc(a_ch, 1)
                act.wait_ge(a_ch, a_count[0])

            act.dma_start(tab[:, :], d["tables"]).then_inc(s_rows, 16)
            act.dma_start(rows[0:N_PAR, P:2 * P], d["params"]).then_inc(s_rows, 16)
            act.dma_start(rows[0:N_ADA, 0:P], d["b_ada"]).then_inc(s_rows, 16)
            act.dma_start(xin[:, 0:2, :], d["x"][0].rearrange("(t p) n -> p t n", p=P)).then_inc(s_xin, 16)
            act.dma_start(xin[:, 2:4, :], d["ctx"][0].rearrange("(t p) n -> p t n", p=P)).then_inc(s_xin, 16)
            act.dma_start(h32[0:N_META, 0:2, :].rearrange("p a b -> p (a b)"), d["meta_tokens_2"])\
                .then_inc(s_xin, 16)
            act.wait_ge(s_turn_v, 1)
            link(nc.scalar.activation(cond[:, :], par_of("c", 0, 2 * KD), ACT.Silu))
            nc.scalar.activation(condr[:, :, 0:2], cond[:, :].rearrange("p (c k) -> p k c", c=2), ACT.Copy)\
                .then_inc(s_cond, 1)
            act.wait_ge(s_turn, 2)
            for c in range(2):
                ins = nc.scalar.activation(sml[:, 2 + c:3 + c], ps[:, 3 - 2 * c, c:c + 1], ACT.Exp)
            ins.then_inc(s_mod, 1)
            for k in range(KD):
                act.wait_ge(s_turn, 3 + k)
                nc.scalar.activation(x_ctx[:, k, :], ps[:, 6 + k % 2, 0:LC], ACT.Copy).then_inc(s_turn_a, 1)
            round_slab(act, 0, 0)
            round_slab(act, 1, 1)
            for s in range(8):
                round_next(act, G["ada0"] + s)
            norm_act(act, link, "fnet")
            for i in range(8 + 1):
                if i < 8:
                    act.wait_ge(s_f1, i + 1)
                    if i >= 2:
                        act.wait_ge(s_f2, i - 1)
                    nc.scalar.activation(uv[:, i % 2, 0:2, :].rearrange("p t c -> p (t c)"),
                                         ps[:, 2 * (i % 2), :], ACT.Copy).then_inc(s_f1a, 1)
                    for s in range(2):
                        round_next(act, G["ada0"] + 8 + 2 * i + s)
                if i >= 1:
                    act.wait_ge(s_f2, i)
                    nc.scalar.activation(hh[:, i - 1, 0:NT], ps[:, 4 + (i - 1) % 2, :], ACT.Copy)\
                        .then_inc(s_f2a, 1)
            for m in range(KD):
                act.wait_ge(s_op, m + 1)
                if m >= 2:
                    act.wait_ge(s_x, m - 1)
                nc.scalar.activation(sq[:, m % 2, :], ps[:, m % 4, :], ACT.Identity, scale=1.0,
                                     bias=par_of("fnet_b", m)).then_inc(s_opa, 1)
                if m % 2:
                    round_next(act, G["fnet_out"] + m // 2)

            def norm_and(name, base):
                act.wait_ge(s_x, base)
                norm_act(act, link, name)

            def silu_gate(i, n, gtile):
                for j in range(2):
                    act.wait_ge(s_gate, gtile + 2 * i + j + 1)
                    positive(act, s_act, gtile + 2 * i + j - 1)
                    nc.scalar.activation(nrm[:, j, 0:n], ps[:, j, 0:n], ACT.Silu).then_inc(s_silu, 1)

            def act_round(layer, s, kk, n):
                base = layer * KF
                positive(act, s_au, s * 2 + (base + kk - 1))
                act.wait_ge(s_act, (layer + 1) * KF)
                nc.scalar.activation(ah[:, kk, 0:n], big[:, bass.ds(s * (2 * n) + kk * n, n)], ACT.Copy)\
                    .then_inc(s_ar, 1)

            def ffn_out(layer, g0, n):
                for kk in range(2):
                    act_round(layer, 0, kk, n)
                for s in range(3):
                    for kk in range(2):
                        act_round(layer, s + 1, kk, n)
                    round_slab(act, g0 + s + 2, g0 + s + 2)
                with act.Fori(0, 1) as i:
                    for j in range(4):
                        for kk in range(2):
                            act_round(layer, i * 4 + 4 + j, kk, n)
                        round_slab(act, i * 4 + (g0 + 5 + j), g0 + 5 + j)
                for s in range(7, 11):
                    if s + 1 < 11:
                        for kk in range(2):
                            act_round(layer, s + 1, kk, n)
                    round_next(act, g0 + s)

            norm_and("ffn0", X_FNET + KD)
            g = G["ffn0_in"]

            def ffn0_turn(i, at):
                round_slab(act, g + 4 * i + 2, g + 2)
                silu_gate(i, NT, 0)
                for j in range(3, 6):
                    round_slab(act, g + 4 * i + j, g + j)

            ffn0_turn(0, 0)
            with act.Fori(1, 11) as i:
                ffn0_turn(i, None)
            ffn_out(0, G["ffn0_out"], NT)
            for s in range(2):
                round_next(act, G["ada1_tail"] + s)
            norm_and("diff", X_FFN0 + KD)
            units_act(act, link, DIFF_UNITS)
            att_act(act, link, ATT["diff"])
            for s in range(4):
                round_next(act, G["diff_out"] + s)
            norm_and("ffn1", X_DIFF + KD)
            g1 = G["ffn1_in"]

            def ffn1_turn(i, at):
                round_slab(act, g1 + 2 * i + 2, at + 2)
                silu_gate(i, L, KF)
                round_slab(act, g1 + 2 * i + 3, at + 3)

            ffn1_turn(0, g1)
            with act.Fori(0, 5) as i:
                for t in range(2):
                    ffn1_turn(2 * i + 1 + t, g1 + 2 + 2 * t)
            ffn_out(1, G["ffn1_out"], L)
            norm_and("second", X_FFN1 + KD)
            units_act(act, link, LAT_UNITS)
            norm_act(act, link, "q_lat")
            norm_act(act, link, "kv_lat")
            units_act(act, link, MLA_UNITS)
            att_act(act, link, ATT["mla"])
            units_act(act, link, NA_UNITS)
            att_act(act, link, ATT["na"])
            for s in range(8):
                round_next(act, G["out2"] + s)
            for t in range(2):
                act.wait_ge(s_fin, 1)
                nc.scalar.activation(big[:, t * D:t * D + 512], ps[:, 2 * t, :], ACT.Copy).then_inc(s_fo, 1)
            act.wait_ge(s_fo, 4)
            for t in range(2):
                act.dma_start(out[0, t * P:(t + 1) * P, :], big[:, t * D:(t + 1) * D]).then_inc(s_out, 16)
            act.wait_ge(s_out, 32)

        @block.vector
        def _(dve):
            def link(ins):
                v_count[0] += 1
                ins.then_inc(v_ch, 1)
                dve.wait_ge(v_ch, v_count[0])

            link(nc.vector.memset(eps_c[:, :], EPS))
            dve.wait_ge(s_turn, 1)
            nc.vector.tensor_copy(par[:, :], ps[:, 0, 0:N_ADA + N_PAR]).then_inc(s_turn_v, 1)
            dve.wait_ge(s_turn_v, 1)
            nc.vector.tensor_tensor(sml[:, 0:1], par_of("lam_a"), par_of("lam_b"), ALU.mult)\
                .then_inc(s_turn_v, 1)
            link(nc.vector.tensor_scalar(subg[:, :], par_of("subln"), 1.0 - LAM_INIT, None, ALU.mult))
            dve.wait_ge(s_cond, 1)
            nc.vector.tensor_tensor(condr[:, :, 2:4], cond[:, :].rearrange("p (c k) -> p k c", c=2),
                                    condr[:, :, 0:2].bitcast(F32), ALU.subtract).then_inc(s_cond, 1)
            dve.wait_ge(s_mod, 1)
            link(nc.vector.tensor_tensor(sml[:, 4:5], sml[:, 3:4], sml[:, 2:3], ALU.subtract))
            link(nc.vector.tensor_scalar(sml[:, 5:6], sml[:, 4:5], -LAM_INIT, None, ALU.add))
            for k in range(KD):
                dve.wait_ge(s_turn, 3 + k)
                nc.vector.tensor_copy(x_lat[:, k, :], ps[:, 4 + k % 2, 0:L]).then_inc(s_turn_v, 1)
            dve.wait_ge(s_turn, 3 + KD)
            nc.vector.tensor_copy(x_meta[:, :, :], ps[:, 2, 0:KD * N_META].rearrange("p (k n) -> p k n", k=KD))\
                .then_inc(s_turn_v, 1)
            split_slab(dve, 0, 0)
            split_slab(dve, 1, 1)

            def ada_out(layer, p, count, s_chain, c0):
                dve.wait_ge(s_ada, count)
                o = ps[:, 6, 0:16].rearrange("p (m c) -> p m c", m=4)
                nc.vector.tensor_copy(ada_lo[:, :, :], o[:, :, 2:4]).then_inc(s_chain, 1)
                dve.wait_ge(s_chain, c0 + 1)
                nc.vector.tensor_tensor(ada_lo[:, :, :], o[:, :, 0:2], ada_lo[:, :, :], ALU.add)\
                    .then_inc(s_chain, 1)
                dve.wait_ge(s_chain, c0 + 2)
                for c in range(2):
                    ins = nc.vector.tensor_tensor(
                        ada[:, layer, bass.ds(p * 4, 4), c], ada_lo[:, :, c],
                        par[:, bass.ds(p * 4 + layer * 6 * KD, 4)], ALU.add)
                ins.then_inc(s_chain, 1)

            def scaled_gain(layer, n):
                sec = 1 if n == 0 else 4
                for c in range(2):
                    link(nc.vector.scalar_tensor_tensor(
                        out=gsc[:, layer, n, :, c], in0=ada[:, layer, sec * KD:(sec + 1) * KD, c], scalar=1.0,
                        in1=par_of("norm_gain", (2 * layer + n) * KD, KD), op0=ALU.add, op1=ALU.mult))

            for s in range(8):
                split_next(dve, G["ada0"] + s)
                if s % 2:
                    p = s // 2
                    ada_out(0, p, p + 1, s_adav, 3 * p)
                    dve.wait_ge(s_adav, 3 * p + 3)
            scaled_gain(0, 0)
            norm_dve(dve, "fnet")
            for i in range(8 + 1):
                if i < 8:
                    dve.wait_ge(s_f1, i + 1)
                    if i >= 2:
                        dve.wait_ge(s_f2, i - 1)
                    nc.vector.tensor_copy(uv[:, i % 2, 2:4, :].rearrange("p t c -> p (t c)"),
                                          ps[:, 2 * (i % 2) + 1, :]).then_inc(s_f1v, 1)
                    for s in range(2):
                        split_next(dve, G["ada0"] + 8 + 2 * i + s)
                    p = 4 + i
                    ada_out(0, p, p + 1, s_adav, 3 * p)
                    dve.wait_ge(s_adav, 3 * p + 3)
                if i >= 1:
                    dve.wait_ge(s_f2a, i)
                    nc.vector.tensor_tensor(hl[:, i - 1, 0:NT], ps[:, 4 + (i - 1) % 2, :],
                                            hh[:, i - 1, 0:NT].bitcast(F32), ALU.subtract).then_inc(s_f2v, 1)
            scaled_gain(0, 1)

            def add_gated(src, layer, sec, m, width, off, x, c):
                return nc.vector.scalar_tensor_tensor(out=x[:, m, :], in0=src[:, off:off + width],
                                                      scalar=ada[:, layer, sec * KD + m, c:c + 1],
                                                      in1=x[:, m, :], op0=ALU.mult, op1=ALU.add)

            for m in range(KD):
                dve.wait_ge(s_opa, m + 1)
                add_gated(sq[:, m % 2, :], 0, 2, m, L, 0, x_lat, 0)
                add_gated(sq[:, m % 2, :], 0, 2, m, LC, L, x_ctx, 1).then_inc(s_x, 1)
                if m % 2:
                    split_next(dve, G["fnet_out"] + m // 2)

            def up_times_gate(i, n, tile):
                for j in range(2):
                    dve.wait_ge(s_up, tile + 2 * i + j + 1)
                    dve.wait_ge(s_silu, tile + 2 * i + j + 1)
                    nc.vector.tensor_tensor(big[:, bass.ds(i * (2 * n) + j * n, n)], nrm[:, j, 0:n],
                                            ps[:, 2 + j, 0:n], ALU.mult).then_inc(s_act, 1)

            def act_split(layer, s, kk, n):
                dve.wait_ge(s_ar, s * 2 + (layer * KF + kk + 1))
                nc.vector.tensor_tensor(al[:, kk, 0:n], big[:, bass.ds(s * (2 * n) + kk * n, n)],
                                        ah[:, kk, 0:n].bitcast(F32), ALU.subtract).then_inc(s_as, 1)

            def ffn_out(layer, g0, n):
                for kk in range(2):
                    act_split(layer, 0, kk, n)
                for s in range(3):
                    for kk in range(2):
                        act_split(layer, s + 1, kk, n)
                    split_slab(dve, g0 + s + 2, g0 + s + 2)
                with dve.Fori(0, 1) as i:
                    for j in range(4):
                        for kk in range(2):
                            act_split(layer, i * 4 + 4 + j, kk, n)
                        split_slab(dve, i * 4 + (g0 + 5 + j), g0 + 5 + j)
                for s in range(7, 11):
                    if s + 1 < 11:
                        for kk in range(2):
                            act_split(layer, s + 1, kk, n)
                    split_next(dve, g0 + s)
                dve.wait_ge(s_ffn, layer + 1)
                for m in range(KD):
                    ins = add_gated(ps[:, m, :], layer, 5, m, L, 0, x_lat, 0)
                    if layer == 0:
                        ins = add_gated(ps[:, m, :], layer, 5, m, LC, L, x_ctx, 1)
                    ins.then_inc(s_x, 1)

            norm_dve(dve, "ffn0")
            g = G["ffn0_in"]

            def ffn0_turn(i):
                split_slab(dve, g + 4 * i + 2, g + 2)
                split_slab(dve, g + 4 * i + 3, g + 3)
                up_times_gate(i, NT, 0)
                split_slab(dve, g + 4 * i + 4, g + 4)
                split_slab(dve, g + 4 * i + 5, g + 5)
                ada_out(1, i, i + 13, s_adav, i * 3 + 36)

            ffn0_turn(0)
            with dve.Fori(1, 11) as i:
                ffn0_turn(i)
            ffn_out(0, G["ffn0_out"], NT)
            for s in range(2):
                split_next(dve, G["ada1_tail"] + s)
            ada_out(1, 11, 24, s_adav, 69)
            dve.wait_ge(s_adav, 72)
            scaled_gain(1, 0)
            scaled_gain(1, 1)
            dve.wait_ge(s_x, X_FFN0 + KD)
            norm_dve(dve, "diff")
            units_dve(dve, link, DIFF_UNITS)
            att_dve(dve, link, ATT["diff"])
            for m in range(KD):
                dve.wait_ge(s_op, KD + m + 1)
                add_gated(ps[:, m % 4, :], 1, 2, m, L, 0, x_lat, 0).then_inc(s_x, 1)
                if m % 2:
                    split_next(dve, G["diff_out"] + m // 2)
            dve.wait_ge(s_x, X_DIFF + KD)
            norm_dve(dve, "ffn1")
            g1 = G["ffn1_in"]

            def ffn1_turn(i, at):
                split_slab(dve, g1 + 2 * i + 2, at + 2)
                split_slab(dve, g1 + 2 * i + 3, at + 3)
                up_times_gate(i, L, KF)

            ffn1_turn(0, g1)
            with dve.Fori(0, 5) as i:
                for t in range(2):
                    ffn1_turn(2 * i + 1 + t, g1 + 2 + 2 * t)
            ffn_out(1, G["ffn1_out"], L)
            dve.wait_ge(s_x, X_FFN1 + KD)
            norm_dve(dve, "second")
            units_dve(dve, link, LAT_UNITS)
            norm_dve(dve, "q_lat")
            norm_dve(dve, "kv_lat")
            units_dve(dve, link, MLA_UNITS)
            att_dve(dve, link, ATT["mla"])
            units_dve(dve, link, NA_UNITS)
            att_dve(dve, link, ATT["na"])
            for s in range(8):
                split_next(dve, G["out2"] + s)
            for t in range(2):
                dve.wait_ge(s_fin, 1)
                nc.vector.tensor_copy(big[:, t * D + 512:(t + 1) * D], ps[:, 2 * t + 1, :]).then_inc(s_fo, 1)

        @block.tensor
        def _(pe):
            pe.wait_ge(s_rows, 48)
            nc.tensor.transpose(ps[:, 0, 0:N_ADA], rows[0:N_ADA, 0:P], T["ident"][0:N_ADA, 0:N_ADA])
            nc.tensor.transpose(ps[:, 0, N_ADA:N_ADA + N_PAR], rows[0:N_PAR, P:2 * P],
                                T["ident"][0:N_PAR, 0:N_PAR]).then_inc(s_turn, 1)
            pe.wait_ge(s_turn_v, 2)
            for c in range(2):
                ins = nc.tensor.matmul(ps[:, 3 - 2 * c, c:c + 1], T["ones"][64 * c:64 * c + 64, :],
                                       sml[64 * c:64 * c + 64, 0:1], start=True, stop=True)
            ins.then_inc(s_turn, 1)
            pe.wait_ge(s_xin, 48)
            for k in range(KD):
                if k >= 2:
                    pe.wait_ge(s_turn_a, k - 1)
                    pe.wait_ge(s_turn_v, k + 1)
                for t in range(4):
                    ins = nc.tensor.transpose(ps[:, 4 + 2 * (t // 2) + k % 2, t % 2 * P:(t % 2 + 1) * P],
                                              xin[:, t, k * P:(k + 1) * P], T["ident"])
                ins.then_inc(s_turn, 1)
            meta = h32[0:N_META, 0:2, :].rearrange("p a b -> p (a b)")
            for k in range(KD):
                ins = nc.tensor.transpose(ps[:, 2, k * N_META:(k + 1) * N_META], meta[:, k * P:(k + 1) * P],
                                          T["ident"][0:N_META, 0:N_META])
            ins.then_inc(s_turn, 1)

            def ada_slab(at, half, g):
                pe.wait_ge(split, g + 1)
                for m in range(2):
                    for k in range(KD):
                        for w in (wh, wl):
                            wv = slab_view(w, at, KD, 256)
                            c = (2 * half + m) * 4
                            ins = nc.tensor.matmul(ps[:, 6, c:c + 4], wv[:, k, m * P:(m + 1) * P],
                                                   condr[:, k, :], start=(k == 0 and w is wh),
                                                   stop=(k == KD - 1 and w is wl))
                ins.then_inc(used, 1)

            def ada_pair(p, at, g, prior):
                positive(pe, s_adav, prior)
                ada_slab(at, 0, g)
                ada_slab(at + 1, 1, g + 1)
                pe.wait_ge(used, g + 2)
                pe.sem_inc(s_ada, 1)

            pe.wait_ge(s_cond, 2)
            pe.wait_ge(s_turn_a, KD)
            pe.wait_ge(s_turn_v, 3 + KD)
            for p in range(4):
                ada_pair(p, G["ada0"] + 2 * p, G["ada0"] + 2 * p, 3 * p)
            pe.wait_ge(s_turn_v, 3 + KD)
            norm_pe(pe, "fnet")

            def fnet_inner(i):
                if i == 0:
                    pe.wait_ge(s_tab, 16)
                pe.wait_ge(s_h, i + 1)
                if i >= 2:
                    pe.wait_ge(s_f1a, i - 1)
                    pe.wait_ge(s_f1v, i - 1)
                for t in range(4):
                    ins = nc.tensor.matmul(ps[:, 2 * (i % 2) + t // 2, t % 2 * L:(t % 2 + 1) * L],
                                           h32[:, i, t * P:(t + 1) * P], dft_g, start=True, stop=True)
                ins.then_inc(s_f1, 1)

            def fnet_outer(i):
                pe.wait_ge(s_f1a, i + 1)
                pe.wait_ge(s_f1v, i + 1)
                if i >= 2:
                    pe.wait_ge(s_f2v, i - 1)
                for s in range(2):
                    for t in range(2):
                        for c, tb in enumerate((cos_l, nsin_l)):
                            ins = nc.tensor.matmul(ps[:, 4 + i % 2, s * L:(s + 1) * L],
                                                   uv[:, i % 2, 2 * s + t, c * P:(c + 1) * P], tb[:, t, :],
                                                   start=(t == 0 and c == 0), stop=(t == 1 and c == 1))
                ins.then_inc(s_f2, 1)

            fnet_inner(0)
            for i in range(8):
                g = G["ada0"] + 8 + 2 * i
                ada_pair(4 + i, g, g, 3 * (4 + i))
                if i < 7:
                    fnet_inner(i + 1)
                fnet_outer(i)
            pe.wait_ge(s_f2v, 8)
            outproj_pe(pe, G["fnet_out"], NT, X_FNET)
            norm_pe(pe, "ffn0")

            def half_ffn(g, at, n, bank, done):
                pe.wait_ge(split, g + 1)
                whv, wlv = slab_view(wh, at, KD, 256), slab_view(wl, at, KD, 256)
                for m in range(2):
                    for k in range(KD):
                        c = slice(m * P, (m + 1) * P)
                        ins = product(ps[:, bank + m, 0:n], whv[:, k, c], wlv[:, k, c], hh[:, k, 0:n],
                                      hl[:, k, 0:n], k == 0, k == KD - 1)
                    ins.then_inc(done, 1)

            def ffn_pair(i, g, at, n, tile):
                positive(pe, s_silu, i * 2 + tile)
                half_ffn(g, at, n, 0, s_gate)
                pe.wait_ge(s_gate, i * 2 + (tile + 2))
                pe.sem_inc(used, 1)
                positive(pe, s_act, i * 2 + tile)
                half_ffn(g + 1, at + 1, n, 2, s_up)
                pe.wait_ge(s_up, i * 2 + (tile + 2))
                pe.sem_inc(used, 1)

            def ffn_out_slab(layer, g, at, s, n, first, last):
                pe.wait_ge(split, g + 1)
                whv, wlv = slab_view(wh, at, 2, D), slab_view(wl, at, 2, D)
                for kk in range(2):
                    pe.wait_ge(s_as, s * 2 + (layer * KF + kk + 1))
                    for m in range(KD):
                        c = slice(m * P, (m + 1) * P)
                        ins = product(ps[:, m, 0:n], whv[:, kk, c], wlv[:, kk, c], ah[:, kk, 0:n],
                                      al[:, kk, 0:n], first and kk == 0, last and kk == 1)
                    ins.then_inc(s_au, 1)
                pe.wait_ge(s_au, s * 2 + (layer * KF + 2))
                pe.sem_inc(used, 1)

            def ffn_out(layer, g0, n):
                pe.wait_ge(s_act, (layer + 1) * KF)
                if layer == 0:
                    pe.wait_ge(s_adav, 69)
                for s in range(3):
                    ffn_out_slab(layer, g0 + s, g0 + s, s, n, s == 0, False)
                with pe.Fori(0, 1) as i:
                    for j in range(4):
                        ffn_out_slab(layer, i * 4 + (g0 + 3 + j), g0 + 3 + j, i * 4 + (3 + j), n, False, False)
                for s in range(7, 11):
                    ffn_out_slab(layer, g0 + s, g0 + s, s, n, False, s == 10)
                pe.sem_inc(s_ffn, 1)

            pe.wait_ge(s_h, BASE["ffn0"] + KD)
            g = G["ffn0_in"]

            def ffn0_turn(i):
                ffn_pair(i, g + 4 * i, g, NT, 0)
                ada_pair(None, g + 2, g + 2 + 4 * i, i * 3 + 36)

            ffn0_turn(0)
            with pe.Fori(1, 11) as i:
                ffn0_turn(i)
            ffn_out(0, G["ffn0_out"], NT)
            pe.wait_ge(s_x, X_FFN0 + KD)
            ada_pair(11, G["ada1_tail"], G["ada1_tail"], 69)
            norm_pe(pe, "diff")
            pe.wait_ge(s_h, BASE["diff"] + KD)
            units_pe(pe, DIFF_UNITS)
            pe.wait_ge(s_urdy, 16)
            pe.wait_ge(s_ucp, 16)
            att_pe(pe, ATT["diff"])
            pe.wait_ge(s_os, 8)
            outproj_pe(pe, G["diff_out"], L, X_DIFF)
            norm_pe(pe, "ffn1")
            pe.wait_ge(s_h, BASE["ffn1"] + KD)
            g1 = G["ffn1_in"]
            ffn_pair(0, g1, g1, L, KF)
            with pe.Fori(0, 5) as i:
                for t in range(2):
                    ffn_pair(2 * i + 1 + t, g1 + 2 + 2 * t + 4 * i, g1 + 2 + 2 * t, L, KF)
            ffn_out(1, G["ffn1_out"], L)
            pe.wait_ge(s_x, X_FFN1 + KD)
            norm_pe(pe, "second")
            pe.wait_ge(s_h, BASE["second"] + KD)
            units_pe(pe, LAT_UNITS)
            norm_pe(pe, "q_lat")
            pe.wait_ge(s_rstd, ORDER.index("q_lat") + 1)
            norm_pe(pe, "kv_lat")
            pe.wait_ge(s_h, BASE["kv_lat"] + 2)
            units_pe(pe, MLA_UNITS)
            pe.wait_ge(s_urdy, ROPED[-1]["r"] + 1)
            pe.wait_ge(s_unrm, max(u["h"] for u in MLA_UNITS if u["kind"] == "head") + 1)
            pe.wait_ge(s_ucp, MLA_UNITS[-1]["c"] + 1)
            att_pe(pe, ATT["mla"])
            pe.wait_ge(s_on, ATT["mla"]["g0"] + 8)
            units_pe(pe, NA_UNITS)
            pe.wait_ge(s_unrm, max(u["h"] for u in NA_UNITS if u["kind"] == "head") + 1)
            pe.wait_ge(s_ucp, NA_UNITS[-1]["c"] + 1)
            att_pe(pe, ATT["na"])
            pe.wait_ge(s_ex, map_base)
            pe.wait_ge(s_os, 24)
            for s in range(8):
                g = G["out2"] + s
                pe.wait_ge(split, g + 1)
                whv, wlv = slab_view(wh, g, 2, D), slab_view(wl, g, 2, D)
                for kk in range(2):
                    k = 2 * s + kk
                    for t in range(2):
                        q = (L2 + t * P) if k < 8 else t * P
                        a_h, a_l = hh[:, k % 8, q:q + P], hl[:, k % 8, q:q + P]
                        for c in range(2):
                            o = ps[:, 2 * t + c, :]
                            n = slice(c * 512, (c + 1) * 512)
                            nc.tensor.matmul(o, a_h, whv[:, kk, n], start=(k == 0), stop=False)
                            nc.tensor.matmul(o, a_h, wlv[:, kk, n], start=False, stop=False)
                            ins = nc.tensor.matmul(o, a_l, whv[:, kk, n], start=False, stop=(k == 15))
                if s < 7:
                    ins.then_inc(used, 1)
            for t in range(2):
                for m in range(KD):
                    ins = nc.tensor.matmul(ps[:, 2 * t + m // 4, m % 4 * P:(m % 4 + 1) * P],
                                           x_lat[:, m, t * P:(t + 1) * P], T["ident"], start=False,
                                           stop=True, skip_group_check=True)
            ins.then_inc(s_fin, 1)


def kernel(**inputs):
    import concourse.bacc as _bacc
    from concourse.bass_utils import run_bass_kernel_spmd as _run

    def flat(name, *shape):
        return np.ascontiguousarray(inputs[name]).reshape(*shape)

    twice = lambda name: np.concatenate([flat(name, 1, 64)] * 2, 1)
    lam = flat("diff_lambda", 4, 64)
    params = np.concatenate([
        flat("norm_gain", 4 * KD, P), flat("fnet_b_out", KD, P), flat("norm_w_2", KD, P),
        flat("q_lat_norm_w_2", 2, P), flat("kv_lat_norm_w_2", 2, P), flat("diff_subln_gain", 1, P),
        flat("diff_q_gain", 1, P), flat("diff_k_gain", 1, P), flat("mla_qn_w_2", 1, P), flat("mla_kn_w_2", 1, P),
        twice("mla_qpe_w_2"), twice("mla_kpe_w_2"), twice("na_q_norm_w_2"), twice("na_k_norm_w_2"),
        np.concatenate([lam[0:1], lam[2:3]], 1), np.concatenate([lam[1:2], lam[3:4]], 1),
        flat("c", KD, P), flat("c_ctx", KD, P)], 0)
    tables = shape_tables()
    names = list(TABLE_COLS)
    kept = np.concatenate([tables[n] for n in names[:9]], 1).astype(np.float32)
    fourier = np.concatenate([tables[n] for n in names[9:]], 1).astype(np.float32)
    arrays = {
        "tables": kept, "fourier": fourier, "params": params, "b_ada": flat("b_ada", N_ADA, P),
        "meta_bias": flat("na_meta_bias_2", NA_HEADS * N_META),
        "rel_bias_rev": flat("na_rel_bias_2", -1)[::-1],
    }
    for name in ("x", "ctx", "w_ada", "ffn_w_in", "ffn_w_out", "fnet_w_out", "diff_w_in", "diff_w_out",
                 "meta_tokens_2", "w_in_2", "w_uq_2", "w_ukv_2", "w_out_2"):
        arrays[name] = inputs[name]
    arrays = {f"in_{n}": np.ascontiguousarray(a) for n, a in arrays.items()}

    nc = _bacc.Bacc("TRN2", target_bir_lowering=False, num_devices=1)
    d = {n[3:]: nc.dram_tensor(n, a.shape, mybir.dt.from_np(a.dtype), kind="ExternalInput").ap()
         for n, a in arrays.items()}
    out = nc.dram_tensor("out_0", (1, L, D), F32, kind="ExternalOutput").ap()
    build(nc, d, out)
    r = _run(nc, [arrays], core_ids=[0])
    return r.results[0]["out_0"]
```

```python
import math
from contextlib import ExitStack

import numpy as np
import concourse.bass as bass
from concourse import mybir

F32 = mybir.dt.float32
F32R = mybir.dt.float32r
ACT = mybir.ActivationFunctionType
ALU = mybir.AluOpType
AX_X = mybir.AxisListType.X

P = 128
D = 1024
KD = D // P
L = 256
LC = 256
NT = L + LC
GRID_W = 64
ROWS = L // GRID_W
EPS = 1e-6
D_FF = 2816
KF = D_FF // P
DIFF_HEADS = 8
DIFF_DIM = 64
LAM_INIT = 0.8 - 0.6 * math.exp(-0.3 * 1)
N_META = 16
L2 = L + N_META
MLA_HEADS, MLA_NOPE, MLA_ROPE, MLA_V, MLA_RANK = 8, 128, 64, 128, 256
NA_HEADS, NA_DIM, NA_WIN_R, NA_WIN_C = 16, 64, 8, 16
REL_R, REL_C = 2 * NA_WIN_R - 1, 2 * NA_WIN_C - 1
MASKED = -1e30

RAW_SLOTS = 4
SPLIT_SLOTS = 4
AHEAD = SPLIT_SLOTS
SLAB = 2048
HALF = SLAB // 2

IN_QLAT, IN_KVLAT, IN_KPE, IN_GMLA = 0, 256, 512, 576
IN_NAQ, IN_NAK, IN_NAV, IN_GNA = 1600, 2624, 3648, 4672

SLOTS_R = 2 * ROWS - 2
RUN = REL_C * (SLOTS_R - 1) + GRID_W
BIAS_W = N_META + SLOTS_R * GRID_W + N_META


def shape_tables():
    eye = np.eye(P)
    half = np.kron(np.eye(2), np.ones((64, 64)))
    rot = np.zeros((P, P))
    for m in range(P):
        if m % 64 < 32:
            rot[m + 32, m] = -1.0
        else:
            rot[m - 32, m] = 1.0
    g = np.arange(P)
    ang_g = 2 * np.pi * (np.outer(g, g) % P) / P
    t = np.arange(L)
    ang_l = 2 * np.pi * (np.outer(t, t) % L) / L
    norm = 1.0 / math.sqrt(L * P)
    dft_g = np.concatenate([np.cos(ang_g), np.sin(ang_g)], 1)
    cos_l = (np.cos(ang_l) * norm).reshape(2, P, L).transpose(1, 0, 2).reshape(P, 2 * L)
    nsin_l = (-np.sin(ang_l) * norm).reshape(2, P, L).transpose(1, 0, 2).reshape(P, 2 * L)

    f32 = np.float32
    inv = (f32(10000.0) ** (-np.arange(16, dtype=f32) / f32(16))).astype(f32)
    row = np.repeat(np.arange(ROWS, dtype=f32), GRID_W)
    col = np.tile(np.arange(GRID_W, dtype=f32), ROWS)
    ang = np.concatenate([row[:, None] * inv, col[:, None] * inv], -1).astype(f32).T
    ang_d = np.tile(ang, (4, 1))
    inv = (f32(10000.0) ** (-(np.arange(0, MLA_ROPE, 2, dtype=f32) / f32(MLA_ROPE)))).astype(f32)
    pos = np.concatenate([np.arange(N_META, L2), np.arange(N_META)]).astype(f32)
    ang = (pos[:, None] * inv).astype(f32).T
    ang_m = np.tile(ang, (4, 1))

    c = np.arange(P) % GRID_W
    c0 = np.clip(c - NA_WIN_C // 2, 0, GRID_W - NA_WIN_C)[:, None]
    kc = np.arange(GRID_W)[None, :]
    mask = np.where((kc >= c0) & (kc < c0 + NA_WIN_C), 0.0, MASKED)
    return {
        "ident": eye, "ones": np.ones((P, P)), "half": half, "rot": rot,
        "cos_d": np.cos(ang_d), "sin_d": np.sin(ang_d), "cos_m": np.cos(ang_m), "sin_m": np.sin(ang_m),
        "mask": mask, "fold": (np.arange(P)[:, None] % 2 == np.arange(2)) & (np.arange(P)[:, None] < 4),
        "dft_g": dft_g, "cos_l": cos_l, "nsin_l": nsin_l,
    }


TABLE_COLS = {"ident": P, "ones": P, "half": P, "rot": P, "cos_d": L, "sin_d": L, "cos_m": L2, "sin_m": L2,
              "mask": GRID_W, "fold": 2, "dft_g": 2 * P, "cos_l": 2 * L, "nsin_l": 2 * L}
N_KEPT = 10
KEPT = sum(list(TABLE_COLS.values())[:N_KEPT])
FOURIER = 2 * P + 4 * L

PAR_ROWS = {"norm_gain": 4 * KD, "fnet_b": KD, "norm_w": KD, "q_lat": 2, "kv_lat": 2, "subln": 1, "dq": 1,
            "dk": 1, "qn": 1, "kn": 1, "qpe": 1, "kpe": 1, "naq": 1, "nak": 1, "lam_a": 1, "lam_b": 1,
            "c": KD, "c_ctx": KD}
PAR_AT = {}
for _name, _n in PAR_ROWS.items():
    PAR_AT[_name] = sum(PAR_ROWS[x] for x in list(PAR_ROWS)[:list(PAR_ROWS).index(_name)])
N_PAR = sum(PAR_ROWS.values())
N_ADA = 2 * 6 * KD


def slab_starts():
    stages = [("ada0", 24), ("fnet_out", 6), ("ffn0_in", 44), ("ffn0_out", 11),
              ("diff_k", 4), ("diff_q", 4), ("diff_v", 4), ("diff_out", 4), ("ffn1_in", 22), ("ffn1_out", 11),
              ("lat", 2), ("kpe", 1), ("gmla", 4), ("uq", 2), ("ukv", 2),
              ("naq", 4), ("nak", 4), ("nav", 4), ("gna", 4), ("out2", 8)]
    at, out = 0, {}
    for name, n in stages:
        out[name] = at
        at += n
    out["end"] = at
    return out


G = slab_starts()
FNET_OUT_Q = [2 * G["fnet_out"] + m + 2 * (m >= 4) + 2 * (m >= 6) for m in range(KD)]


def build(nc, d, out):
    with ExitStack() as ctx:
        def sb(name, shape, dt=F32):
            return ctx.enter_context(nc.sbuf_tensor(name, shape, dt))

        def sem(name):
            return ctx.enter_context(nc.semaphore(name))

        ps = ctx.enter_context(nc.psum_tensor("ps", [P, 8, 512], F32))
        x_lat = sb("x_lat", [P, KD, L])
        x_ctx = sb("x_ctx", [P, KD, LC])
        x_meta = sb("x_meta", [P, KD, N_META])
        HW = L2 + L
        hh = sb("hh", [P, KD, HW], F32R)
        hl = sb("hl", [P, KD, HW], F32R)
        ah = sb("ah", [P, 2, HW], F32R)
        al = sb("al", [P, 2, HW], F32R)
        raw = sb("raw", [P, RAW_SLOTS, SLAB])
        wh = sb("wh", [P, SPLIT_SLOTS, HALF], F32R)
        wl = sb("wl", [P, SPLIT_SLOTS, HALF], F32R)
        big = sb("big", [P, 13824])
        tab = sb("tab", [P, KEPT])
        ex = sb("ex", [P, 2, 2, 512])
        sq = sb("sq", [P, 2, HW])
        rstd = sb("rstd", [P, 2, HW])
        nrm = sb("nrm", [P, 2, HW])
        t1 = sb("t1", [P, L2])
        rows = big[:, 12000:12000 + 2 * P]
        par = sb("par", [P, N_ADA + N_PAR])
        ada = sb("ada", [P, 2, 6 * KD, 2])
        ada_flat = ada[:].rearrange("p l s c -> p (l s) c")
        ada_row = rstd[:, 1, 0:512]
        gsc = sb("gsc", [P, 2, 2, KD, 2])
        gb = sb("gb", [P, KD, 2])
        cond = sb("cond", [P, 2 * KD])
        condr = sb("condr", [P, KD, 4], F32R)
        eps_c = sb("eps_c", [P, 1])
        sml = sb("sml", [P, 16])
        nm = sb("nm", [P, 2, 2])
        sm = sb("sm", [P, 2, 2])
        rc = sb("rc", [P, 2, 2])
        meta_b = sb("meta_b", [P, NA_HEADS * N_META])
        subg = sb("subg", [P, 1])

        T, at = {}, 0
        for name in list(TABLE_COLS)[:N_KEPT]:
            T[name] = tab[:, at:at + TABLE_COLS[name]]
            at += TABLE_COLS[name]

        def view(at, n, pattern=None, **kw):
            v = big[:, at:at + n]
            return v.rearrange(pattern, **kw) if pattern else v

        xin = view(0, 4096, "p (t d) -> p t d", t=4)
        h32 = view(4096, 4096, "p (k n) -> p k n", k=KD)
        uv = view(8192, 2048, "p (s t c) -> p s t c", s=2, t=4)
        dft_g = view(10240, 2 * P)
        cos_l = view(10240 + 2 * P, 2 * L, "p (t n) -> p t n", t=2)
        nsin_l = view(10240 + 2 * P + 2 * L, 2 * L, "p (t n) -> p t n", t=2)
        dq = view(0, 2048, "p (h n) -> p h n", h=8)
        dk = view(2048, 4096, "p (h n) -> p h n", h=8)
        dv = view(6144, 4096, "p (t e) -> p t e", t=4)
        qn = view(0, 2048, "p (h n) -> p h n", h=8)
        qp = view(2048, 2048, "p (h n) -> p h n", h=8)
        kn = view(4096, 8 * L2, "p (h n) -> p h n", h=8)
        kp = view(6272, L2)
        mv = view(6544, 3072, "p (t e) -> p t e", t=3)
        mg = view(9616, 2048, "p (h n) -> p h n", h=8)
        lat32 = ex[:].rearrange("p a b c -> p (a b c)")[:, 0:2 * HW].rearrange("p (k n) -> p k n", k=2)
        nq = view(0, 2048, "p (h n) -> p h n", h=8)
        nkx = view(2048, 8 * (L2 + N_META), "p (h n) -> p h n", h=8)
        nv = view(4352, 3072, "p (t e) -> p t e", t=3)
        ng = view(7424, 2048, "p (h n) -> p h n", h=8)
        runs = view(9472, NA_HEADS * RUN, "p (h n) -> p h n", h=NA_HEADS)
        bias = view(12976, 2 * BIAS_W, "p (s n) -> p s n", s=2)
        wT = x_ctx[:].rearrange("p k n -> p (k n)").rearrange("p (s c n) -> p s c n", s=2, c=4)

        def par_of(name, k=0, n=1):
            at = N_ADA + PAR_AT[name] + k
            return par[:, at:at + n]

        s_rows = sem("rows_landed")
        s_tab = sem("tables_landed")
        s_xin = sem("x_landed")
        landed = [sem(f"slab_landed_{i}") for i in range(RAW_SLOTS)]
        rounded = sem("half_rounded")
        split = sem("half_split")
        used = sem("half_used")
        s_turn = sem("turned")
        s_turn_a = sem("turned_out_act")
        s_turn_v = sem("turned_out_dve")
        s_cond = sem("cond_ready")
        s_adac = sem("ada_pair_copied")
        s_adat = sem("ada_pair_turned")
        s_adav = sem("ada_pair_out")
        s_mod = sem("modulation_ready")
        a_ch = sem("act_chain")
        v_ch = sem("dve_chain")
        s_sq = sem("norm_squared")
        s_sum = sem("norm_summed")
        s_rstd = sem("norm_rstd")
        s_mul = sem("norm_scaled")
        s_hh = sem("norm_rounded")
        s_h = sem("norm_out")
        s_f1 = sem("fnet_inner")
        s_f1a = sem("fnet_inner_out_act")
        s_f1v = sem("fnet_inner_out_dve")
        s_f2 = sem("fnet_outer")
        s_f2a = sem("fnet_rounded")
        s_f2v = sem("fnet_split")
        s_opa = sem("outproj_biased")
        s_x = sem("x_updated")
        s_silu = sem("gate_silu")
        s_fin = sem("ffn_tile_complete")
        s_act = sem("act_written")
        s_ar = sem("act_rounded")
        s_as = sem("act_split")
        s_unit = sem("unit_done")
        s_usq = sem("unit_squared")
        s_usum = sem("unit_summed")
        s_urs = sem("unit_rstd")
        s_unrm = sem("unit_normed")
        s_urot = sem("unit_rotated")
        s_ucp = sem("unit_copied")
        s_urdy = sem("unit_ready")
        s_sc = sem("scores_done")
        s_sb = sem("scores_biased")
        s_mx = sem("row_max")
        s_ex = sem("exp_done")
        s_w = sem("weights_ready")
        s_tr = sem("weights_turned")
        s_trc = sem("weights_copied")
        s_pv = sem("pv_done")
        s_osq = sem("o_squared")
        s_osum = sem("o_summed")
        s_ors = sem("o_rstd")
        s_on = sem("o_scaled")
        s_or = sem("o_rounded")
        s_os = sem("o_split")
        s_bias = sem("bias_ready")
        s_runs = sem("bias_runs_landed")
        s_metab = sem("meta_bias_landed")
        s_fo = sem("final_copied")
        s_out = sem("out_stored")
        s_eps = sem("eps_written")

        def positive(eng, s, value):
            if type(value) is int and value <= 0:
                return
            eng.wait_ge(s, value)

        def raw_half(at):
            g, half = divmod(at, 2)
            v = raw[:, g % RAW_SLOTS, :]
            if G["ffn0_out"] <= g < G["ffn0_out"] + 11 or G["ffn1_out"] <= g < G["ffn1_out"] + 11 \
                    or g >= G["out2"]:
                return v[:, half * D:(half + 1) * D], D, 1
            if g == G["kpe"]:
                return v[:, half * 256:(half + 1) * 256], 256, 1
            k, n = {G["uq"]: (2, 768), G["uq"] + 1: (2, 768), G["ukv"]: (2, 1024),
                    G["ukv"] + 1: (2, 1024)}.get(g, (KD, 256))
            v = v[:, 0:k * n].rearrange("p (k n) -> p k n", k=k)[:, :, half * n // 2:(half + 1) * n // 2]
            return v, k * n // 2, k

        def split_half(which, at):
            _, n, k = raw_half(at)
            v = which[:, at % SPLIT_SLOTS, 0:n]
            return v.rearrange("p (k n) -> p k n", k=k) if k > 1 else v

        def round_half(act, q, at):
            act.wait_ge(landed[at // 2 % RAW_SLOTS], 2 * (q - at) + 16 * (at // 2 // RAW_SLOTS + 1))
            positive(act, used, q - SPLIT_SLOTS + 1)
            nc.scalar.activation(split_half(wh, at), raw_half(at)[0], ACT.Copy).then_inc(rounded, 1)

        def split_low(dve, q, at):
            dve.wait_ge(rounded, q + 1)
            nc.vector.tensor_tensor(split_half(wl, at), raw_half(at)[0], split_half(wh, at).bitcast(F32),
                                    ALU.subtract).then_inc(split, 1)

        def load_slab(sp, g, at, src, k, n):
            positive(sp, split, 2 * (g - RAW_SLOTS + 1))
            sp.dma_start(raw[:, at % RAW_SLOTS, 0:k * n].rearrange("p (k n) -> p k n", k=k),
                         src.rearrange("(k p) n -> p k n", p=P)).then_inc(landed[at % RAW_SLOTS], 16)

        def tile_of(which, at, k, n):
            return which[:, at % SPLIT_SLOTS, 0:k * n].rearrange("p (k n) -> p k n", k=k)

        def product(o, w_hi, w_lo, m_hi, m_lo, first, last, **kw):
            nc.tensor.matmul(o, w_hi, m_hi, start=first, stop=False, **kw)
            nc.tensor.matmul(o, w_hi, m_lo, start=False, stop=False, **kw)
            return nc.tensor.matmul(o, w_lo, m_hi, start=False, stop=last, **kw)

        def round_next(act, q, n=1):
            for h in range(q, q + n):
                if h + AHEAD < 2 * G["end"]:
                    round_half(act, h + AHEAD, h + AHEAD)

        def split_next(dve, q, n=1):
            for h in range(q, q + n):
                if h + AHEAD < 2 * G["end"]:
                    split_low(dve, h + AHEAD, h + AHEAD)

        def mod_parts(layer, n, ctx_too):
            sec = 0 if n == 0 else 3
            parts = [(lambda k: x_lat[:, k, :], 0, L, lambda k: gsc[:, layer, n, k, 0:1],
                      lambda k: ada[:, layer, sec * KD + k, 0:1])]
            if ctx_too:
                parts.append((lambda k: x_ctx[:, k, :], L, LC, lambda k: gsc[:, layer, n, k, 1:2],
                              lambda k: ada[:, layer, sec * KD + k, 1:2]))
            return parts

        NORMS = {
            "fnet": (KD, D, mod_parts(0, 0, True), None, None),
            "ffn0": (KD, D, mod_parts(0, 1, True), hh, hl),
            "diff": (KD, D, mod_parts(1, 0, True), hh, hl),
            "ffn1": (KD, D, mod_parts(1, 1, False), hh, hl),
            "second": (KD, D, [(lambda k: x_lat[:, k, :], 0, L, lambda k: par_of("norm_w", k), None),
                               (lambda k: x_meta[:, k, :], L, N_META, lambda k: par_of("norm_w", k), None)],
                       hh, hl),
            "lat": (2, MLA_RANK, [(lambda k: lat32[:, k, 0:L], 0, L, lambda k: par_of("q_lat", k), None),
                                  (lambda k: lat32[:, k, L:HW], L, L2, lambda k: par_of("kv_lat", k), None)],
                    ah, al),
        }
        BASE, SPLIT_BASE, at = {}, {}, 0
        at_s = 0
        for name, (tiles, *_rest) in NORMS.items():
            BASE[name], SPLIT_BASE[name] = at, at_s
            at += tiles
            at_s += tiles if _rest[2] is not None else 0
        ORDER = list(NORMS)
        SUMS = {"fnet": [(5, 0, NT)], "ffn0": [(5, 0, NT)], "diff": [(0, 0, NT)], "ffn1": [(7, 0, L)],
                "second": [(0, 0, L2)], "lat": [(7, 0, L), (6, L, HW)]}

        def norm_square(act, name, k):
            _, _, parts, _, _ = NORMS[name]
            b = BASE[name]
            if name in X_OF:
                act.wait_ge(s_x, X_OF[name] + k + 1)
            if k >= 2:
                act.wait_ge(s_sum, b + k - 1)
            at = 0
            for src, _, w, _, _ in parts:
                ins = nc.scalar.activation(sq[:, k % 2, at:at + w], src(k), ACT.Square)
                at += w
            ins.then_inc(s_sq, 1)

        def norm_rstd(act, link, name):
            tiles, dim, parts, _, _ = NORMS[name]
            n = sum(p[2] for p in parts)
            act.wait_ge(s_sum, BASE[name] + tiles)
            for bank, a, b in SUMS[name]:
                ins = nc.scalar.activation(rstd[:, 1, a:b], ps[:, bank, 0:b - a], ACT.Ln, bias=eps_c[:, 0:1],
                                           scale=1.0 / dim)
            link(ins)
            nc.scalar.activation(rstd[:, 0, 0:n], rstd[:, 1, 0:n], ACT.Exp, scale=-0.5).then_inc(s_rstd, 1)

        def norm_round(act, name):
            tiles, _, parts, hi, _ = NORMS[name]
            for k in range(tiles):
                act.wait_ge(s_mul, BASE[name] + k + 1)
                at = 0
                for _, off, w, _, shift in parts:
                    ins = nc.scalar.activation(hi[:, k, off:off + w], nrm[:, k % 2, at:at + w], ACT.Identity,
                                               bias=shift(k) if shift else 0.0)
                    at += w
                ins.then_inc(s_hh, 1)

        def norm_act(act, link, name):
            for k in range(NORMS[name][0]):
                norm_square(act, name, k)
            norm_rstd(act, link, name)
            if NORMS[name][3] is not None:
                norm_round(act, name)

        def norm_dve(dve, name):
            tiles, _, parts, hi, lo = NORMS[name]
            b, sb_ = BASE[name], SPLIT_BASE[name]
            dve.wait_ge(s_rstd, ORDER.index(name) + 1)
            positive(dve, s_h, b)

            def scaled(k):
                if k >= 2:
                    dve.wait_ge(s_h, b + k - 1)
                at = 0
                for src, _, w, scale, _ in parts:
                    ins = nc.vector.scalar_tensor_tensor(out=nrm[:, k % 2, at:at + w], in0=src(k),
                                                         scalar=scale(k), in1=rstd[:, 0, at:at + w],
                                                         op0=ALU.mult, op1=ALU.mult)
                    at += w
                ins.then_inc(s_mul, 1)

            def shifted(k):
                dve.wait_ge(s_mul, b + k + 1)
                if hi is not None:
                    dve.wait_ge(s_hh, sb_ + k + 1)
                at = 0
                for _, off, w, _, shift in parts:
                    src = nrm[:, k % 2, at:at + w]
                    if hi is None:
                        ins = nc.vector.tensor_scalar(h32[:, k, off:off + w], src, shift(k), None, ALU.add)
                    else:
                        ins = nc.vector.scalar_tensor_tensor(
                            out=lo[:, k, off:off + w], in0=src, scalar=shift(k) if shift else 0.0,
                            in1=hi[:, k, off:off + w].bitcast(F32), op0=ALU.add, op1=ALU.subtract)
                    at += w
                ins.then_inc(s_h, 1)

            scaled(0)
            for k in range(tiles):
                if k + 1 < tiles:
                    scaled(k + 1)
                shifted(k)

        def norm_sum(pe, name, k):
            tiles, _, parts, _, _ = NORMS[name]
            pe.wait_ge(s_sq, BASE[name] + k + 1)
            for bank, a, b in SUMS[name]:
                ins = nc.tensor.matmul(ps[:, bank, 0:b - a], T["ones"], sq[:, k % 2, a:b], start=(k == 0),
                                       stop=(k == tiles - 1))
            ins.then_inc(s_sum, 1)

        def norm_pe(pe, name):
            for k in range(NORMS[name][0]):
                norm_sum(pe, name, k)

        def unit(kind, q, k, col, cols, width, frees, **kw):
            return dict(kind=kind, q=q, k=k, col=col, cols=cols, w=width, frees=frees, **kw)

        def seg(dst, a, b):
            return (dst, a, b)

        DIFF_UNITS, LAT_UNITS, GATE_UNITS, MLA_UNITS, NA_UNITS = [], [], [], [], []
        for h in range(8):
            DIFF_UNITS.append(unit("head", 2 * G["diff_k"] + h, KD, 0, P, NT, 1,
                                   red="half", dim=64, gain="dk", rope=("cos_d", "sin_d", L),
                                   out=[seg(dk[:, h, L:NT], L, NT)], dst=dk[:, h, 0:L]))
        for h in range(8):
            DIFF_UNITS.append(unit("head", 2 * G["diff_q"] + h, KD, 0, P, L, 1,
                                   red="half", dim=64, gain="dq", rope=("cos_d", "sin_d", L), out=[],
                                   dst=dq[:, h, :]))
        for s in range(4):
            for t in range(4):
                DIFF_UNITS.append(unit("token", 2 * (G["diff_v"] + s) + 1, KD, 0, 256, P, 2 * (t == 3), tok=t * P,
                                       dst=dv[:, t, s * 256:(s + 1) * 256]))
        for m in range(2):
            LAT_UNITS.append(unit("copy", 2 * G["lat"] + m, KD, 0, P, L, 1, dst=lat32[:, m, 0:L]))
        for m in range(2):
            LAT_UNITS.append(unit("copy", 2 * G["lat"] + 2 + m, KD, 0, P, L2, 1, dst=lat32[:, m, L:HW]))
        LAT_UNITS.append(unit("head", 2 * G["kpe"] + 1, KD, 0, MLA_ROPE, L2, 2, red="ones", dim=64,
                              gain="kpe", rope=("cos_m", "sin_m", L2), out=[], dst=kp[0:MLA_ROPE, :]))
        hd = MLA_NOPE + MLA_ROPE
        for h in range(8):
            q = 2 * G["uq"] + h // 2
            MLA_UNITS.append(unit("head", q, 2, h % 2 * hd, P, L, 0, red="ones",
                                  dim=128, gain="qn", rope=None, out=[seg(qn[:, h, :], 0, L)], src=0))
            MLA_UNITS.append(unit("head", q, 2, h % 2 * hd + P, MLA_ROPE, L, h % 2,
                                  red="ones", dim=64, gain="qpe", rope=("cos_m", "sin_m", L), out=[],
                                  dst=qp[0:MLA_ROPE, h, :], src=0))
        for h2 in range(4):
            q = 2 * G["ukv"] + h2
            for j in range(2):
                h = 2 * h2 + j
                MLA_UNITS.append(unit("head", q, 2, j * 256, P, L2, 0, red="ones",
                                      dim=128, gain="kn", rope=None, out=[seg(kn[:, h, :], 0, L2)], src=L))
            for t in range(3):
                MLA_UNITS.append(unit("token", q, 2, None, 256, P if t < 2 else N_META,
                                      int(t == 2), tok=L + t * P, src=L,
                                      dst=mv[0:(P if t < 2 else N_META), t, h2 * 256:(h2 + 1) * 256]))
        for m in range(8):
            GATE_UNITS.append(unit("silu", 2 * G["gmla"] + m, KD, 0, P, L, 1, dst=mg[:, m, :]))
        for m in range(8):
            NA_UNITS.append(unit("head", 2 * G["naq"] + m, KD, 0, P, L, 1, red="half",
                                 dim=64, gain="naq", rope=None, out=[seg(nq[:, m, :], 0, L)]))
        for m in range(8):
            NA_UNITS.append(unit("head", 2 * G["nak"] + m, KD, 0, P, L2, 1, red="half",
                                 dim=64, gain="nak", rope=None,
                                 out=[seg(nkx[:, m, 0:N_META], L, L2),
                                      seg(nkx[:, m, N_META:N_META + L2], 0, L2)]))
        for s in range(4):
            for t in range(3):
                NA_UNITS.append(unit("token", 2 * (G["nav"] + s) + 1, KD, 0, 256, P if t < 2 else N_META,
                                     2 * (t == 2), tok=t * P,
                                     dst=nv[0:(P if t < 2 else N_META), t, s * 256:(s + 1) * 256]))
        for m in range(8):
            NA_UNITS.append(unit("silu", 2 * G["gna"] + m, KD, 0, P, L, 1, dst=ng[:, m, :]))
        PHASES = [DIFF_UNITS, LAT_UNITS, GATE_UNITS, MLA_UNITS, NA_UNITS]
        n_unit = n_head = n_rope = n_copy = n_mid = 0
        for phase in PHASES:
            for u in phase:
                u["u"] = n_unit
                n_unit += 1
                n_mid += not u["frees"]
                u["mid"] = n_mid
                if u["kind"] == "head":
                    u["h"] = n_head
                    n_head += 1
                    if u["rope"]:
                        u["r"] = n_rope
                        n_rope += 1
                else:
                    u["c"] = n_copy
                    n_copy += 1
        ALL_UNITS = [u for phase in PHASES for u in phase]
        ROPED = [u for u in ALL_UNITS if u.get("rope")]

        def unit_out(u):
            bank = u["u"] % 3
            if u["kind"] == "token":
                return ps[0:u["w"], bank, 0:u["cols"]]
            return ps[0:u["cols"], bank, 0:u["w"]]

        def unit_done(eng, u):
            if u["frees"]:
                eng.wait_ge(used, u["q"] + 1)
            else:
                eng.wait_ge(s_unit, u["mid"])

        def unit_pe(pe, u, first_of_half, h_base):
            if first_of_half:
                pe.wait_ge(split, u["q"] + 1)
            if u["u"] >= 3:
                v = ALL_UNITS[u["u"] - 3]
                if v["kind"] == "head":
                    pe.wait_ge(s_unrm, v["h"] + 1)
                else:
                    pe.wait_ge(s_ucp, v["c"] + 1)
            mh, ml = (ah, al) if "src" in u else (hh, hl)
            off = u.get("src", 0)
            o = unit_out(u)
            q = u["q"]
            for k in range(u["k"]):
                first, last = k == 0, k == u["k"] - 1
                if h_base is not None:
                    pe.wait_ge(s_h, h_base + k + 1)
                if u["kind"] == "token":
                    tok = slice(u["tok"], u["tok"] + u["w"])
                    if u["col"] is None:
                        def cols(w):
                            return tile_of(w, q, 2, 512)[:, k, :].rearrange("p (h two e) -> p h two e", h=2,
                                                                            two=2)[:, :, 1, :]
                    else:
                        def cols(w):
                            at = (q - 1) % SPLIT_SLOTS
                            return w[:, at:at + 2, k * P:(k + 1) * P]
                    oo = o.rearrange("p (h e) -> p h e", h=2)
                    nc.tensor.matmul(oo, mh[:, k, tok], cols(wh), start=first, stop=False)
                    nc.tensor.matmul(oo, mh[:, k, tok], cols(wl), start=False, stop=False)
                    ins = nc.tensor.matmul(oo, ml[:, k, tok], cols(wh), start=False, stop=last)
                elif q == 2 * G["kpe"] + 1:
                    at = q - 1 + k // 4
                    m = slice(off, off + u["w"])
                    ins = product(o, tile_of(wh, at, 4, MLA_ROPE)[:, k % 4, :],
                                  tile_of(wl, at, 4, MLA_ROPE)[:, k % 4, :], mh[:, k, m], ml[:, k, m], first, last)
                else:
                    n = P if u["k"] == KD else (384 if q < 2 * G["ukv"] else 512)
                    whv, wlv = tile_of(wh, q, u["k"], n), tile_of(wl, q, u["k"], n)
                    c = slice(u["col"], u["col"] + u["cols"])
                    m = slice(off, off + u["w"])
                    ins = product(o, whv[:, k, c], wlv[:, k, c], mh[:, k, m], ml[:, k, m], first, last)
            if u["frees"]:
                ins.then_inc(used, u["frees"])
            else:
                ins.then_inc(s_unit, 1)

        def units_pe(pe, phase, h_base=None):
            for i in range(len(phase) + 2):
                if i < len(phase):
                    unit_pe(pe, phase[i], i == 0 or phase[i - 1]["q"] != phase[i]["q"],
                            h_base if i == 0 else None)
                if 1 <= i <= len(phase) and phase[i - 1]["kind"] == "head":
                    u = phase[i - 1]
                    h, m = u["h"], u["cols"]
                    pe.wait_ge(s_usq, h + 1)
                    positive(pe, s_urs, h - 1)
                    nc.tensor.matmul(ps[0:m, 3 + h % 2, 0:u["w"]], T[u["red"]][0:m, 0:m],
                                     sq[0:m, h % 2, 0:u["w"]], start=True, stop=True).then_inc(s_usum, 1)
                if 2 <= i and phase[i - 2].get("rope"):
                    u = phase[i - 2]
                    m, w = u["cols"], u["rope"][2]
                    pe.wait_ge(s_unrm, u["h"] + 1)
                    positive(pe, s_urdy, u["r"] - 1)
                    nc.tensor.matmul(ps[0:m, 5 + u["r"] % 2, 0:w], T["rot"][0:m, 0:m],
                                     nrm[0:m, u["h"] % 2, 0:w], start=True, stop=True).then_inc(s_urot, 1)

        def units_act(act, link, phase):
            for i in range(len(phase) + 1):
                if i < len(phase):
                    u = phase[i]
                    unit_done(act, u)
                    if u["kind"] == "head":
                        positive(act, s_usum, u["h"] - 1)
                        nc.scalar.activation(sq[0:u["cols"], u["h"] % 2, 0:u["w"]], unit_out(u),
                                             ACT.Square).then_inc(s_usq, 1)
                    else:
                        f = ACT.Silu if u["kind"] == "silu" else ACT.Copy
                        nc.scalar.activation(u["dst"], unit_out(u), f).then_inc(s_ucp, 1)
                    if u["frees"]:
                        round_next(act, u["q"] + 1 - u["frees"], u["frees"])
                if i >= 1 and phase[i - 1]["kind"] == "head":
                    u = phase[i - 1]
                    m, w = u["cols"], u["w"]
                    act.wait_ge(s_usum, u["h"] + 1)
                    positive(act, s_unrm, u["h"])
                    link(nc.scalar.activation(rstd[0:m, 1, 0:w], ps[0:m, 3 + u["h"] % 2, 0:w], ACT.Ln,
                                              bias=eps_c[0:m, 0:1], scale=1.0 / u["dim"]))
                    nc.scalar.activation(rstd[0:m, 0, 0:w], rstd[0:m, 1, 0:w], ACT.Exp,
                                         scale=-0.5).then_inc(s_urs, 1)

        def units_dve(dve, link, phase):
            for i in range(len(phase) + 2):
                if i < len(phase) and phase[i]["frees"]:
                    split_next(dve, phase[i]["q"] + 1 - phase[i]["frees"], phase[i]["frees"])
                if 1 <= i <= len(phase) and phase[i - 1]["kind"] == "head":
                    u = phase[i - 1]
                    m = u["cols"]
                    o = unit_out(u)
                    dve.wait_ge(s_urs, u["h"] + 1)
                    outs = list(u["out"])
                    if u["rope"]:
                        w = u["rope"][2]
                        old = [v for v in ROPED if v["h"] == u["h"] - 2]
                        if old:
                            dve.wait_ge(s_urdy, old[0]["r"] + 1)
                        outs.append((nrm[0:m, u["h"] % 2, 0:w], 0, w))
                    for dst, a, b in outs:
                        ins = nc.vector.scalar_tensor_tensor(
                            out=dst, in0=o[:, a:b], scalar=par_of(u["gain"])[0:m, :], in1=rstd[0:m, 0, a:b],
                            op0=ALU.mult, op1=ALU.mult)
                    ins.then_inc(s_unrm, 1)
                if i >= 2 and phase[i - 2].get("rope"):
                    u = phase[i - 2]
                    m = u["cols"]
                    cos, sin, w = u["rope"]
                    dve.wait_ge(s_unrm, u["h"] + 1)
                    positive(dve, s_urdy, u["r"])
                    tile = nrm[0:m, u["h"] % 2, 0:w]
                    link(nc.vector.tensor_tensor(t1[0:m, 0:w], tile, T[cos][0:m, 0:w], ALU.mult))
                    dve.wait_ge(s_urot, u["r"] + 1)
                    link(nc.vector.tensor_tensor(tile, ps[0:m, 5 + u["r"] % 2, 0:w], T[sin][0:m, 0:w],
                                                 ALU.mult))
                    nc.vector.tensor_tensor(u["dst"], t1[0:m, 0:w], tile, ALU.add).then_inc(s_urdy, 1)
            done = [u for u in phase if u.get("rope")]
            if done:
                dve.wait_ge(s_urdy, done[-1]["r"] + 1)

        def chunk_plan(keys):
            return [(a, min(P, keys - a)) for a in range(0, keys, P)]

        ATT = {
            "diff": dict(heads=8, maps=2, keys=NT, scale=DIFF_DIM ** -0.5, pair=1),
            "mla": dict(heads=8, maps=1, keys=L2, scale=(MLA_NOPE + MLA_ROPE) ** -0.5, pair=1),
            "na": dict(heads=16, maps=1, keys=L2, scale=NA_DIM ** -0.5, pair=2),
        }
        step_base = head_base = group_base = map_base = 0
        for name, a in ATT.items():
            a.update(name=name, steps=2 * a["heads"], s0=step_base, h0=head_base, g0=group_base, m0=map_base)
            a["groups"] = a["heads"] // a["pair"]
            step_base += a["steps"]
            head_base += a["heads"]
            group_base += a["groups"]
            map_base += a["maps"] * a["steps"]

        def scores_of(a, h, t, c):
            q = slice(t * P, (t + 1) * P)
            if a["name"] == "diff":
                r = slice(64 * c, 64 * c + 64)
                return [(dq[r, h, q], dk[r, h, :])]
            if a["name"] == "mla":
                return [(qn[:, h, q], kn[:, h, :]), (qp[0:MLA_ROPE, h, q], kp[0:MLA_ROPE, :])]
            r = slice(64 * (h % 2), 64 * (h % 2) + 64)
            off = N_META if t == 0 else 0
            return [(nq[r, h // 2, q], nkx[r, h // 2, off:off + L2])]

        def chunks_of(a, t):
            if a["name"] == "na" and t == 1:
                return [(N_META, P), (N_META + P, P), (0, N_META)]
            return chunk_plan(a["keys"])

        def values_of(a, h, j, n):
            v = {"diff": dv, "mla": mv, "na": nv}[a["name"]]
            w = P // a["pair"]
            return v[0:n, j, h * w:(h + 1) * w]

        def score_bank(a, i, c):
            return (i % 2) * a["maps"] + c

        def o_psum(a, f):
            return ps[:, 6 + f % 2, 0:L]

        def att_pe(pe, a):
            for i in range(a["steps"] + 6):
                if i < a["steps"]:
                    h, t = divmod(i, 2)
                    if i >= 2:
                        pe.wait_ge(s_ex, a["m0"] + (i - 1) * a["maps"])
                    for c in range(a["maps"]):
                        pairs = scores_of(a, h, t, c)
                        for j, (w, m) in enumerate(pairs):
                            ins = nc.tensor.matmul(ps[:, score_bank(a, i, c), 0:a["keys"]], w, m,
                                                   start=(j == 0), stop=(j == len(pairs) - 1))
                    ins.then_inc(s_sc, 1)
                if 2 <= i < a["steps"] + 2:
                    j0 = i - 2
                    pe.wait_ge(s_w, a["s0"] + j0 + 1)
                    positive(pe, s_trc, a["s0"] + j0 - 1)
                    for j, (at, n) in enumerate(chunks_of(a, j0 % 2)):
                        ins = nc.tensor.transpose(ps[0:n, 4 + j0 % 2, j * P:(j + 1) * P],
                                                  ex[:, j0 % 2, 0, at:at + n], T["ident"])
                    ins.then_inc(s_tr, 1)
                if a["name"] == "diff" and i % 2 == 0 and 0 <= (i - 6) // 2 < a["heads"]:
                    sub_sum(pe, a, (i - 6) // 2)
                if i % 2 == 0 and 0 <= (i - 4) // 2 < a["heads"]:
                    h = (i - 4) // 2
                    f = h // a["pair"]
                    pe.wait_ge(s_trc, a["s0"] + 2 * h + 2)
                    if h % a["pair"] == 0:
                        positive(pe, s_on, a["g0"] + f - 1)
                    part = P // a["pair"]
                    row = h % a["pair"] * part
                    plan = chunk_plan(a["keys"])
                    for j, (_, n) in enumerate(plan):
                        ins = nc.tensor.matmul(o_psum(a, f)[row:row + part, :], values_of(a, h, j, n),
                                               wT[0:n, h % 2, j, :], start=(j == 0), stop=(j == len(plan) - 1))
                    ins.then_inc(s_pv, 1)

        def sub_sum(pe, a, h):
            pe.wait_ge(s_osq, h + 1)
            nc.tensor.matmul(ps[:, 6 + h % 2, L:2 * L], T["ones"], sq[:, h % 2, 0:L], start=True,
                             stop=True).then_inc(s_osum, 1)

        def att_act(act, link, a):
            diff = a["name"] == "diff"
            for i in range(a["steps"] + 10):
                if i < a["steps"]:
                    for c in range(a["maps"]):
                        act.wait_ge(s_mx, a["s0"] + i + 1)
                        src = ex[:, i % 2, 1, 0:a["keys"]] if a["name"] == "na" else \
                            ps[:, score_bank(a, i, c), 0:a["keys"]]
                        positive(act, s_tr, a["s0"] + i - 1)
                        nc.scalar.activation(ex[:, i % 2, c, 0:a["keys"]], src, ACT.Exp,
                                             bias=nm[:, i % 2, c:c + 1],
                                             accum_out=sm[:, i % 2, c:c + 1]).then_inc(s_ex, 1)
                if 2 <= i < a["steps"] + 2:
                    j0 = i - 2
                    h, t = divmod(j0, 2)
                    act.wait_ge(s_tr, a["s0"] + j0 + 1)
                    if h >= 2:
                        act.wait_ge(s_pv, a["h0"] + h - 1)
                    full = [c for c in chunk_plan(a["keys"]) if c[1] == P]
                    ins = nc.scalar.activation(
                        wT[:, h % 2, 0:len(full), t * P:(t + 1) * P],
                        ps[:, 4 + j0 % 2, 0:len(full) * P].rearrange("p (c n) -> p c n", c=len(full)), ACT.Copy)
                    if len(full) < len(chunk_plan(a["keys"])):
                        ins = nc.scalar.activation(wT[0:N_META, h % 2, len(full), t * P:(t + 1) * P],
                                                   ps[0:N_META, 4 + j0 % 2, len(full) * P:(len(full) + 1) * P],
                                                   ACT.Copy)
                    ins.then_inc(s_trc, 1)
                if diff and i % 2 == 1 and 0 <= (i - 5) // 2 < a["heads"]:
                    h = (i - 5) // 2
                    act.wait_ge(s_pv, a["h0"] + h + 1)
                    positive(act, s_osum, h - 1)
                    nc.scalar.activation(sq[:, h % 2, 0:L], o_psum(a, h), ACT.Square).then_inc(s_osq, 1)
                if diff and i % 2 == 0 and 0 <= (i - 6) // 2 < a["heads"]:
                    h = (i - 6) // 2
                    act.wait_ge(s_osum, h + 1)
                    positive(act, s_on, h)
                    link(nc.scalar.activation(rstd[:, 1, 0:L], ps[:, 6 + h % 2, L:2 * L], ACT.Ln, bias=eps_c[:, 0:1],
                                              scale=1.0 / P))
                    nc.scalar.activation(rstd[:, 0, 0:L], rstd[:, 1, 0:L], ACT.Exp, scale=-0.5)\
                        .then_inc(s_ors, 1)
                f, rest = divmod(i - (8 if diff else 2 * a["pair"] + 4), 2 * a["pair"])
                if rest == 0 and 0 <= f < a["groups"]:
                    o_round(act, a, f)

        def o_out(a, f, which):
            return which[:, f, L2:L2 + L] if a["name"] == "mla" else which[:, f, 0:L]

        def o_round(act, a, f):
            act.wait_ge(s_on, a["g0"] + f + 1)
            nc.scalar.activation(o_out(a, f, hh), nrm[:, f % 2, 0:L], ACT.Copy).then_inc(s_or, 1)

        def o_split(dve, a, f):
            dve.wait_ge(s_or, a["g0"] + f + 1)
            nc.vector.tensor_tensor(o_out(a, f, hl), nrm[:, f % 2, 0:L], o_out(a, f, hh).bitcast(F32),
                                    ALU.subtract).then_inc(s_os, 1)

        def att_dve(dve, link, a):
            diff, na = a["name"] == "diff", a["name"] == "na"
            n = a["keys"]
            for i in range(a["steps"] + 10):
                if i < a["steps"]:
                    dve.wait_ge(s_sc, a["s0"] + i + 1)
                    if na:
                        h, t = divmod(i, 2)
                        off = N_META + 2 * GRID_W if t == 0 else 0
                        dve.wait_ge(s_bias, h + 1)
                        nc.vector.tensor_tensor(ex[:, i % 2, 1, 0:n], ps[:, score_bank(a, i, 0), 0:n],
                                                bias[:, h % 2, off:off + n], ALU.add).then_inc(s_sb, 1)
                        dve.wait_ge(s_sb, i + 1)
                        nc.vector.tensor_reduce(nm[:, i % 2, 0:1], ex[:, i % 2, 1, 0:n], AX_X, ALU.max,
                                                negate=True).then_inc(s_mx, 1)
                    else:
                        b = score_bank(a, i, 0)
                        nc.vector.tensor_reduce(nm[:, i % 2, 0:a["maps"]], ps[:, b:b + a["maps"], 0:n], AX_X,
                                                ALU.max, negate=True).then_inc(s_mx, 1)
                if 1 <= i <= a["steps"]:
                    j = (i - 1) % 2
                    dve.wait_ge(s_ex, a["m0"] + i * a["maps"])
                    link(nc.vector.reciprocal(rc[:, j, 0:a["maps"]], sm[:, j, 0:a["maps"]]))
                    if diff:
                        link(nc.vector.tensor_scalar(rc[:, j, 1:2], rc[:, j, 1:2], sml[:, 5:6], None,
                                                     ALU.mult))
                        link(nc.vector.tensor_scalar(ex[:, j, 0, 0:n], ex[:, j, 0, 0:n], rc[:, j, 0:1], None,
                                                     ALU.mult))
                        nc.vector.scalar_tensor_tensor(out=ex[:, j, 0, 0:n], in0=ex[:, j, 1, 0:n],
                                                       scalar=rc[:, j, 1:2], in1=ex[:, j, 0, 0:n],
                                                       op0=ALU.mult, op1=ALU.add).then_inc(s_w, 1)
                    else:
                        nc.vector.tensor_scalar(ex[:, j, 0, 0:n], ex[:, j, 0, 0:n], rc[:, j, 0:1], None,
                                                ALU.mult).then_inc(s_w, 1)
                if diff:
                    if i % 2 == 1 and 0 <= (i - 7) // 2 < a["groups"]:
                        f = (i - 7) // 2
                        dve.wait_ge(s_ors, f + 1)
                        positive(dve, s_os, a["g0"] + f - 1)
                        nc.vector.scalar_tensor_tensor(out=nrm[:, f % 2, 0:L], in0=o_psum(a, f),
                                                       scalar=subg[:, 0:1], in1=rstd[:, 0, 0:L],
                                                       op0=ALU.mult, op1=ALU.mult).then_inc(s_on, 1)
                    if i % 2 == 1 and 0 <= (i - 9) // 2 < a["groups"]:
                        o_split(dve, a, (i - 9) // 2)
                else:
                    per = 2 * a["pair"]
                    f, rest = divmod(i - per - 3, per)
                    if rest == 0 and 0 <= f < a["groups"]:
                        dve.wait_ge(s_pv, a["h0"] + a["pair"] * (f + 1))
                        positive(dve, s_os, a["g0"] + f - 1)
                        gate = mg if a["name"] == "mla" else ng
                        nc.vector.tensor_tensor(nrm[:, f % 2, 0:L], o_psum(a, f), gate[:, f, :],
                                                ALU.mult).then_inc(s_on, 1)
                    f, rest = divmod(i - per - 5, per)
                    if rest == 0 and 0 <= f < a["groups"]:
                        o_split(dve, a, f)

        def outproj_pe(pe, halves, n, base, norm, first_wait, between=None):
            for m, q in enumerate(halves):
                pe.wait_ge(split, q + 1)
                if m >= 4:
                    pe.wait_ge(s_x, base + m - 3)
                whv, wlv = tile_of(wh, q, KD, P), tile_of(wl, q, KD, P)
                for k in range(KD):
                    if m == 0:
                        first_wait(k)
                    ins = product(ps[:, m % 4, 0:n], whv[:, k, :], wlv[:, k, :], hh[:, k, 0:n], hl[:, k, 0:n],
                                  k == 0, k == KD - 1)
                ins.then_inc(used, 1)
                if m >= 2:
                    norm_sum(pe, norm, m - 2)
                if between:
                    between(m, q)
            norm_sum(pe, norm, KD - 2)
            norm_sum(pe, norm, KD - 1)

        X_FNET, X_FFN0, X_DIFF, X_FFN1 = 0, 8, 16, 24
        X_OF = {"ffn0": X_FNET, "diff": X_FFN0, "ffn1": X_DIFF, "second": X_FFN1}

        block = ctx.enter_context(nc.Block())
        v_count = [0]
        a_count = [0]

        @block.sync
        def _(sp):
            def load(g, src, k, n):
                load_slab(sp, g, g, src, k, n)

            for s in range(24):
                load(G["ada0"] + s, d["w_ada"][0, :, s * 256:(s + 1) * 256], KD, 256)
            for m in range(0, KD, 2):
                load(FNET_OUT_Q[m] // 2, d["fnet_w_out"][0, :, m * P:(m + 2) * P], KD, 256)
                if m in (2, 4):
                    load(FNET_OUT_Q[m] // 2 + 1, d["w_ada"][1, :, (m - 2) * P:m * P], KD, 256)

            def ffn0_turn(i):
                g = G["ffn0_in"]
                for j, (w, lay, col) in enumerate(((d["ffn_w_in"], 0, i * 256), (d["w_ada"], 1, i * 512 + 512),
                                                   (d["ffn_w_in"], 0, i * 256 + D_FF),
                                                   (d["w_ada"], 1, i * 512 + 768))):
                    load_slab(sp, g + 4 * i + j, g + j, w[lay, :, bass.ds(col, 256)], KD, 256)

            ffn0_turn(0)
            with sp.Fori(1, 11) as i:
                ffn0_turn(i)

            def ffn_out(layer, g, s, at):
                load_slab(sp, g, at, d["ffn_w_out"][layer, bass.ds(s * 256, 256), :], 2, D)

            def ffn_out_all(layer, g0):
                for s in range(3):
                    ffn_out(layer, g0 + s, s, g0 + s)
                with sp.Fori(0, 2) as i:
                    for j in range(4):
                        ffn_out(layer, g0 + 3 + j + i * 4, i * 4 + 3 + j, g0 + 3 + j)

            ffn_out_all(0, G["ffn0_out"])
            for g, col in ((G["diff_k"], D), (G["diff_q"], 0), (G["diff_v"], 2 * D)):
                for s in range(4):
                    load(g + s, d["diff_w_in"][0, :, col + s * 256:col + (s + 1) * 256], KD, 256)
            for s in range(4):
                load(G["diff_out"] + s, d["diff_w_out"][0, :, s * 256:(s + 1) * 256], KD, 256)

            def ffn1(i, t, at):
                for j in range(2):
                    load_slab(sp, G["ffn1_in"] + 2 * t + j, at + j,
                              d["ffn_w_in"][1, :, bass.ds(t * 256 + j * D_FF, 256)], KD, 256)

            ffn1(0, 0, G["ffn1_in"])
            with sp.Fori(0, 5) as i:
                for t in range(2):
                    ffn1(i, 2 * i + 1 + t, G["ffn1_in"] + 2 + 2 * t)
            ffn_out_all(1, G["ffn1_out"])

            w_in = d["w_in_2"]
            load(G["lat"], w_in[0, :, IN_QLAT:IN_QLAT + 256], KD, 256)
            load(G["lat"] + 1, w_in[0, :, IN_KVLAT:IN_KVLAT + 256], KD, 256)
            load(G["kpe"], w_in[0, :, IN_KPE:IN_KPE + MLA_ROPE], KD, MLA_ROPE)
            for s in range(4):
                load(G["gmla"] + s, w_in[0, :, IN_GMLA + s * 256:IN_GMLA + (s + 1) * 256], KD, 256)
            for s in range(2):
                load(G["uq"] + s, d["w_uq_2"][0, :, s * 768:(s + 1) * 768], 2, 768)
            for s in range(2):
                load(G["ukv"] + s, d["w_ukv_2"][0, :, s * 1024:(s + 1) * 1024], 2, 1024)
            for g, col in ((G["naq"], IN_NAQ), (G["nak"], IN_NAK), (G["nav"], IN_NAV),
                           (G["gna"], IN_GNA)):
                for s in range(4):
                    load(g + s, w_in[0, :, col + s * 256:col + (s + 1) * 256], KD, 256)
            for s in range(8):
                load(G["out2"] + s, d["w_out_2"][0, s * 256:(s + 1) * 256, :], 2, D)

        @block.gpsimd
        def _(pool):
            pool.dma_start(tab[:, 2 * P:], d["tables"][:, 2 * P:]).then_inc(s_tab, 16)
            pool.dma_start(big[:, 10240:10240 + FOURIER], d["fourier"]).then_inc(s_tab, 16)
            pool.dma_start(meta_b[:, :], d["meta_bias"].to_broadcast([P, NA_HEADS * N_META])
                           if False else bass.AP(tensor=d["meta_bias"].tensor, offset=0,
                                                 ap=[[0, P], [1, NA_HEADS * N_META]])).then_inc(s_metab, 16)
            pool.wait_ge(s_metab, 16)
            pool.wait_ge(s_tab, 32)
            pool.wait_ge(s_on, ATT["mla"]["g0"] + ATT["mla"]["groups"])
            flat = NA_HEADS * REL_R * REL_C
            for half in range(2):
                first = flat - 1 - (NA_HEADS - 1) * REL_R * REL_C - (NA_WIN_R - 1 - 2 - half) * REL_C \
                    - (NA_WIN_C - 1) - (RUN - 1)
                pool.dma_start(runs[64 * half:64 * half + 64, :, :],
                               bass.AP(tensor=d["rel_bias_rev"].tensor, offset=first,
                                       ap=[[1, 64], [REL_R * REL_C, NA_HEADS], [1, RUN]])).then_inc(s_runs, 16)
            pool.wait_ge(s_runs, 32)
            for h in range(NA_HEADS):
                s = h % 2
                if h >= 2:
                    pool.wait_ge(s_sb, 2 * (h - 1))
                at = 9472 + (NA_HEADS - 1 - h) * RUN + RUN - 1
                run = bass.AP(tensor=big, offset=at, ap=[[13824, P], [-REL_C, SLOTS_R], [-1, GRID_W]])
                mask = bass.AP(tensor=tab, offset=sum(list(TABLE_COLS.values())[:N_KEPT - 2]), ap=[[KEPT, P], [0, SLOTS_R], [1, GRID_W]])
                for c in (0, N_META + SLOTS_R * GRID_W):
                    nc.gpsimd.tensor_copy(bias[:, s, c:c + N_META], meta_b[:, h * N_META:(h + 1) * N_META])
                nc.gpsimd.tensor_tensor(
                    bias[:, s, N_META:N_META + SLOTS_R * GRID_W].rearrange("p (j c) -> p j c", j=SLOTS_R),
                    run, mask, ALU.add).then_inc(s_bias, 1)

        @block.scalar
        def _(act):
            def link(ins):
                a_count[0] += 1
                ins.then_inc(a_ch, 1)
                act.wait_ge(a_ch, a_count[0])

            def exp_and_ln():
                nc.scalar.preload_act_table_set("natural_log_exp_and_others")

            act.dma_start(rows[0:N_PAR, P:2 * P], d["params"]).then_inc(s_rows, 16)
            act.dma_start(rows[0:N_ADA, 0:P], d["b_ada"]).then_inc(s_rows, 16)
            act.dma_start(tab[:, 0:2 * P], d["tables"][:, 0:2 * P]).then_inc(s_rows, 16)
            act.dma_start(xin[:, 0:2, :], d["x"][0].rearrange("(t p) n -> p t n", p=P)).then_inc(s_xin, 16)
            act.dma_start(xin[:, 2:4, :], d["ctx"][0].rearrange("(t p) n -> p t n", p=P)).then_inc(s_xin, 16)
            act.dma_start(h32[0:N_META, 0:2, :].rearrange("p a b -> p (a b)"), d["meta_tokens_2"])\
                .then_inc(s_xin, 16)
            act.wait_ge(s_turn_v, 1)
            link(nc.scalar.activation(cond[:, :], par_of("c", 0, 2 * KD), ACT.Silu))
            nc.scalar.activation(condr[:, :, 0:2], cond[:, :].rearrange("p (c k) -> p k c", c=2), ACT.Copy)\
                .then_inc(s_cond, 1)
            act.wait_ge(s_turn, 2)
            for c in range(2):
                ins = nc.scalar.activation(sml[:, 2 + c:3 + c], ps[:, 3 - 2 * c, c:c + 1], ACT.Exp)
            ins.then_inc(s_mod, 1)
            for q in range(AHEAD):
                round_half(act, q, q)
            round_next(act, 0, 8)
            for k in range(KD):
                act.wait_ge(s_turn, 3 + k)
                nc.scalar.activation(x_ctx[:, k, :], ps[:, 2 + k % 2, 0:LC], ACT.Copy).then_inc(s_turn_a, 1)
            exp_and_ln()
            act.wait_ge(s_turn_a, KD)
            act.wait_ge(s_turn_v, 3 + KD)
            for half in range(2):
                round_next(act, 8 + 4 * half, 4)
                for k in range(4 * half, 4 * half + 4):
                    norm_square(act, "fnet", k)
            norm_rstd(act, link, "fnet")
            for i in range(8 + 1):
                if i < 8:
                    act.wait_ge(s_f1, i + 1)
                    if i >= 2:
                        act.wait_ge(s_f2, i - 1)
                    nc.scalar.activation(uv[:, i % 2, 0:2, :].rearrange("p t c -> p (t c)"),
                                         ps[:, 2 * (i % 2), :], ACT.Copy).then_inc(s_f1a, 1)
                    round_next(act, 16 + 4 * i, 4)
                if i >= 1:
                    act.wait_ge(s_f2, i)
                    nc.scalar.activation(hh[:, i - 1, 0:NT], ps[:, 4 + (i - 1) % 2, :], ACT.Copy)\
                        .then_inc(s_f2a, 1)
            for m, q in enumerate(FNET_OUT_Q):
                round_next(act, q)
                act.wait_ge(used, q + 1)
                if m >= 2:
                    act.wait_ge(s_x, m - 1)
                nc.scalar.activation(ex[:, m % 2, 0, :], ps[:, m % 4, :], ACT.Identity, scale=1.0,
                                     bias=par_of("fnet_b", m)).then_inc(s_opa, 1)
                if m >= 1:
                    norm_square(act, "ffn0", m - 1)
                if m in (3, 5):
                    round_next(act, q + 1, 2)
            norm_square(act, "ffn0", KD - 1)
            norm_rstd(act, link, "ffn0")
            norm_round(act, "ffn0")

            def silu_gate(i, j, n, gtile, q):
                act.wait_ge(used, q + 1)
                positive(act, s_act, gtile + 2 * i + j - 1)
                nc.scalar.activation(nrm[:, j, 0:n], ps[:, j, 0:n], ACT.Silu).then_inc(s_silu, 1)

            def act_round(layer, k, at, n, q0):
                positive(act, used, k + (q0 - 1))
                nc.scalar.activation(ah[:, at % 2, 0:n], big[:, bass.ds(k * n, n)], ACT.Copy)\
                    .then_inc(s_ar, 1)

            def ffn_out(layer, g0, n, norm):
                q0 = 2 * g0
                exp_and_ln()
                act.wait_ge(s_act, layer * KF + 20)
                for k in range(2):
                    act_round(layer, k, k, n, q0)
                for k in range(2):
                    act_round(layer, k + 2, k, n, q0)
                    round_next(act, q0 + k)
                with act.Fori(0, 2) as i:
                    for j in range(8):
                        act_round(layer, i * 8 + (j + 4), j, n, q0)
                        round_half(act, i * 8 + (q0 + 2 + j + AHEAD), q0 + 2 + j + AHEAD)
                act.wait_ge(s_act, (layer + 1) * KF)
                for k in range(18, 20):
                    act_round(layer, k + 2, k, n, q0)
                    round_next(act, q0 + k)
                for m in range(KD):
                    norm_square(act, norm, m)
                round_next(act, q0 + 20, 2)
                norm_rstd(act, link, norm)
                norm_round(act, norm)

            act.wait_ge(s_hh, KD)
            nc.scalar.preload_act_table(ACT.Silu)
            q = 2 * G["ffn0_in"]

            def ffn0_turn(i, at):
                for j in range(8):
                    round_half(act, i * 8 + (q + j + AHEAD), at + j + AHEAD)
                    if j < 2:
                        silu_gate(i, j, NT, 0, i * 8 + (q + j))

            ffn0_turn(0, q)
            with act.Fori(1, 10) as i:
                ffn0_turn(i, q)
            ffn0_turn(10, q + 80)
            ffn_out(0, G["ffn0_out"], NT, "diff")
            units_act(act, link, DIFF_UNITS)
            att_act(act, link, ATT["diff"])
            for m in range(KD):
                round_next(act, 2 * G["diff_out"] + m)
                if m >= 1:
                    norm_square(act, "ffn1", m - 1)
            norm_square(act, "ffn1", KD - 1)
            norm_rstd(act, link, "ffn1")
            norm_round(act, "ffn1")
            nc.scalar.preload_act_table(ACT.Silu)
            q1 = 2 * G["ffn1_in"]

            def ffn1_turn(i, at):
                first = i * 4 + q1
                for j in range(4):
                    round_half(act, first + (j + AHEAD), at + j + AHEAD)
                    if j < 2:
                        silu_gate(i, j, L, KF, first + j)

            ffn1_turn(0, q1)
            with act.Fori(0, 4) as i:
                for t in range(2):
                    ffn1_turn(2 * i + 1 + t, q1 + 4 + 4 * t)
            for t in (9, 10):
                ffn1_turn(t, q1 + 4 * t)
            ffn_out(1, G["ffn1_out"], L, "second")
            units_act(act, link, LAT_UNITS)
            norm_act(act, link, "lat")
            units_act(act, link, GATE_UNITS)
            exp_and_ln()
            units_act(act, link, MLA_UNITS)
            att_act(act, link, ATT["mla"])
            units_act(act, link, NA_UNITS)
            exp_and_ln()
            att_act(act, link, ATT["na"])
            round_next(act, 2 * G["out2"], 16)
            for t in range(2):
                act.wait_ge(used, 2 * G["end"])
                nc.scalar.activation(big[:, t * D:t * D + 512], ps[:, 2 * t, :], ACT.Copy).then_inc(s_fo, 1)
            act.wait_ge(s_fo, 4)
            for t in range(2):
                act.dma_start(out[0, t * P:(t + 1) * P, :], big[:, t * D:(t + 1) * D]).then_inc(s_out, 16)
            act.wait_ge(s_out, 32)

        @block.vector
        def _(dve):
            def link(ins):
                v_count[0] += 1
                ins.then_inc(v_ch, 1)
                dve.wait_ge(v_ch, v_count[0])

            link(nc.vector.memset(eps_c[:, :], EPS))
            dve.wait_ge(s_turn, 1)
            nc.vector.tensor_copy(par[:, :], ps[:, 0, 0:N_ADA + N_PAR]).then_inc(s_turn_v, 1)
            dve.wait_ge(s_turn_v, 1)
            nc.vector.tensor_tensor(sml[:, 0:1], par_of("lam_a"), par_of("lam_b"), ALU.mult)\
                .then_inc(s_turn_v, 1)
            link(nc.vector.tensor_scalar(subg[:, :], par_of("subln"), 1.0 - LAM_INIT, None, ALU.mult))
            for gain, scale in (("dq", ATT["diff"]["scale"]), ("qn", ATT["mla"]["scale"]),
                                ("qpe", ATT["mla"]["scale"]), ("naq", ATT["na"]["scale"])):
                link(nc.vector.tensor_scalar(par_of(gain), par_of(gain), scale, None, ALU.mult))
            dve.wait_ge(s_cond, 1)
            nc.vector.tensor_tensor(condr[:, :, 2:4], cond[:, :].rearrange("p (c k) -> p k c", c=2),
                                    condr[:, :, 0:2].bitcast(F32), ALU.subtract).then_inc(s_cond, 1)
            dve.wait_ge(s_mod, 1)
            link(nc.vector.tensor_tensor(sml[:, 4:5], sml[:, 3:4], sml[:, 2:3], ALU.subtract))
            link(nc.vector.tensor_scalar(sml[:, 5:6], sml[:, 4:5], -LAM_INIT, None, ALU.add))
            for q in range(AHEAD):
                split_low(dve, q, q)

            def ada_copy(p, q):
                dve.wait_ge(used, q + 1)
                positive(dve, s_adat, p)
                nc.vector.tensor_copy(ada_row[0:4, :], ps[0:4, 6, :]).then_inc(s_adac, 1)

            def ada_bias(p):
                dve.wait_ge(s_adat, p + 1)
                bias_of = par[:, bass.ds(p * 4, 4)]
                for c in range(2):
                    ins = nc.vector.tensor_tensor(
                        ada_flat[:, bass.ds(p * 4, 4), c],
                        ps[:, 7, 0:8].rearrange("p (m c) -> p m c", m=4)[:, :, c], bias_of, ALU.add)
                ins.then_inc(s_adav, 1)

            def scaled_gain(layer, n):
                sec = 1 if n == 0 else 4
                for c in range(2):
                    link(nc.vector.scalar_tensor_tensor(
                        out=gsc[:, layer, n, :, c], in0=ada[:, layer, sec * KD:(sec + 1) * KD, c], scalar=1.0,
                        in1=par_of("norm_gain", (2 * layer + n) * KD, KD), op0=ALU.add, op1=ALU.mult))

            for p in range(4):
                split_next(dve, 4 * p, 2)
                ada_copy(p, 4 * p + 3)
                split_next(dve, 4 * p + 2, 2)
                if p >= 1:
                    ada_bias(p - 1)
                if p == 1:
                    for k in range(KD):
                        dve.wait_ge(s_turn, 3 + k)
                        nc.vector.tensor_copy(x_lat[:, k, :], ps[:, k % 2, 0:L]).then_inc(s_turn_v, 1)
                    dve.wait_ge(s_turn, 3 + KD)
                    nc.vector.tensor_copy(x_meta[:, :, :], ps[:, 4, 0:KD * N_META]
                                          .rearrange("p (k n) -> p k n", k=KD)).then_inc(s_turn_v, 1)
            ada_bias(3)
            dve.wait_ge(s_adav, 4)
            scaled_gain(0, 0)
            norm_dve(dve, "fnet")
            for i in range(8 + 1):
                if i < 8:
                    dve.wait_ge(s_f1, i + 1)
                    if i >= 2:
                        dve.wait_ge(s_f2, i - 1)
                    nc.vector.tensor_copy(uv[:, i % 2, 2:4, :].rearrange("p t c -> p (t c)"),
                                          ps[:, 2 * (i % 2) + 1, :]).then_inc(s_f1v, 1)
                    q = 16 + 4 * i
                    split_next(dve, q, 2)
                    ada_copy(4 + i, q + 3)
                    split_next(dve, q + 2, 2)
                if i >= 1:
                    dve.wait_ge(s_f2a, i)
                    nc.vector.tensor_tensor(hl[:, i - 1, 0:NT], ps[:, 4 + (i - 1) % 2, :],
                                            hh[:, i - 1, 0:NT].bitcast(F32), ALU.subtract).then_inc(s_f2v, 1)
                if i < 8:
                    ada_bias(4 + i)
            dve.wait_ge(s_adav, 12)
            scaled_gain(0, 1)

            def add_gated(src, layer, sec, m, width, off, x, c):
                return nc.vector.scalar_tensor_tensor(out=x[:, m, :], in0=src[:, off:off + width],
                                                      scalar=ada[:, layer, sec * KD + m, c:c + 1],
                                                      in1=x[:, m, :], op0=ALU.mult, op1=ALU.add)

            for m, q in enumerate(FNET_OUT_Q):
                split_next(dve, q)
                dve.wait_ge(s_opa, m + 1)
                add_gated(ex[:, m % 2, 0, :], 0, 2, m, L, 0, x_lat, 0)
                add_gated(ex[:, m % 2, 0, :], 0, 2, m, LC, L, x_ctx, 1).then_inc(s_x, 1)
                if m in (3, 5):
                    split_next(dve, q + 1, 2)
                if m == 5:
                    ada_copy(12, q + 2)
            ada_bias(12)

            def up_times_gate(i, j, n, tile, q):
                dve.wait_ge(used, q + 1)
                dve.wait_ge(s_silu, tile + 2 * i + j + 1)
                nc.vector.tensor_tensor(big[:, bass.ds(i * (2 * n) + j * n, n)], nrm[:, j, 0:n],
                                        ps[:, 2 + j, 0:n], ALU.mult).then_inc(s_act, 1)

            def act_split(layer, k, at, n, q0):
                dve.wait_ge(s_ar, k + (layer * KF + 1))
                nc.vector.tensor_tensor(al[:, at % 2, 0:n], big[:, bass.ds(k * n, n)],
                                        ah[:, at % 2, 0:n].bitcast(F32), ALU.subtract).then_inc(s_as, 1)

            def ffn_out(layer, g0, n):
                q0 = 2 * g0
                for k in range(2):
                    act_split(layer, k, k, n, q0)
                if layer == 0:
                    ada_bias(23)
                    dve.wait_ge(s_adav, 24)
                    scaled_gain(1, 0)
                    scaled_gain(1, 1)
                for k in range(2):
                    act_split(layer, k + 2, k, n, q0)
                    split_next(dve, q0 + k)
                with dve.Fori(0, 2) as i:
                    for j in range(8):
                        act_split(layer, i * 8 + (j + 4), j, n, q0)
                        split_low(dve, i * 8 + (q0 + 2 + j + AHEAD), q0 + 2 + j + AHEAD)
                for k in range(18, 20):
                    act_split(layer, k + 2, k, n, q0)
                    split_next(dve, q0 + k)
                for m in range(KD):
                    if m < KD - 1:
                        dve.wait_ge(s_fin, layer * (KD - 1) + m + 1)
                    else:
                        dve.wait_ge(used, q0 + KF)
                    ins = add_gated(ps[:, m, :], layer, 5, m, L, 0, x_lat, 0)
                    if layer == 0:
                        ins = add_gated(ps[:, m, :], layer, 5, m, LC, L, x_ctx, 1)
                    ins.then_inc(s_x, 1)
                split_next(dve, q0 + 20, 2)

            norm_dve(dve, "ffn0")
            q = 2 * G["ffn0_in"]

            def ffn0_turn(i, at):
                for j in range(8):
                    split_low(dve, i * 8 + (q + j + AHEAD), at + j + AHEAD)
                    if j in (4, 5):
                        up_times_gate(i, j - 4, NT, 0, i * 8 + (q + j))
                    if j == 3 and (type(i) is not int or i >= 1):
                        ada_bias(i + 12)
                ada_copy(i + 13, i * 8 + (q + 7))

            ffn0_turn(0, q)
            with dve.Fori(1, 10) as i:
                ffn0_turn(i, q)
            ffn0_turn(10, q + 80)
            ffn_out(0, G["ffn0_out"], NT)
            dve.wait_ge(s_x, X_FFN0 + KD)
            norm_dve(dve, "diff")
            units_dve(dve, link, DIFF_UNITS)
            att_dve(dve, link, ATT["diff"])
            for m in range(KD):
                q = 2 * G["diff_out"] + m
                split_next(dve, q)
                dve.wait_ge(used, q + 1)
                add_gated(ps[:, m % 4, :], 1, 2, m, L, 0, x_lat, 0).then_inc(s_x, 1)
            dve.wait_ge(s_x, X_DIFF + KD)
            norm_dve(dve, "ffn1")
            q1 = 2 * G["ffn1_in"]

            def ffn1_turn(i, at):
                first = i * 4 + q1
                for j in range(4):
                    split_low(dve, first + (j + AHEAD), at + j + AHEAD)
                    if j >= 2:
                        up_times_gate(i, j - 2, L, KF, first + j)

            ffn1_turn(0, q1)
            with dve.Fori(0, 4) as i:
                for t in range(2):
                    ffn1_turn(2 * i + 1 + t, q1 + 4 + 4 * t)
            for t in (9, 10):
                ffn1_turn(t, q1 + 4 * t)
            ffn_out(1, G["ffn1_out"], L)
            dve.wait_ge(s_x, X_FFN1 + KD)
            norm_dve(dve, "second")
            units_dve(dve, link, LAT_UNITS)
            norm_dve(dve, "lat")
            units_dve(dve, link, GATE_UNITS)
            units_dve(dve, link, MLA_UNITS)
            att_dve(dve, link, ATT["mla"])
            units_dve(dve, link, NA_UNITS)
            att_dve(dve, link, ATT["na"])
            split_next(dve, 2 * G["out2"], 16)
            for t in range(2):
                dve.wait_ge(used, 2 * G["end"])
                nc.vector.tensor_copy(big[:, t * D + 512:(t + 1) * D], ps[:, 2 * t + 1, :]).then_inc(s_fo, 1)

        @block.tensor
        def _(pe):
            pe.wait_ge(s_rows, 48)
            nc.tensor.transpose(ps[:, 0, 0:N_ADA], rows[0:N_ADA, 0:P], T["ident"][0:N_ADA, 0:N_ADA])
            nc.tensor.transpose(ps[:, 0, N_ADA:N_ADA + N_PAR], rows[0:N_PAR, P:2 * P],
                                T["ident"][0:N_PAR, 0:N_PAR]).then_inc(s_turn, 1)
            pe.wait_ge(s_turn_v, 2)
            for c in range(2):
                ins = nc.tensor.matmul(ps[:, 3 - 2 * c, c:c + 1], T["ones"][64 * c:64 * c + 64, :],
                                       sml[64 * c:64 * c + 64, 0:1], start=True, stop=True)
            ins.then_inc(s_turn, 1)
            def ada_slab(at, half, q):
                pe.wait_ge(split, q + 2)
                for k in range(KD):
                    for w in (wh, wl):
                        ins = nc.tensor.matmul(
                            ps[0:4, 6, half * 256:(half + 1) * 256].rearrange("p (h e) -> p h e", h=2),
                            condr[:, k, :], w[:, at % SPLIT_SLOTS:at % SPLIT_SLOTS + 2, k * P:(k + 1) * P],
                            start=(k == 0 and w is wh), stop=(k == KD - 1 and w is wl))
                ins.then_inc(used, 2)

            def ada_turn(p):
                pe.wait_ge(s_adac, p + 1)
                positive(pe, s_adav, p)
                for m in range(4):
                    ins = nc.tensor.matmul(ps[:, 7, 2 * m:2 * m + 2], ada_row[0:4, m * P:(m + 1) * P],
                                           T["fold"][0:4, :], start=True, stop=True)
                ins.then_inc(s_adat, 1)

            def ada_pair(at, q, p):
                positive(pe, s_adac, p)
                ada_slab(at, 0, q)
                ada_slab(at + 2, 1, q + 2)

            pe.wait_ge(s_cond, 2)

            def turn_x():
                pe.wait_ge(s_xin, 48)
                pe.wait_ge(s_mod, 1)
                for k in range(KD):
                    if k >= 2:
                        pe.wait_ge(s_turn_a, k - 1)
                        pe.wait_ge(s_turn_v, k + 1)
                    for t in range(4):
                        ins = nc.tensor.transpose(ps[:, 2 * (t // 2) + k % 2, t % 2 * P:(t % 2 + 1) * P],
                                                  xin[:, t, k * P:(k + 1) * P], T["ident"])
                    ins.then_inc(s_turn, 1)
                meta = h32[0:N_META, 0:2, :].rearrange("p a b -> p (a b)")
                for k in range(KD):
                    ins = nc.tensor.transpose(ps[:, 4, k * N_META:(k + 1) * N_META],
                                              meta[:, k * P:(k + 1) * P], T["ident"][0:N_META, 0:N_META])
                ins.then_inc(s_turn, 1)

            for p in range(4):
                ada_pair(4 * p, 4 * p, p)
                if p == 1:
                    pe.wait_ge(s_tab, 32)
                if p >= 1:
                    ada_turn(p - 1)
                if p == 1:
                    turn_x()
                if p >= 2:
                    for k in range(4 * p - 8, 4 * p - 4):
                        if k == KD - 1:
                            ada_turn(3)
                        norm_sum(pe, "fnet", k)
            pe.wait_ge(s_turn_v, 3 + KD)

            def fnet_inner(i):
                pe.wait_ge(s_h, i + 1)
                if i >= 2:
                    pe.wait_ge(s_f1a, i - 1)
                    pe.wait_ge(s_f1v, i - 1)
                for t in range(4):
                    ins = nc.tensor.matmul(ps[:, 2 * (i % 2) + t // 2, t % 2 * L:(t % 2 + 1) * L],
                                           h32[:, i, t * P:(t + 1) * P], dft_g, start=True, stop=True)
                ins.then_inc(s_f1, 1)

            def fnet_outer(i):
                pe.wait_ge(s_f1a, i + 1)
                pe.wait_ge(s_f1v, i + 1)
                if i >= 2:
                    pe.wait_ge(s_f2v, i - 1)
                for s in range(2):
                    for t in range(2):
                        for c, tb in enumerate((cos_l, nsin_l)):
                            ins = nc.tensor.matmul(ps[:, 4 + i % 2, s * L:(s + 1) * L],
                                                   uv[:, i % 2, 2 * s + t, c * P:(c + 1) * P], tb[:, t, :],
                                                   start=(t == 0 and c == 0), stop=(t == 1 and c == 1))
                ins.then_inc(s_f2, 1)

            fnet_inner(0)
            for i in range(8):
                ada_pair(16 + 4 * i, 16 + 4 * i, 4 + i)
                if i < 7:
                    fnet_inner(i + 1)
                fnet_outer(i)
                ada_turn(4 + i)
            pe.wait_ge(s_adav, 12)

            def fnet_out_between(m, q):
                if m in (3, 5):
                    if m == 3:
                        pe.wait_ge(s_adac, 12)
                    ada_slab(q + 1, m // 4, q + 1)
                if m == 6:
                    ada_turn(12)

            outproj_pe(pe, FNET_OUT_Q, NT, X_FNET, "ffn0", lambda k: pe.wait_ge(s_f2v, k + 1),
                       fnet_out_between)

            def half_ffn(q, at, n, bank, h_base=None):
                order = [(m, k) for m in range(2) for k in range(KD)] if h_base is None else \
                    [(m, k) for k in range(KD) for m in range(2)]
                for m, k in order:
                    if k == 0:
                        pe.wait_ge(split, q + (m + 1))
                    if h_base is not None and m == 0:
                        pe.wait_ge(s_h, h_base + k + 1)
                    ins = product(ps[:, bank + m, 0:n], tile_of(wh, at + m, KD, P)[:, k, :],
                                  tile_of(wl, at + m, KD, P)[:, k, :], hh[:, k, 0:n], hl[:, k, 0:n], k == 0,
                                  k == KD - 1)
                    if k == KD - 1:
                        ins.then_inc(used, 1)

            def ffn_out_half(layer, q, at, k, n, first, last):
                pe.wait_ge(split, q + 1)
                pe.wait_ge(s_as, k + (layer * KF + 1))
                whv, wlv = wh[:, at % SPLIT_SLOTS, :], wl[:, at % SPLIT_SLOTS, :]
                for m in range(KD):
                    c = slice(m * P, (m + 1) * P)
                    if first and layer == 0 and m == 5:
                        ada_turn(23)
                    if first and layer == 0 and m == 7:
                        pe.wait_ge(s_adav, 24)
                    ins = product(ps[:, m, 0:n], whv[:, c], wlv[:, c], ah[:, at % 2, 0:n], al[:, at % 2, 0:n],
                                  first, last)
                ins.then_inc(used, 1)

            def ffn_out(layer, g0, n, norm):
                q0 = 2 * g0
                pe.wait_ge(s_act, (layer + 1) * KF)
                for k in range(2):
                    ffn_out_half(layer, q0 + k, q0 + k, k, n, k == 0, False)
                with pe.Fori(0, 2) as i:
                    for j in range(8):
                        ffn_out_half(layer, i * 8 + (q0 + 2 + j), q0 + 2 + j, i * 8 + (2 + j), n, False, False)
                for k in range(18, 20):
                    ffn_out_half(layer, q0 + k, q0 + k, k, n, False, False)
                pe.wait_ge(split, q0 + KF)
                pe.wait_ge(s_as, (layer + 1) * KF)
                for m in range(KD):
                    c = slice(m * P, (m + 1) * P)
                    for k in (20, 21):
                        at = (q0 + k) % SPLIT_SLOTS
                        ins = product(ps[:, m, 0:n], wh[:, at, c], wl[:, at, c], ah[:, k % 2, 0:n],
                                      al[:, k % 2, 0:n], False, k == 21)
                    if m < KD - 1:
                        ins.then_inc(s_fin, 1)
                    else:
                        ins.then_inc(used, 2)
                    if m >= 2:
                        norm_sum(pe, norm, m - 2)
                norm_sum(pe, norm, KD - 2)
                norm_sum(pe, norm, KD - 1)

            q = 2 * G["ffn0_in"]

            def ffn0_turn(i, h_base=None):
                first = i * 8 + q
                positive(pe, s_silu, i * 2)
                half_ffn(first, q, NT, 0, h_base)
                if h_base is None:
                    ada_turn(i + 12)
                ada_slab(q + 2, 0, first + 2)
                positive(pe, s_act, i * 2)
                half_ffn(first + 4, q + 4, NT, 2)
                ada_slab(q + 6, 1, first + 6)

            ffn0_turn(0, BASE["ffn0"])
            with pe.Fori(1, 11) as i:
                ffn0_turn(i)
            ffn_out(0, G["ffn0_out"], NT, "diff")
            pe.wait_ge(s_x, X_FFN0 + KD)
            units_pe(pe, DIFF_UNITS, BASE["diff"])
            pe.wait_ge(s_urdy, 16)
            pe.wait_ge(s_ucp, 16)
            att_pe(pe, ATT["diff"])
            outproj_pe(pe, [2 * G["diff_out"] + m for m in range(KD)], L, X_DIFF, "ffn1",
                       lambda k: pe.wait_ge(s_os, k + 1))
            q1 = 2 * G["ffn1_in"]

            def ffn1_turn(i, at, h_base=None):
                first = i * 4 + q1
                positive(pe, s_silu, i * 2 + KF)
                half_ffn(first, at, L, 0, h_base)
                positive(pe, s_act, i * 2 + KF)
                half_ffn(first + 2, at + 2, L, 2)

            ffn1_turn(0, q1, BASE["ffn1"])
            with pe.Fori(0, 5) as i:
                for t in range(2):
                    ffn1_turn(2 * i + 1 + t, q1 + 4 + 4 * t)
            ffn_out(1, G["ffn1_out"], L, "second")
            pe.wait_ge(s_x, X_FFN1 + KD)
            units_pe(pe, LAT_UNITS, BASE["second"])
            norm_pe(pe, "lat")
            units_pe(pe, GATE_UNITS)
            pe.wait_ge(s_h, BASE["lat"] + 2)
            units_pe(pe, MLA_UNITS)
            pe.wait_ge(s_urdy, ROPED[-1]["r"] + 1)
            pe.wait_ge(s_unrm, max(u["h"] for u in MLA_UNITS if u["kind"] == "head") + 1)
            pe.wait_ge(s_ucp, MLA_UNITS[-1]["c"] + 1)
            att_pe(pe, ATT["mla"])
            pe.wait_ge(s_on, ATT["mla"]["g0"] + 8)
            units_pe(pe, NA_UNITS)
            pe.wait_ge(s_unrm, max(u["h"] for u in NA_UNITS if u["kind"] == "head") + 1)
            pe.wait_ge(s_ucp, NA_UNITS[-1]["c"] + 1)
            att_pe(pe, ATT["na"])
            pe.wait_ge(s_ex, map_base)
            pe.wait_ge(s_os, 24)
            for k in range(16):
                q = 2 * G["out2"] + k
                pe.wait_ge(split, q + 1)
                if k == 1:
                    for t in range(2):
                        for m in range(KD):
                            nc.tensor.matmul(ps[:, 2 * t + m // 4, m % 4 * P:(m % 4 + 1) * P],
                                             x_lat[:, m, t * P:(t + 1) * P], T["ident"], start=False,
                                             stop=False, skip_group_check=True)
                for t in range(2):
                    at = (L2 + t * P) if k < 8 else t * P
                    a_h, a_l = hh[:, k % 8, at:at + P], hl[:, k % 8, at:at + P]
                    for c in range(2):
                        o = ps[:, 2 * t + c, :]
                        n = slice(c * 512, (c + 1) * 512)
                        w_h, w_l = wh[:, q % SPLIT_SLOTS, n], wl[:, q % SPLIT_SLOTS, n]
                        nc.tensor.matmul(o, a_h, w_h, start=(k == 0), stop=False, skip_group_check=True)
                        nc.tensor.matmul(o, a_h, w_l, start=False, stop=False, skip_group_check=True)
                        ins = nc.tensor.matmul(o, a_l, w_h, start=False, stop=(k == 15), skip_group_check=True)
                ins.then_inc(used, 1)


def kernel(**inputs):
    import concourse.bacc as _bacc
    from concourse.bass_utils import run_bass_kernel_spmd as _run

    def flat(name, *shape):
        return np.ascontiguousarray(inputs[name]).reshape(*shape)

    twice = lambda name: np.concatenate([flat(name, 1, 64)] * 2, 1)
    lam = flat("diff_lambda", 4, 64)
    params = np.concatenate([
        flat("norm_gain", 4 * KD, P), flat("fnet_b_out", KD, P), flat("norm_w_2", KD, P),
        flat("q_lat_norm_w_2", 2, P), flat("kv_lat_norm_w_2", 2, P), flat("diff_subln_gain", 1, P),
        flat("diff_q_gain", 1, P), flat("diff_k_gain", 1, P), flat("mla_qn_w_2", 1, P), flat("mla_kn_w_2", 1, P),
        twice("mla_qpe_w_2"), twice("mla_kpe_w_2"), twice("na_q_norm_w_2"), twice("na_k_norm_w_2"),
        np.concatenate([lam[0:1], lam[2:3]], 1), np.concatenate([lam[1:2], lam[3:4]], 1),
        flat("c", KD, P), flat("c_ctx", KD, P)], 0)
    tables = shape_tables()
    names = list(TABLE_COLS)
    kept = np.concatenate([tables[n] for n in names[:N_KEPT]], 1).astype(np.float32)
    fourier = np.concatenate([tables[n] for n in names[N_KEPT:]], 1).astype(np.float32)
    arrays = {
        "tables": kept, "fourier": fourier, "params": params, "b_ada": flat("b_ada", N_ADA, P),
        "meta_bias": flat("na_meta_bias_2", NA_HEADS * N_META),
        "rel_bias_rev": flat("na_rel_bias_2", -1)[::-1],
    }
    for name in ("x", "ctx", "w_ada", "ffn_w_in", "ffn_w_out", "fnet_w_out", "diff_w_in", "diff_w_out",
                 "meta_tokens_2", "w_in_2", "w_uq_2", "w_ukv_2", "w_out_2"):
        arrays[name] = inputs[name]
    arrays = {f"in_{n}": np.ascontiguousarray(a) for n, a in arrays.items()}

    nc = _bacc.Bacc("TRN2", target_bir_lowering=False, num_devices=1)
    d = {n[3:]: nc.dram_tensor(n, a.shape, mybir.dt.from_np(a.dtype), kind="ExternalInput").ap()
         for n, a in arrays.items()}
    out = nc.dram_tensor("out_0", (1, L, D), F32, kind="ExternalOutput").ap()
    build(nc, d, out)
    r = _run(nc, [arrays], core_ids=[0])
    return r.results[0]["out_0"]
```

```python
import math
from contextlib import ExitStack

import numpy as np
import concourse.bass as bass
from concourse import mybir

F32 = mybir.dt.float32
F32R = mybir.dt.float32r
ACT = mybir.ActivationFunctionType
ALU = mybir.AluOpType
AX_X = mybir.AxisListType.X

P = 128
D = 1024
KD = D // P
L = 256
LC = 256
NT = L + LC
GRID_W = 64
ROWS = L // GRID_W
EPS = 1e-6
D_FF = 2816
KF = D_FF // P
DIFF_HEADS = 8
DIFF_DIM = 64
LAM_INIT = 0.8 - 0.6 * math.exp(-0.3 * 1)
N_META = 16
L2 = L + N_META
MLA_HEADS, MLA_NOPE, MLA_ROPE, MLA_V, MLA_RANK = 8, 128, 64, 128, 256
NA_HEADS, NA_DIM, NA_WIN_R, NA_WIN_C = 16, 64, 8, 16
REL_R, REL_C = 2 * NA_WIN_R - 1, 2 * NA_WIN_C - 1
MASKED = -1e30

RAW_SLOTS = 4
SPLIT_SLOTS = 4
AHEAD = SPLIT_SLOTS
SLAB = 2048
HALF = SLAB // 2

IN_QLAT, IN_KVLAT, IN_KPE, IN_GMLA = 0, 256, 512, 576
IN_NAQ, IN_NAK, IN_NAV, IN_GNA = 1600, 2624, 3648, 4672

SLOTS_R = 2 * ROWS - 2
RUN = REL_C * (SLOTS_R - 1) + GRID_W
RUNS_AT = 6400
BIAS_W = N_META + SLOTS_R * GRID_W + N_META


def shape_tables():
    eye = np.eye(P)
    half = np.kron(np.eye(2), np.ones((64, 64)))
    rot = np.zeros((P, P))
    for m in range(P):
        if m % 64 < 32:
            rot[m + 32, m] = -1.0
        else:
            rot[m - 32, m] = 1.0
    g = np.arange(P)
    ang_g = 2 * np.pi * (np.outer(g, g) % P) / P
    t = np.arange(L)
    ang_l = 2 * np.pi * (np.outer(t, t) % L) / L
    norm = 1.0 / math.sqrt(L * P)
    dft_g = np.concatenate([np.cos(ang_g), np.sin(ang_g)], 1)
    cos_l = (np.cos(ang_l) * norm).reshape(2, P, L).transpose(1, 0, 2).reshape(P, 2 * L)
    nsin_l = (-np.sin(ang_l) * norm).reshape(2, P, L).transpose(1, 0, 2).reshape(P, 2 * L)

    f32 = np.float32
    inv = (f32(10000.0) ** (-np.arange(16, dtype=f32) / f32(16))).astype(f32)
    row = np.repeat(np.arange(ROWS, dtype=f32), GRID_W)
    col = np.tile(np.arange(GRID_W, dtype=f32), ROWS)
    ang = np.concatenate([row[:, None] * inv, col[:, None] * inv], -1).astype(f32).T
    ang_d = np.tile(ang, (4, 1))
    inv = (f32(10000.0) ** (-(np.arange(0, MLA_ROPE, 2, dtype=f32) / f32(MLA_ROPE)))).astype(f32)
    pos = np.concatenate([np.arange(N_META, L2), np.arange(N_META)]).astype(f32)
    ang = (pos[:, None] * inv).astype(f32).T
    ang_m = np.tile(ang, (4, 1))

    c = np.arange(P) % GRID_W
    c0 = np.clip(c - NA_WIN_C // 2, 0, GRID_W - NA_WIN_C)[:, None]
    kc = np.arange(GRID_W)[None, :]
    mask = np.where((kc >= c0) & (kc < c0 + NA_WIN_C), 0.0, MASKED)
    return {
        "ident": eye, "ones": np.ones((P, P)), "half": half, "rot": rot,
        "cos_d": np.cos(ang_d), "sin_d": np.sin(ang_d), "cos_m": np.cos(ang_m), "sin_m": np.sin(ang_m),
        "mask": mask, "fold": (np.arange(P)[:, None] % 2 == np.arange(2)) & (np.arange(P)[:, None] < 4),
        "dft_g": dft_g, "cos_l": cos_l, "nsin_l": nsin_l,
    }


TABLE_COLS = {"ident": P, "ones": P, "fold": 2, "half": P, "rot": P, "cos_d": L, "sin_d": L, "cos_m": L2, "sin_m": L2,
              "mask": GRID_W, "dft_g": 2 * P, "cos_l": 2 * L, "nsin_l": 2 * L}
N_KEPT = 10
ROTARY_AT = sum(list(TABLE_COLS.values())[:list(TABLE_COLS).index("cos_d")])
FIRST = 2 * P + 2
KEPT = sum(list(TABLE_COLS.values())[:N_KEPT])
FOURIER = 2 * P + 4 * L

PAR_ROWS = {"norm_gain": 4 * KD, "fnet_b": KD, "norm_w": KD, "q_lat": 2, "kv_lat": 2, "subln": 1, "dq": 1,
            "dk": 1, "qn": 1, "kn": 1, "qpe": 1, "kpe": 1, "naq": 1, "nak": 1, "lam_a": 1, "lam_b": 1,
            "c": KD, "c_ctx": KD}
PAR_AT = {}
for _name, _n in PAR_ROWS.items():
    PAR_AT[_name] = sum(PAR_ROWS[x] for x in list(PAR_ROWS)[:list(PAR_ROWS).index(_name)])
N_PAR = sum(PAR_ROWS.values())
N_ADA = 2 * 6 * KD


def slab_starts():
    stages = [("ada0", 24), ("fnet_out", 6), ("ffn0_in", 22), ("ffn0_out", 11),
              ("diff_k", 4), ("diff_q", 4), ("diff_v", 4), ("diff_out", 4), ("ffn1_in", 22), ("ffn1_out", 11),
              ("kpe", 1), ("lat", 2), ("gmla", 4), ("mix", 8),
              ("gna", 4), ("naq", 4), ("nak", 4), ("out2", 8)]
    at, out = 0, {}
    for name, n in stages:
        out[name] = at
        at += n
    out["end"] = at
    return out


G = slab_starts()
NAV_G = [G["mix"] + 2 * s for s in range(4)]
UQ_G = [G["mix"] + 1, G["mix"] + 3]
UKV_G = [G["mix"] + 5, G["mix"] + 7]
FNET_OUT_Q = [2 * G["fnet_out"] + m + 2 * (m >= 4) + 2 * (m >= 6) for m in range(KD)]


def build(nc, d, out):
    with ExitStack() as ctx:
        def sb(name, shape, dt=F32):
            return ctx.enter_context(nc.sbuf_tensor(name, shape, dt))

        def sem(name):
            return ctx.enter_context(nc.semaphore(name))

        ps = ctx.enter_context(nc.psum_tensor("ps", [P, 8, 512], F32))
        x_lat = sb("x_lat", [P, KD, L])
        x_ctx = sb("x_ctx", [P, KD, LC])
        x_meta = sb("x_meta", [P, KD, N_META])
        HW = L2 + L
        hh = sb("hh", [P, KD, HW], F32R)
        hl = sb("hl", [P, KD, HW], F32R)
        ah = sb("ah", [P, 2, HW], F32R)
        al = sb("al", [P, 2, HW], F32R)
        raw = sb("raw", [P, RAW_SLOTS, SLAB])
        wh = sb("wh", [P, SPLIT_SLOTS, HALF], F32R)
        wl = sb("wl", [P, SPLIT_SLOTS, HALF], F32R)
        big = sb("big", [P, 13824])
        tab = sb("tab", [P, KEPT])
        ex = sb("ex", [P, 2, 2, 512])
        sq = sb("sq", [P, 2, HW])
        rstd = sb("rstd", [P, 2, HW])
        nrm = sb("nrm", [P, 2, HW])
        t1 = sb("t1", [P, L2])
        rows = big[:, 12000:12000 + 2 * P]
        par = sb("par", [P, N_ADA + N_PAR])
        ada = sb("ada", [P, 2, 6 * KD, 2])
        ada_flat = ada[:].rearrange("p l s c -> p (l s) c")
        ada_buf = [big[:, 11264:13312], ex[:].rearrange("p a b c -> p (a b c)")]
        ada_acc = [big[:, 13312:13824], sq[:, 0, 0:512]]
        ada_row = ex[:, 0, 1, :]
        gsc = sb("gsc", [P, 2, 2, KD, 2])
        gb = sb("gb", [P, KD, 2])
        cond = sb("cond", [P, 2 * KD])
        condr = sb("condr", [P, KD, 4], F32R)
        eps_c = sb("eps_c", [P, 1])
        sml = sb("sml", [P, 16])
        nm = sb("nm", [P, 2, 2])
        sm = sb("sm", [P, 2, 2])
        rc = sb("rc", [P, 2, 2])
        meta_b = sb("meta_b", [P, NA_HEADS * N_META])
        subg = sb("subg", [P, 1])

        T, at = {}, 0
        for name in list(TABLE_COLS)[:N_KEPT]:
            T[name] = tab[:, at:at + TABLE_COLS[name]]
            at += TABLE_COLS[name]

        def view(at, n, pattern=None, **kw):
            v = big[:, at:at + n]
            return v.rearrange(pattern, **kw) if pattern else v

        xin = view(0, 4096, "p (t d) -> p t d", t=4)
        h32 = view(4096, 4096, "p (k n) -> p k n", k=KD)
        uv = view(8192, 2048, "p (s t c) -> p s t c", s=2, t=4)
        dft_g = view(10240, 2 * P)
        cos_l = view(10240 + 2 * P, 2 * L, "p (t n) -> p t n", t=2)
        nsin_l = view(10240 + 2 * P + 2 * L, 2 * L, "p (t n) -> p t n", t=2)
        dq = view(0, 2048, "p (h n) -> p h n", h=8)
        dk = view(2048, 4096, "p (h n) -> p h n", h=8)
        dv = view(6144, 4096, "p (t e) -> p t e", t=4)
        qn = view(0, 2048, "p (h n) -> p h n", h=8)
        qp = view(2048, 2048, "p (h n) -> p h n", h=8)
        kn = view(4096, 8 * L2, "p (h n) -> p h n", h=8)
        kp = view(6272, L2)
        mv = view(6544, 3072, "p (t e) -> p t e", t=3)
        mg = view(9616, 2048, "p (h n) -> p h n", h=8)
        lat32 = ex[:].rearrange("p a b c -> p (a b c)")[:, 0:2 * HW].rearrange("p (k n) -> p k n", k=2)
        nq = view(0, 2048, "p (h n) -> p h n", h=8)
        nkx = view(2048, 8 * (L2 + N_META), "p (h n) -> p h n", h=8)
        ng = view(4352, 2048, "p (h n) -> p h n", h=8)
        runs = view(RUNS_AT, NA_HEADS * RUN, "p (h n) -> p h n", h=NA_HEADS)
        bias = view(RUNS_AT + NA_HEADS * RUN, 2 * BIAS_W, "p (s n) -> p s n", s=2)
        nv_real = view(11664, 2048, "p (t e) -> p t e", t=2)
        assert RUNS_AT + NA_HEADS * RUN + 2 * BIAS_W <= 11664
        x_ctx_flat = x_ctx[:].rearrange("p k n -> p (k n)")
        wT = x_ctx_flat.rearrange("p (s c n) -> p s c n", s=2, c=4)
        wT3 = x_ctx_flat[:, 0:6 * L].rearrange("p (s c n) -> p s c n", s=2, c=3)

        def nv_of(t, at, n):
            if t < 2:
                return nv_real[:, t, at:at + n]
            if at < 512:
                return tab[0:N_META, ROTARY_AT + at:ROTARY_AT + at + n]
            return x_ctx_flat[0:N_META, 6 * L + at - 512:6 * L + at - 512 + n]


        def par_of(name, k=0, n=1):
            at = N_ADA + PAR_AT[name] + k
            return par[:, at:at + n]

        s_rows = sem("rows_landed")
        s_tab = sem("tables_landed")
        s_xin = sem("x_landed")
        landed = [sem(f"slab_landed_{i}") for i in range(RAW_SLOTS)]
        rounded = sem("half_rounded")
        split = sem("half_split")
        used = sem("half_used")
        s_turn = sem("turned")
        s_turn_a = sem("turned_out_act")
        s_turn_v = sem("turned_out_dve")
        s_cond = sem("cond_ready")
        s_adac = sem("ada_pair_copied")
        s_adat = sem("ada_pair_turned")
        s_adal = [sem(f"ada_half_landed_{h}") for h in range(4)]
        s_am = sem("ada_products")
        s_asum = sem("ada_slab_summed")
        s_adav = sem("ada_pair_out")
        s_mod = sem("modulation_ready")
        a_ch = sem("act_chain")
        v_ch = sem("dve_chain")
        s_sq = sem("norm_squared")
        s_sum = sem("norm_summed")
        s_rstd = sem("norm_rstd")
        s_mul = sem("norm_scaled")
        s_hh = sem("norm_rounded")
        s_h = sem("norm_out")
        s_f1 = sem("fnet_inner")
        s_f1a = sem("fnet_inner_out_act")
        s_f1v = sem("fnet_inner_out_dve")
        s_f2 = sem("fnet_outer")
        s_f2a = sem("fnet_rounded")
        s_f2v = sem("fnet_split")
        s_opa = sem("outproj_biased")
        s_x = sem("x_updated")
        s_silu = sem("gate_silu")
        s_fin = sem("ffn_tile_complete")
        s_act = sem("act_written")
        s_ar = sem("act_rounded")
        s_as = sem("act_split")
        s_unit = sem("unit_done")
        s_usq = sem("unit_squared")
        s_usum = sem("unit_summed")
        s_urs = sem("unit_rstd")
        s_unrm = sem("unit_normed")
        s_urot = sem("unit_rotated")
        s_ucp = sem("unit_copied")
        s_urdy = sem("unit_ready")
        s_sc = sem("scores_done")
        s_sb = sem("scores_biased")
        s_mx = sem("row_max")
        s_ex = sem("exp_done")
        s_lam = sem("lambda_applied")
        s_w = sem("weights_ready")
        s_tr = sem("weights_turned")
        s_trc = sem("weights_copied")
        s_pv = sem("pv_done")
        s_osq = sem("o_squared")
        s_osum = sem("o_summed")
        s_ors = sem("o_rstd")
        s_on = sem("o_scaled")
        s_or = sem("o_rounded")
        s_os = sem("o_split")
        s_bias = sem("bias_ready")
        s_runs = sem("bias_runs_landed")
        s_metab = sem("meta_bias_landed")
        s_top = sem("first_tokens_complete")
        s_fo = sem("final_copied")
        s_fov = sem("final_copied_dve")
        s_out = sem("out_stored")
        s_eps = sem("eps_written")

        def positive(eng, s, value):
            if type(value) is int and value <= 0:
                return
            eng.wait_ge(s, value)

        def raw_half(at):
            g, half = divmod(at, 2)
            v = raw[:, g % RAW_SLOTS, :]
            if G["ffn0_out"] <= g < G["ffn0_out"] + 11 or G["ffn1_out"] <= g < G["ffn1_out"] + 11 \
                    or g >= G["out2"]:
                return v[:, half * D:(half + 1) * D], D, 1
            if g == G["kpe"]:
                return v[:, half * 256:(half + 1) * 256], 256, 1
            k, n = (2, 768) if g in UQ_G else (2, 1024) if g in UKV_G else (KD, 256)
            v = v[:, 0:k * n].rearrange("p (k n) -> p k n", k=k)[:, :, half * n // 2:(half + 1) * n // 2]
            return v, k * n // 2, k

        def split_half(which, at):
            _, n, k = raw_half(at)
            v = which[:, at % SPLIT_SLOTS, 0:n]
            return v.rearrange("p (k n) -> p k n", k=k) if k > 1 else v

        def round_half(act, q, at):
            act.wait_ge(landed[at // 2 % RAW_SLOTS], 2 * (q - at) + 16 * (at // 2 // RAW_SLOTS + 1))
            positive(act, used, q - SPLIT_SLOTS + 1)
            nc.scalar.activation(split_half(wh, at), raw_half(at)[0], ACT.Copy).then_inc(rounded, 1)

        def split_low(dve, q, at):
            dve.wait_ge(rounded, q + 1)
            nc.vector.tensor_tensor(split_half(wl, at), raw_half(at)[0], split_half(wh, at).bitcast(F32),
                                    ALU.subtract).then_inc(split, 1)

        def load_slab(sp, g, at, src, k, n):
            positive(sp, split, 2 * (g - RAW_SLOTS + 1))
            sp.dma_start(raw[:, at % RAW_SLOTS, 0:k * n].rearrange("p (k n) -> p k n", k=k),
                         src.rearrange("(k p) n -> p k n", p=P)).then_inc(landed[at % RAW_SLOTS], 16)

        def tile_of(which, at, k, n):
            return which[:, at % SPLIT_SLOTS, 0:k * n].rearrange("p (k n) -> p k n", k=k)

        def product(o, w_hi, w_lo, m_hi, m_lo, first, last, **kw):
            nc.tensor.matmul(o, w_hi, m_hi, start=first, stop=False, **kw)
            nc.tensor.matmul(o, w_hi, m_lo, start=False, stop=False, **kw)
            return nc.tensor.matmul(o, w_lo, m_hi, start=False, stop=last, **kw)

        def round_next(act, q, n=1):
            for h in range(q, q + n):
                if h + AHEAD < 2 * G["end"]:
                    round_half(act, h + AHEAD, h + AHEAD)

        def split_next(dve, q, n=1):
            for h in range(q, q + n):
                if h + AHEAD < 2 * G["end"]:
                    split_low(dve, h + AHEAD, h + AHEAD)

        def mod_parts(layer, n, ctx_too):
            sec = 0 if n == 0 else 3
            parts = [(lambda k: x_lat[:, k, :], 0, L, lambda k: gsc[:, layer, n, k, 0:1],
                      lambda k: ada[:, layer, sec * KD + k, 0:1])]
            if ctx_too:
                parts.append((lambda k: x_ctx[:, k, :], L, LC, lambda k: gsc[:, layer, n, k, 1:2],
                              lambda k: ada[:, layer, sec * KD + k, 1:2]))
            return parts

        NORMS = {
            "fnet": (KD, D, mod_parts(0, 0, True), None, None),
            "ffn0": (KD, D, mod_parts(0, 1, True), hh, hl),
            "diff": (KD, D, mod_parts(1, 0, True), hh, hl),
            "ffn1": (KD, D, mod_parts(1, 1, False), hh, hl),
            "second": (KD, D, [(lambda k: x_lat[:, k, :], 0, L, lambda k: par_of("norm_w", k), None),
                               (lambda k: x_meta[:, k, :], L, N_META, lambda k: par_of("norm_w", k), None)],
                       hh, hl),
            "lat": (2, MLA_RANK, [(lambda k: lat32[:, k, 0:L], 0, L, lambda k: par_of("q_lat", k), None),
                                  (lambda k: lat32[:, k, L:HW], L, L2, lambda k: par_of("kv_lat", k), None)],
                    ah, al),
        }
        BASE, SPLIT_BASE, at = {}, {}, 0
        at_s = 0
        for name, (tiles, *_rest) in NORMS.items():
            BASE[name], SPLIT_BASE[name] = at, at_s
            at += tiles
            at_s += tiles if _rest[2] is not None else 0
        ORDER = list(NORMS)
        SUMS = {"fnet": [(5, 0, NT)], "ffn0": [(5, 0, NT)], "diff": [(0, 0, NT)], "ffn1": [(7, 0, L)],
                "second": [(0, 0, L2)], "lat": [(7, 0, L), (6, L, HW)]}

        def norm_square(act, name, k):
            _, _, parts, _, _ = NORMS[name]
            b = BASE[name]
            if name in X_OF:
                act.wait_ge(s_x, X_OF[name] + k + 1)
            if k >= 2:
                act.wait_ge(s_sum, b + k - 1)
            at = 0
            for src, _, w, _, _ in parts:
                ins = nc.scalar.activation(sq[:, k % 2, at:at + w], src(k), ACT.Square)
                at += w
            ins.then_inc(s_sq, 1)

        def norm_rstd(act, link, name):
            tiles, dim, parts, _, _ = NORMS[name]
            n = sum(p[2] for p in parts)
            act.wait_ge(s_sum, BASE[name] + tiles)
            for bank, a, b in SUMS[name]:
                ins = nc.scalar.activation(rstd[:, 1, a:b], ps[:, bank, 0:b - a], ACT.Ln, bias=eps_c[:, 0:1],
                                           scale=1.0 / dim)
            link(ins)
            nc.scalar.activation(rstd[:, 0, 0:n], rstd[:, 1, 0:n], ACT.Exp, scale=-0.5).then_inc(s_rstd, 1)

        def norm_round(act, name):
            tiles, _, parts, hi, _ = NORMS[name]
            for k in range(tiles):
                act.wait_ge(s_mul, BASE[name] + k + 1)
                at = 0
                for _, off, w, _, shift in parts:
                    ins = nc.scalar.activation(hi[:, k, off:off + w], nrm[:, k % 2, at:at + w], ACT.Identity,
                                               bias=shift(k) if shift else 0.0)
                    at += w
                ins.then_inc(s_hh, 1)

        def norm_act(act, link, name):
            for k in range(NORMS[name][0]):
                norm_square(act, name, k)
            norm_rstd(act, link, name)
            if NORMS[name][3] is not None:
                norm_round(act, name)

        def norm_dve(dve, name):
            tiles, _, parts, hi, lo = NORMS[name]
            b, sb_ = BASE[name], SPLIT_BASE[name]
            dve.wait_ge(s_rstd, ORDER.index(name) + 1)
            positive(dve, s_h, b)

            def scaled(k):
                if k >= 2:
                    dve.wait_ge(s_h, b + k - 1)
                at = 0
                for src, _, w, scale, _ in parts:
                    ins = nc.vector.scalar_tensor_tensor(out=nrm[:, k % 2, at:at + w], in0=src(k),
                                                         scalar=scale(k), in1=rstd[:, 0, at:at + w],
                                                         op0=ALU.mult, op1=ALU.mult)
                    at += w
                ins.then_inc(s_mul, 1)

            def shifted(k):
                dve.wait_ge(s_mul, b + k + 1)
                if hi is not None:
                    dve.wait_ge(s_hh, sb_ + k + 1)
                at = 0
                for _, off, w, _, shift in parts:
                    src = nrm[:, k % 2, at:at + w]
                    if hi is None:
                        ins = nc.vector.tensor_scalar(h32[:, k, off:off + w], src, shift(k), None, ALU.add)
                    else:
                        ins = nc.vector.scalar_tensor_tensor(
                            out=lo[:, k, off:off + w], in0=src, scalar=shift(k) if shift else 0.0,
                            in1=hi[:, k, off:off + w].bitcast(F32), op0=ALU.add, op1=ALU.subtract)
                    at += w
                ins.then_inc(s_h, 1)

            scaled(0)
            for k in range(tiles):
                if k + 1 < tiles:
                    scaled(k + 1)
                shifted(k)

        def norm_sum(pe, name, k):
            tiles, _, parts, _, _ = NORMS[name]
            pe.wait_ge(s_sq, BASE[name] + k + 1)
            for bank, a, b in SUMS[name]:
                ins = nc.tensor.matmul(ps[:, bank, 0:b - a], T["ones"], sq[:, k % 2, a:b], start=(k == 0),
                                       stop=(k == tiles - 1))
            ins.then_inc(s_sum, 1)

        def norm_pe(pe, name):
            for k in range(NORMS[name][0]):
                norm_sum(pe, name, k)

        def unit(kind, q, k, col, cols, width, frees, **kw):
            return dict(kind=kind, q=q, k=k, col=col, cols=cols, w=width, frees=frees, **kw)

        def seg(dst, a, b):
            return (dst, a, b)

        DIFF_UNITS, LAT_UNITS, GATE_UNITS, MLA_UNITS, NA_GATE_UNITS, NA_UNITS = [], [], [], [], [], []
        for h in range(8):
            DIFF_UNITS.append(unit("head", 2 * G["diff_k"] + h, KD, 0, P, NT, 1,
                                   red="half", dim=64, gain="dk", rope=("cos_d", "sin_d", L),
                                   out=[seg(dk[:, h, L:NT], L, NT)], dst=dk[:, h, 0:L]))
        for h in range(8):
            DIFF_UNITS.append(unit("head", 2 * G["diff_q"] + h, KD, 0, P, L, 1,
                                   red="half", dim=64, gain="dq", rope=("cos_d", "sin_d", L), out=[],
                                   dst=dq[:, h, :]))
        for s in range(4):
            for t in range(4):
                DIFF_UNITS.append(unit("token", 2 * (G["diff_v"] + s) + 1, KD, 0, 256, P, 2 * (t == 3), tok=t * P,
                                       dst=dv[:, t, s * 256:(s + 1) * 256]))
        LAT_UNITS.append(unit("head", 2 * G["kpe"] + 1, KD, 0, MLA_ROPE, L2, 2, red="ones", dim=64,
                              gain="kpe", rope=("cos_m", "sin_m", L2), out=[], dst=kp[0:MLA_ROPE, :]))
        for m in range(2):
            LAT_UNITS.append(unit("copy", 2 * G["lat"] + m, KD, 0, P, L, 1, dst=lat32[:, m, 0:L]))
        for m in range(2):
            LAT_UNITS.append(unit("copy", 2 * G["lat"] + 2 + m, KD, 0, P, L2, 1, dst=lat32[:, m, L:HW]))
        hd = MLA_NOPE + MLA_ROPE

        def query_units(h):
            q = 2 * UQ_G[h // 4] + h // 2 % 2
            return [unit("head", q, 2, h % 2 * hd, P, L, 0, red="ones", dim=128, gain="qn", rope=None,
                         out=[seg(qn[:, h, :], 0, L)], src=0),
                    unit("head", q, 2, h % 2 * hd + P, MLA_ROPE, L, h % 2, red="ones", dim=64, gain="qpe",
                         rope=("cos_m", "sin_m", L), out=[], dst=qp[0:MLA_ROPE, h, :], src=0)]

        def key_value_units(h2):
            q = 2 * UKV_G[h2 // 2] + h2 % 2
            keys = [unit("head", q, 2, j * 256, P, L2, 0, red="ones", dim=128, gain="kn", rope=None,
                         out=[seg(kn[:, 2 * h2 + j, :], 0, L2)], src=L) for j in range(2)]
            values = [unit("token", q, 2, None, 256, P if t < 2 else N_META, int(t == 2), tok=L + t * P, src=L,
                           dst=mv[0:(P if t < 2 else N_META), t, h2 * 256:(h2 + 1) * 256]) for t in range(3)]
            return keys + values

        def na_value_units(s):
            return [unit("token", 2 * NAV_G[s] + 1, KD, 0, 256, P if t < 2 else N_META, 2 * (t == 2), tok=t * P,
                         dst=nv_of(t, s * 256, 256)) for t in range(3)]

        na_v = [na_value_units(s) for s in range(4)]
        MLA_UNITS.append(na_v[0][0])
        for s in range(4):
            second, third = na_v[s][1:]
            ahead = [na_v[s + 1][0]] if s < 3 else []
            if s < 2:
                a = query_units(4 * s) + query_units(4 * s + 1)
                b = query_units(4 * s + 2) + query_units(4 * s + 3)
                MLA_UNITS += a[:1] + [second] + a[1:3] + [third] + a[3:] + b[:3] + ahead + b[3:]
            else:
                a, b = key_value_units(2 * s - 4), key_value_units(2 * s - 3)
                MLA_UNITS += a[:1] + [second] + a[1:2] + [third] + a[2:] + b[:3] + ahead + b[3:]
        for m in range(8):
            GATE_UNITS.append(unit("silu", 2 * G["gmla"] + m, KD, 0, P, L, 1, dst=mg[:, m, :]))
        for m in range(8):
            NA_UNITS.append(unit("head", 2 * G["naq"] + m, KD, 0, P, L, 1, red="half",
                                 dim=64, gain="naq", rope=None, out=[seg(nq[:, m, :], 0, L)]))
        for m in range(8):
            NA_UNITS.append(unit("head", 2 * G["nak"] + m, KD, 0, P, L2, 1, red="half",
                                 dim=64, gain="nak", rope=None,
                                 out=[seg(nkx[:, m, 0:N_META], L, L2),
                                      seg(nkx[:, m, N_META:N_META + L2], 0, L2)]))
        for m in range(8):
            NA_GATE_UNITS.append(unit("silu", 2 * G["gna"] + m, KD, 0, P, L, 1, dst=ng[:, m, :]))
        PHASES = [DIFF_UNITS, LAT_UNITS, GATE_UNITS, MLA_UNITS, NA_GATE_UNITS, NA_UNITS]
        n_unit = n_head = n_rope = n_copy = n_mid = 0
        for phase in PHASES:
            for u in phase:
                u["u"] = n_unit
                n_unit += 1
                n_mid += not u["frees"]
                u["mid"] = n_mid
                if u["kind"] == "head":
                    u["h"] = n_head
                    n_head += 1
                    if u["rope"]:
                        u["r"] = n_rope
                        n_rope += 1
                else:
                    u["c"] = n_copy
                    n_copy += 1
        ALL_UNITS = [u for phase in PHASES for u in phase]
        ROPED = [u for u in ALL_UNITS if u.get("rope")]

        def unit_out(u):
            bank = u["u"] % 3
            if u["kind"] == "token":
                return ps[0:u["w"], bank, 0:u["cols"]]
            return ps[0:u["cols"], bank, 0:u["w"]]

        def unit_done(eng, u):
            if u["frees"]:
                eng.wait_ge(used, u["q"] + 1)
            else:
                eng.wait_ge(s_unit, u["mid"])

        def unit_start(pe, u, first_of_half):
            if first_of_half:
                pe.wait_ge(split, u["q"] + 1)
            if u["u"] >= 3:
                v = ALL_UNITS[u["u"] - 3]
                if v["kind"] == "head":
                    pe.wait_ge(s_unrm, v["h"] + 1)
                else:
                    pe.wait_ge(s_ucp, v["c"] + 1)

        def unit_tile(u, k):
            mh, ml = (ah, al) if "src" in u else (hh, hl)
            off = u.get("src", 0)
            o = unit_out(u)
            q = u["q"]
            first, last = k == 0, k == u["k"] - 1
            if u["kind"] == "token":
                tok = slice(u["tok"], u["tok"] + u["w"])
                if u["col"] is None:
                    def cols(w):
                        return tile_of(w, q, 2, 512)[:, k, :].rearrange("p (h two e) -> p h two e", h=2,
                                                                        two=2)[:, :, 1, :]
                else:
                    def cols(w):
                        at = (q - 1) % SPLIT_SLOTS
                        return w[:, at:at + 2, k * P:(k + 1) * P]
                oo = o.rearrange("p (h e) -> p h e", h=2)
                nc.tensor.matmul(oo, mh[:, k, tok], cols(wh), start=first, stop=False)
                nc.tensor.matmul(oo, mh[:, k, tok], cols(wl), start=False, stop=False)
                ins = nc.tensor.matmul(oo, ml[:, k, tok], cols(wh), start=False, stop=last)
            elif q == 2 * G["kpe"] + 1:
                at = q - 1 + k // 4
                m = slice(off, off + u["w"])
                ins = product(o, tile_of(wh, at, 4, MLA_ROPE)[:, k % 4, :],
                              tile_of(wl, at, 4, MLA_ROPE)[:, k % 4, :], mh[:, k, m], ml[:, k, m], first, last)
            else:
                n = P if u["k"] == KD else (384 if q // 2 in UQ_G else 512)
                whv, wlv = tile_of(wh, q, u["k"], n), tile_of(wl, q, u["k"], n)
                c = slice(u["col"], u["col"] + u["cols"])
                m = slice(off, off + u["w"])
                ins = product(o, whv[:, k, c], wlv[:, k, c], mh[:, k, m], ml[:, k, m], first, last)
            if last:
                if u["frees"]:
                    ins.then_inc(used, u["frees"])
                else:
                    ins.then_inc(s_unit, 1)

        def units_pe(pe, phase, h_base=None, before=0):
            for i in range(len(phase) + 2):
                if i == 0 and h_base is not None:
                    for u in phase[:2]:
                        unit_start(pe, u, True)
                    for k in range(KD):
                        pe.wait_ge(s_h, h_base + k + 1)
                        for u in phase[:2]:
                            unit_tile(u, k)
                elif before <= i < len(phase) and (i > 1 or h_base is None):
                    unit_start(pe, phase[i], i == 0 or phase[i - 1]["q"] != phase[i]["q"])
                    for k in range(phase[i]["k"]):
                        unit_tile(phase[i], k)
                if 1 <= i <= len(phase) and phase[i - 1]["kind"] == "head":
                    u = phase[i - 1]
                    h, m = u["h"], u["cols"]
                    pe.wait_ge(s_usq, h + 1)
                    positive(pe, s_urs, h - 1)
                    nc.tensor.matmul(ps[0:m, 3 + h % 2, 0:u["w"]], T[u["red"]][0:m, 0:m],
                                     sq[0:m, h % 2, 0:u["w"]], start=True, stop=True).then_inc(s_usum, 1)
                if 2 <= i and phase[i - 2].get("rope"):
                    u = phase[i - 2]
                    m, w = u["cols"], u["rope"][2]
                    pe.wait_ge(s_unrm, u["h"] + 1)
                    positive(pe, s_urdy, u["r"] - 1)
                    nc.tensor.matmul(ps[0:m, 5 + u["r"] % 2, 0:w], T["rot"][0:m, 0:m],
                                     nrm[0:m, u["h"] % 2, 0:w], start=True, stop=True).then_inc(s_urot, 1)

        def halves_after(phase, i):
            halves = []
            if 1 <= i <= len(phase) and phase[i - 1]["frees"] == 2:
                halves.append(phase[i - 1]["q"])
            if i < len(phase) and phase[i]["frees"]:
                halves.append(phase[i]["q"] + 1 - phase[i]["frees"])
            return halves

        def units_act(act, link, phase):
            for i in range(len(phase) + 1):
                if i < len(phase):
                    u = phase[i]
                    unit_done(act, u)
                    if u["kind"] == "head":
                        positive(act, s_usum, u["h"] - 1)
                        nc.scalar.activation(sq[0:u["cols"], u["h"] % 2, 0:u["w"]], unit_out(u),
                                             ACT.Square).then_inc(s_usq, 1)
                    else:
                        f = ACT.Silu if u["kind"] == "silu" else ACT.Copy
                        nc.scalar.activation(u["dst"], unit_out(u), f).then_inc(s_ucp, 1)
                if i >= 1 and phase[i - 1]["kind"] == "head":
                    u = phase[i - 1]
                    m, w = u["cols"], u["w"]
                    act.wait_ge(s_usum, u["h"] + 1)
                    positive(act, s_unrm, u["h"])
                    link(nc.scalar.activation(rstd[0:m, 1, 0:w], ps[0:m, 3 + u["h"] % 2, 0:w], ACT.Ln,
                                              bias=eps_c[0:m, 0:1], scale=1.0 / u["dim"]))
                    nc.scalar.activation(rstd[0:m, 0, 0:w], rstd[0:m, 1, 0:w], ACT.Exp,
                                         scale=-0.5).then_inc(s_urs, 1)
                for q in halves_after(phase, i):
                    round_next(act, q)

        def units_dve(dve, link, phase):
            for i in range(len(phase) + 2):
                if 1 <= i <= len(phase) and phase[i - 1]["kind"] == "head":
                    u = phase[i - 1]
                    m = u["cols"]
                    o = unit_out(u)
                    dve.wait_ge(s_urs, u["h"] + 1)
                    outs = list(u["out"])
                    if u["rope"]:
                        w = u["rope"][2]
                        old = [v for v in ROPED if v["h"] == u["h"] - 2]
                        if old:
                            dve.wait_ge(s_urdy, old[0]["r"] + 1)
                        outs.append((nrm[0:m, u["h"] % 2, 0:w], 0, w))
                    for dst, a, b in outs:
                        ins = nc.vector.scalar_tensor_tensor(
                            out=dst, in0=o[:, a:b], scalar=par_of(u["gain"])[0:m, :], in1=rstd[0:m, 0, a:b],
                            op0=ALU.mult, op1=ALU.mult)
                    ins.then_inc(s_unrm, 1)
                if i >= 2 and phase[i - 2].get("rope"):
                    u = phase[i - 2]
                    m = u["cols"]
                    cos, sin, w = u["rope"]
                    dve.wait_ge(s_unrm, u["h"] + 1)
                    positive(dve, s_urdy, u["r"])
                    tile = nrm[0:m, u["h"] % 2, 0:w]
                    link(nc.vector.tensor_tensor(t1[0:m, 0:w], tile, T[cos][0:m, 0:w], ALU.mult))
                    dve.wait_ge(s_urot, u["r"] + 1)
                    link(nc.vector.tensor_tensor(tile, ps[0:m, 5 + u["r"] % 2, 0:w], T[sin][0:m, 0:w],
                                                 ALU.mult))
                    nc.vector.tensor_tensor(u["dst"], t1[0:m, 0:w], tile, ALU.add).then_inc(s_urdy, 1)
                for q in halves_after(phase, i):
                    split_next(dve, q)
            done = [u for u in phase if u.get("rope")]
            if done:
                dve.wait_ge(s_urdy, done[-1]["r"] + 1)

        def chunk_plan(keys):
            return [(a, min(P, keys - a)) for a in range(0, keys, P)]

        ATT = {
            "diff": dict(heads=8, maps=2, keys=NT, scale=DIFF_DIM ** -0.5, pair=1),
            "mla": dict(heads=8, maps=1, keys=L2, scale=(MLA_NOPE + MLA_ROPE) ** -0.5, pair=1),
            "na": dict(heads=16, maps=1, keys=L2, scale=NA_DIM ** -0.5, pair=2),
        }
        step_base = head_base = group_base = map_base = 0
        for name, a in ATT.items():
            a.update(name=name, steps=2 * a["heads"], s0=step_base, h0=head_base, g0=group_base, m0=map_base)
            a["groups"] = a["heads"] // a["pair"]
            step_base += a["steps"]
            head_base += a["heads"]
            group_base += a["groups"]
            map_base += a["maps"] * a["steps"]

        def scores_of(a, h, t, c):
            q = slice(t * P, (t + 1) * P)
            if a["name"] == "diff":
                r = slice(64 * c, 64 * c + 64)
                return [(dq[r, h, q], dk[r, h, :])]
            if a["name"] == "mla":
                return [(qn[:, h, q], kn[:, h, :]), (qp[0:MLA_ROPE, h, q], kp[0:MLA_ROPE, :])]
            r = slice(64 * (h % 2), 64 * (h % 2) + 64)
            off = N_META if t == 0 else 0
            return [(nq[r, h // 2, q], nkx[r, h // 2, off:off + L2])]

        def chunks_of(a, t):
            if a["name"] == "na" and t == 1:
                return [(N_META, P), (N_META + P, P), (0, N_META)]
            return chunk_plan(a["keys"])

        def values_of(a, h, j, n):
            if a["name"] == "na":
                return nv_of(j, h * NA_DIM, NA_DIM)
            v = dv if a["name"] == "diff" else mv
            return v[0:n, j, h * P:(h + 1) * P]

        def turned(a):
            return wT if a["name"] == "diff" else wT3

        def score_bank(a, i, c):
            return (i % 2) * a["maps"] + c

        def o_psum(a, f):
            return ps[:, 6 + f % 2, 0:L]

        def att_pe(pe, a, tail=None):
            for i in range(a["steps"] + 6):
                if i < a["steps"]:
                    h, t = divmod(i, 2)
                    if i >= 2:
                        if a["name"] == "na":
                            pe.wait_ge(s_sb, i - 1)
                        else:
                            pe.wait_ge(s_ex, a["m0"] + (i - 1) * a["maps"])
                    for c in range(a["maps"]):
                        pairs = scores_of(a, h, t, c)
                        for j, (w, m) in enumerate(pairs):
                            ins = nc.tensor.matmul(ps[:, score_bank(a, i, c), 0:a["keys"]], w, m,
                                                   start=(j == 0), stop=(j == len(pairs) - 1))
                    ins.then_inc(s_sc, 1)
                if i % 2 == 1 and 0 <= (i - 5) // 2 < a["heads"]:
                    h = (i - 5) // 2
                    f = h // a["pair"]
                    pe.wait_ge(s_trc, a["s0"] + 2 * h + 2)
                    if h % a["pair"] == 0:
                        positive(pe, s_on, a["g0"] + f - 1)
                    part = P // a["pair"]
                    row = h % a["pair"] * part
                    plan = chunk_plan(a["keys"])
                    for j, (_, n) in enumerate(plan):
                        ins = nc.tensor.matmul(o_psum(a, f)[row:row + part, :], values_of(a, h, j, n),
                                               turned(a)[0:n, h % 2, j, :], start=(j == 0), stop=(j == len(plan) - 1))
                    ins.then_inc(s_pv, 1)
                if a["name"] == "diff" and i % 2 == 0 and 0 <= (i - 6) // 2 < a["heads"]:
                    sub_sum(pe, a, (i - 6) // 2)
                if 2 <= i < a["steps"] + 2:
                    j0 = i - 2
                    pe.wait_ge(s_w, a["s0"] + j0 + 1)
                    positive(pe, s_trc, a["s0"] + j0 - 1)
                    for j, (at, n) in enumerate(chunks_of(a, j0 % 2)):
                        ins = nc.tensor.transpose(ps[0:n, 4 + j0 % 2, j * P:(j + 1) * P],
                                                  ex[:, j0 % 2, 0, at:at + n], T["ident"])
                    ins.then_inc(s_tr, 1)
                if tail:
                    tail(i)

        def sub_sum(pe, a, h):
            pe.wait_ge(s_osq, h + 1)
            nc.tensor.matmul(ps[:, 6 + h % 2, L:2 * L], T["ones"], sq[:, h % 2, 0:L], start=True,
                             stop=True).then_inc(s_osum, 1)

        def att_act(act, link, a):
            diff = a["name"] == "diff"
            for i in range(a["steps"] + 10):
                if i < a["steps"]:
                    for c in range(a["maps"]):
                        act.wait_ge(s_mx, a["s0"] + i + 1)
                        src = ex[:, i % 2, 1, 0:a["keys"]] if a["name"] == "na" else \
                            ps[:, score_bank(a, i, c), 0:a["keys"]]
                        positive(act, s_tr, a["s0"] + i - 1)
                        nc.scalar.activation(ex[:, i % 2, c, 0:a["keys"]], src, ACT.Exp,
                                             bias=nm[:, i % 2, c:c + 1],
                                             accum_out=sm[:, i % 2, c:c + 1]).then_inc(s_ex, 1)
                if 2 <= i < a["steps"] + 2:
                    j0 = i - 2
                    h, t = divmod(j0, 2)
                    act.wait_ge(s_tr, a["s0"] + j0 + 1)
                    if h >= 2:
                        act.wait_ge(s_pv, a["h0"] + h - 1)
                    full = [c for c in chunk_plan(a["keys"]) if c[1] == P]
                    ins = nc.scalar.activation(
                        turned(a)[:, h % 2, 0:len(full), t * P:(t + 1) * P],
                        ps[:, 4 + j0 % 2, 0:len(full) * P].rearrange("p (c n) -> p c n", c=len(full)), ACT.Copy)
                    if len(full) < len(chunk_plan(a["keys"])):
                        ins = nc.scalar.activation(turned(a)[0:N_META, h % 2, len(full), t * P:(t + 1) * P],
                                                   ps[0:N_META, 4 + j0 % 2, len(full) * P:(len(full) + 1) * P],
                                                   ACT.Copy)
                    ins.then_inc(s_trc, 1)
                if diff and i % 2 == 1 and 0 <= (i - 5) // 2 < a["heads"]:
                    h = (i - 5) // 2
                    act.wait_ge(s_pv, a["h0"] + h + 1)
                    positive(act, s_osum, h - 1)
                    nc.scalar.activation(sq[:, h % 2, 0:L], o_psum(a, h), ACT.Square).then_inc(s_osq, 1)
                if diff and i % 2 == 0 and 0 <= (i - 6) // 2 < a["heads"]:
                    h = (i - 6) // 2
                    act.wait_ge(s_osum, h + 1)
                    positive(act, s_on, h)
                    link(nc.scalar.activation(rstd[:, 1, 0:L], ps[:, 6 + h % 2, L:2 * L], ACT.Ln, bias=eps_c[:, 0:1],
                                              scale=1.0 / P))
                    nc.scalar.activation(rstd[:, 0, 0:L], rstd[:, 1, 0:L], ACT.Exp, scale=-0.5)\
                        .then_inc(s_ors, 1)
                f, rest = divmod(i - (8 if diff else 2 * a["pair"] + 4), 2 * a["pair"])
                if rest == 0 and 0 <= f < a["groups"]:
                    o_round(act, a, f)

        def o_out(a, f, which):
            return which[:, f, L2:L2 + L] if a["name"] == "mla" else which[:, f, 0:L]

        def o_round(act, a, f):
            act.wait_ge(s_on, a["g0"] + f + 1)
            nc.scalar.activation(o_out(a, f, hh), nrm[:, f % 2, 0:L], ACT.Copy).then_inc(s_or, 1)

        def o_split(dve, a, f):
            dve.wait_ge(s_or, a["g0"] + f + 1)
            nc.vector.tensor_tensor(o_out(a, f, hl), nrm[:, f % 2, 0:L], o_out(a, f, hh).bitcast(F32),
                                    ALU.subtract).then_inc(s_os, 1)

        def att_dve(dve, link, mark, a):
            diff, na = a["name"] == "diff", a["name"] == "na"
            n = a["keys"]
            def inverse(i):
                dve.wait_ge(s_ex, a["m0"] + (i + 1) * a["maps"])
                return mark(nc.vector.reciprocal(rc[:, i % 2, 0:a["maps"]], sm[:, i % 2, 0:a["maps"]]))

            def weights(i, inverted):
                j = i % 2
                dve.wait_ge(v_ch, inverted)
                if diff:
                    nc.vector.tensor_scalar(rc[:, j, 1:2], rc[:, j, 1:2], sml[:, 5:6], None, ALU.mult)\
                        .then_inc(s_lam, 1)
                    link(nc.vector.tensor_scalar(ex[:, j, 0, 0:n], ex[:, j, 0, 0:n], rc[:, j, 0:1], None,
                                                 ALU.mult))
                    dve.wait_ge(s_lam, i + 1)
                    nc.vector.scalar_tensor_tensor(out=ex[:, j, 0, 0:n], in0=ex[:, j, 1, 0:n],
                                                   scalar=rc[:, j, 1:2], in1=ex[:, j, 0, 0:n],
                                                   op0=ALU.mult, op1=ALU.add).then_inc(s_w, 1)
                else:
                    nc.vector.tensor_scalar(ex[:, j, 0, 0:n], ex[:, j, 0, 0:n], rc[:, j, 0:1], None,
                                            ALU.mult).then_inc(s_w, 1)

            for i in range(a["steps"] + 10):
                if i < a["steps"]:
                    dve.wait_ge(s_sc, a["s0"] + i + 1)
                    if na:
                        h, t = divmod(i, 2)
                        off = N_META + 2 * GRID_W if t == 0 else 0
                        dve.wait_ge(s_bias, h + 1)
                        nc.vector.tensor_tensor(ex[:, i % 2, 1, 0:n], ps[:, score_bank(a, i, 0), 0:n],
                                                bias[:, h % 2, off:off + n], ALU.add).then_inc(s_sb, 1)
                if 1 <= i <= a["steps"]:
                    inverted = inverse(i - 1)
                if i < a["steps"]:
                    if na:
                        dve.wait_ge(s_sb, i + 1)
                        nc.vector.tensor_reduce(nm[:, i % 2, 0:1], ex[:, i % 2, 1, 0:n], AX_X, ALU.max,
                                                negate=True).then_inc(s_mx, 1)
                    else:
                        b = score_bank(a, i, 0)
                        nc.vector.tensor_reduce(nm[:, i % 2, 0:a["maps"]], ps[:, b:b + a["maps"], 0:n], AX_X,
                                                ALU.max, negate=True).then_inc(s_mx, 1)
                if 1 <= i <= a["steps"]:
                    weights(i - 1, inverted)
                if diff:
                    if i % 2 == 1 and 0 <= (i - 7) // 2 < a["groups"]:
                        f = (i - 7) // 2
                        dve.wait_ge(s_ors, f + 1)
                        positive(dve, s_os, a["g0"] + f - 1)
                        nc.vector.scalar_tensor_tensor(out=nrm[:, f % 2, 0:L], in0=o_psum(a, f),
                                                       scalar=subg[:, 0:1], in1=rstd[:, 0, 0:L],
                                                       op0=ALU.mult, op1=ALU.mult).then_inc(s_on, 1)
                    if i % 2 == 1 and 0 <= (i - 9) // 2 < a["groups"]:
                        o_split(dve, a, (i - 9) // 2)
                else:
                    per = 2 * a["pair"]
                    f, rest = divmod(i - per - 3, per)
                    if rest == 0 and 0 <= f < a["groups"]:
                        dve.wait_ge(s_pv, a["h0"] + a["pair"] * (f + 1))
                        positive(dve, s_os, a["g0"] + f - 1)
                        gate = mg if a["name"] == "mla" else ng
                        nc.vector.tensor_tensor(nrm[:, f % 2, 0:L], o_psum(a, f), gate[:, f, :],
                                                ALU.mult).then_inc(s_on, 1)
                    f, rest = divmod(i - per - 5, per)
                    if rest == 0 and 0 <= f < a["groups"]:
                        o_split(dve, a, f)

        def outproj_part(pe, q, m, ks, n, first_wait):
            pe.wait_ge(split, q + 1)
            for k in ks:
                first_wait(k)
                product(ps[:, m % 4, 0:n], tile_of(wh, q, KD, P)[:, k, :], tile_of(wl, q, KD, P)[:, k, :],
                        hh[:, k, 0:n], hl[:, k, 0:n], k == 0, False)

        def outproj_pe(pe, halves, n, base, norm, first_wait, between=None, before=()):
            for m, q in enumerate(halves):
                pe.wait_ge(split, q + 1)
                if m >= 4:
                    pe.wait_ge(s_x, base + m - 3)
                whv, wlv = tile_of(wh, q, KD, P), tile_of(wl, q, KD, P)
                for k in range(KD):
                    if (m, k) in before:
                        continue
                    if m == 0:
                        first_wait(k)
                    ins = product(ps[:, m % 4, 0:n], whv[:, k, :], wlv[:, k, :], hh[:, k, 0:n], hl[:, k, 0:n],
                                  k == 0, k == KD - 1)
                ins.then_inc(used, 1)
                if m >= 2:
                    norm_sum(pe, norm, m - 2)
                if between:
                    between(m, q)
            norm_sum(pe, norm, KD - 2)
            norm_sum(pe, norm, KD - 1)

        X_FNET, X_FFN0, X_DIFF, X_FFN1 = 0, 8, 16, 24
        X_OF = {"ffn0": X_FNET, "diff": X_FFN0, "ffn1": X_DIFF, "second": X_FFN1}

        block = ctx.enter_context(nc.Block())
        v_count = [0]
        a_count = [0]

        @block.sync
        def _(sp):
            def load(g, src, k, n):
                load_slab(sp, g, g, src, k, n)

            sp.dma_start(rows[0:N_PAR, P:2 * P], d["params"]).then_inc(s_rows, 16)
            sp.dma_start(tab[:, 0:FIRST], d["tables"][:, 0:FIRST]).then_inc(s_rows, 16)
            sp.dma_start(rows[0:N_ADA, 0:P], d["b_ada"]).then_inc(s_rows, 16)
            for s in range(24):
                if s == RAW_SLOTS:
                    for a, src in enumerate((d["x"], d["ctx"])):
                        sp.dma_start(xin[:, 2 * a:2 * a + 2, :], src[0].rearrange("(t p) n -> p t n", p=P))\
                            .then_inc(s_xin, 16)
                    sp.dma_start(h32[0:N_META, 0:2, :].rearrange("p a b -> p (a b)"), d["meta_tokens_2"])\
                        .then_inc(s_xin, 16)
                load(G["ada0"] + s, d["w_ada"][0, :, s * 256:(s + 1) * 256], KD, 256)
            for m in range(0, KD, 2):
                load(FNET_OUT_Q[m] // 2, d["fnet_w_out"][0, :, m * P:(m + 2) * P], KD, 256)
                if m in (2, 4):
                    load(FNET_OUT_Q[m] // 2 + 1, d["w_ada"][1, :, (m - 2) * P:m * P], KD, 256)

            def ffn0(i, at):
                g = G["ffn0_in"]
                for j in range(2):
                    load_slab(sp, g + 2 * i + j, at + j, d["ffn_w_in"][0, :, bass.ds(i * 256 + j * D_FF, 256)],
                              KD, 256)
            ffn0(0, G["ffn0_in"])
            with sp.Fori(0, 5) as i:
                for t in range(2):
                    ffn0(2 * i + 1 + t, G["ffn0_in"] + 2 + 2 * t)

            def ffn_out(layer, g, s, at):
                load_slab(sp, g, at, d["ffn_w_out"][layer, bass.ds(s * 256, 256), :], 2, D)

            def ffn_out_all(layer, g0):
                for s in range(3):
                    ffn_out(layer, g0 + s, s, g0 + s)
                with sp.Fori(0, 2) as i:
                    for j in range(4):
                        ffn_out(layer, g0 + 3 + j + i * 4, i * 4 + 3 + j, g0 + 3 + j)

            ffn_out_all(0, G["ffn0_out"])
            for g, col in ((G["diff_k"], D), (G["diff_q"], 0), (G["diff_v"], 2 * D)):
                for s in range(4):
                    load(g + s, d["diff_w_in"][0, :, col + s * 256:col + (s + 1) * 256], KD, 256)
            for s in range(4):
                load(G["diff_out"] + s, d["diff_w_out"][0, :, s * 256:(s + 1) * 256], KD, 256)

            def ffn1(i, t, at):
                for j in range(2):
                    load_slab(sp, G["ffn1_in"] + 2 * t + j, at + j,
                              d["ffn_w_in"][1, :, bass.ds(t * 256 + j * D_FF, 256)], KD, 256)

            ffn1(0, 0, G["ffn1_in"])
            with sp.Fori(0, 5) as i:
                for t in range(2):
                    ffn1(i, 2 * i + 1 + t, G["ffn1_in"] + 2 + 2 * t)
            ffn_out_all(1, G["ffn1_out"])

            w_in = d["w_in_2"]
            load(G["kpe"], w_in[0, :, IN_KPE:IN_KPE + MLA_ROPE], KD, MLA_ROPE)
            load(G["lat"], w_in[0, :, IN_QLAT:IN_QLAT + 256], KD, 256)
            load(G["lat"] + 1, w_in[0, :, IN_KVLAT:IN_KVLAT + 256], KD, 256)
            for s in range(4):
                load(G["gmla"] + s, w_in[0, :, IN_GMLA + s * 256:IN_GMLA + (s + 1) * 256], KD, 256)
            for s in range(4):
                load(NAV_G[s], w_in[0, :, IN_NAV + s * 256:IN_NAV + (s + 1) * 256], KD, 256)
                if s < 2:
                    load(UQ_G[s], d["w_uq_2"][0, :, s * 768:(s + 1) * 768], 2, 768)
                else:
                    load(UKV_G[s - 2], d["w_ukv_2"][0, :, (s - 2) * 1024:(s - 1) * 1024], 2, 1024)
            for g, col in ((G["gna"], IN_GNA), (G["naq"], IN_NAQ), (G["nak"], IN_NAK)):
                for s in range(4):
                    load(g + s, w_in[0, :, col + s * 256:col + (s + 1) * 256], KD, 256)
            for s in range(8):
                load(G["out2"] + s, d["w_out_2"][0, s * 256:(s + 1) * 256, :], 2, D)
            for t in range(2):
                sp.wait_ge(s_fo, t + 1)
                sp.wait_ge(s_fov, t + 1)
                sp.dma_start(out[0, t * P:(t + 1) * P, :], big[:, t * D:(t + 1) * D]).then_inc(s_out, 16)
            sp.wait_ge(s_out, 32)

        @block.gpsimd
        def _(pool):
            pool.wait_ge(s_xin, 48)
            pool.dma_start(tab[:, FIRST:], d["tables"][:, FIRST:]).then_inc(s_tab, 16)
            pool.dma_start(big[:, 10240:10240 + FOURIER], d["fourier"]).then_inc(s_tab, 16)
            pool.dma_start(meta_b[:, :], bass.AP(tensor=d["meta_bias"].tensor, offset=0,
                                                 ap=[[0, P], [1, NA_HEADS * N_META]])).then_inc(s_metab, 16)
            pool.wait_ge(s_metab, 16)
            pool.wait_ge(s_tab, 32)

            def modulation(i):
                for h in range(4):
                    if type(i) is int and i == 0:
                        pool.wait_ge(s_x, X_FNET + KD)
                    else:
                        pool.wait_ge(s_am, i * 32 + (8 * h - 24))
                    pool.dma_start(ada_buf[h // 2][:, h % 2 * 1024:(h % 2 + 1) * 1024]
                                   .rearrange("p (k n) -> p k n", k=4),
                                   d["w_ada"][1, h % 2 * 512:(h % 2 + 1) * 512,
                                              bass.ds(i * 512 + (512 + h // 2 * 256), 256)]
                                   .rearrange("(k p) n -> p k n", p=P)).then_inc(s_adal[h], 16)

            modulation(0)
            with pool.Fori(1, 11) as i:
                modulation(i)
            pool.wait_ge(s_on, ATT["mla"]["g0"] + ATT["mla"]["groups"])
            flat = NA_HEADS * REL_R * REL_C
            for half in range(2):
                first = flat - 1 - (NA_HEADS - 1) * REL_R * REL_C - (NA_WIN_R - 1 - 2 - half) * REL_C \
                    - (NA_WIN_C - 1) - (RUN - 1)
                pool.dma_start(runs[64 * half:64 * half + 64, :, :],
                               bass.AP(tensor=d["rel_bias_rev"].tensor, offset=first,
                                       ap=[[1, 64], [REL_R * REL_C, NA_HEADS], [1, RUN]])).then_inc(s_runs, 16)
            pool.wait_ge(s_runs, 32)
            for h in range(NA_HEADS):
                s = h % 2
                if h >= 2:
                    pool.wait_ge(s_sb, 2 * (h - 1))
                at = RUNS_AT + (NA_HEADS - 1 - h) * RUN + RUN - 1
                run = bass.AP(tensor=big, offset=at, ap=[[13824, P], [-REL_C, SLOTS_R], [-1, GRID_W]])
                mask = bass.AP(tensor=tab, offset=sum(list(TABLE_COLS.values())[:N_KEPT - 1]), ap=[[KEPT, P], [0, SLOTS_R], [1, GRID_W]])
                for c in (0, N_META + SLOTS_R * GRID_W):
                    nc.gpsimd.tensor_copy(bias[:, s, c:c + N_META], meta_b[:, h * N_META:(h + 1) * N_META])
                nc.gpsimd.tensor_tensor(
                    bias[:, s, N_META:N_META + SLOTS_R * GRID_W].rearrange("p (j c) -> p j c", j=SLOTS_R),
                    run, mask, ALU.add).then_inc(s_bias, 1)

        @block.scalar
        def _(act):
            def link(ins):
                a_count[0] += 1
                ins.then_inc(a_ch, 1)
                act.wait_ge(a_ch, a_count[0])

            def exp_and_ln():
                nc.scalar.preload_act_table_set("natural_log_exp_and_others")

            act.wait_ge(s_turn_v, 1)
            link(nc.scalar.activation(cond[:, :], par_of("c", 0, 2 * KD), ACT.Silu))
            nc.scalar.activation(condr[:, :, 0:2], cond[:, :].rearrange("p (c k) -> p k c", c=2), ACT.Copy)\
                .then_inc(s_cond, 1)
            act.wait_ge(s_turn, 2)
            for c in range(2):
                ins = nc.scalar.activation(sml[:, 2 + c:3 + c], ps[:, 3 - 2 * c, c:c + 1], ACT.Exp)
            ins.then_inc(s_mod, 1)
            for q in range(AHEAD):
                round_half(act, q, q)
            round_next(act, 0, 4)
            for k in range(KD):
                act.wait_ge(s_turn, 3 + k)
                nc.scalar.activation(x_ctx[:, k, :], ps[:, 2 + k % 2, 0:LC], ACT.Copy).then_inc(s_turn_a, 1)
            round_next(act, 4, 2)
            exp_and_ln()
            round_next(act, 6, 2)
            act.wait_ge(s_turn_a, KD)
            act.wait_ge(s_turn_v, 3 + KD)
            norm_square(act, "fnet", 0)
            norm_square(act, "fnet", 1)
            round_next(act, 8, 4)
            norm_square(act, "fnet", 2)
            norm_square(act, "fnet", 3)
            round_next(act, 12, 4)
            for k in range(4, 8):
                norm_square(act, "fnet", k)
            norm_rstd(act, link, "fnet")
            for i in range(8 + 1):
                if i < 8:
                    act.wait_ge(s_f1, i + 1)
                    if i >= 2:
                        act.wait_ge(s_f2, i - 1)
                    nc.scalar.activation(uv[:, i % 2, 0:2, :].rearrange("p t c -> p (t c)"),
                                         ps[:, 2 * (i % 2), :], ACT.Copy).then_inc(s_f1a, 1)
                    round_next(act, 16 + 4 * i, 4)
                if i >= 1:
                    act.wait_ge(s_f2, i)
                    nc.scalar.activation(hh[:, i - 1, 0:NT], ps[:, 4 + (i - 1) % 2, :], ACT.Copy)\
                        .then_inc(s_f2a, 1)
            for m, q in enumerate(FNET_OUT_Q):
                act.wait_ge(used, q + 1)
                if m >= 2:
                    act.wait_ge(s_x, m - 1)
                nc.scalar.activation(ex[:, m % 2, 0, :], ps[:, m % 4, :], ACT.Identity, scale=1.0,
                                     bias=par_of("fnet_b", m)).then_inc(s_opa, 1)
                if m >= 1:
                    norm_square(act, "ffn0", m - 1)
                if m == KD - 1:
                    norm_square(act, "ffn0", m)
                round_next(act, q)
                if m in (3, 5):
                    round_next(act, q + 1, 2)
            norm_rstd(act, link, "ffn0")
            norm_round(act, "ffn0")

            def silu_gate(i, j, n, gtile, q):
                act.wait_ge(used, q + 1)
                positive(act, s_act, gtile + 2 * i + j - 1)
                nc.scalar.activation(nrm[:, j, 0:n], ps[:, j, 0:n], ACT.Silu).then_inc(s_silu, 1)

            def act_round(layer, k, at, n, q0):
                if type(k) is not int or k >= 2:
                    act.wait_ge(used, k + (q0 - 1))
                nc.scalar.activation(ah[:, at % 2, 0:n], big[:, bass.ds(k * n, n)], ACT.Copy)\
                    .then_inc(s_ar, 1)

            def ffn_out(layer, g0, n, norm):
                q0 = 2 * g0
                exp_and_ln()
                for k in range(2):
                    act_round(layer, k + 2, k, n, q0)
                    round_next(act, q0 + k)
                with act.Fori(0, 2) as i:
                    for j in range(8):
                        act_round(layer, i * 8 + (j + 4), j, n, q0)
                        round_half(act, i * 8 + (q0 + 2 + j + AHEAD), q0 + 2 + j + AHEAD)
                act.wait_ge(s_act, (layer + 1) * KF)
                for k in range(18, 20):
                    act_round(layer, k + 2, k, n, q0)
                    round_next(act, q0 + k)
                for m in range(KD):
                    norm_square(act, norm, m)
                round_next(act, q0 + 20)
                norm_rstd(act, link, norm)
                norm_round(act, norm)
                round_next(act, q0 + 21)

            act.wait_ge(s_hh, KD)
            nc.scalar.preload_act_table(ACT.Silu)
            q = 2 * G["ffn0_in"]

            def first_rounds(layer, n, q0):
                act.wait_ge(s_act, layer * KF + 2)
                for k in range(2):
                    act_round(layer, k, k, n, q0)

            def ffn0_turn(i, at):
                for j in range(4):
                    round_half(act, i * 4 + (q + j + AHEAD), at + j + AHEAD)
                    if j < 2:
                        silu_gate(i, j, NT, 0, i * 4 + (q + j))
                    if j == 1 and type(i) is int and i == 10:
                        first_rounds(0, NT, 2 * G["ffn0_out"])

            ffn0_turn(0, q)
            with act.Fori(0, 4) as i:
                for t in range(2):
                    ffn0_turn(2 * i + 1 + t, q + 4 + 4 * t)
            for t in (9, 10):
                ffn0_turn(t, q + 4 * t)
            ffn_out(0, G["ffn0_out"], NT, "diff")
            units_act(act, link, DIFF_UNITS)
            att_act(act, link, ATT["diff"])
            for m in range(KD):
                if m >= 1:
                    norm_square(act, "ffn1", m - 1)
                if m == KD - 1:
                    norm_square(act, "ffn1", m)
                round_next(act, 2 * G["diff_out"] + m)
            norm_rstd(act, link, "ffn1")
            norm_round(act, "ffn1")
            nc.scalar.preload_act_table(ACT.Silu)
            q1 = 2 * G["ffn1_in"]

            def ffn1_turn(i, at):
                first = i * 4 + q1
                for j in range(4):
                    round_half(act, first + (j + AHEAD), at + j + AHEAD)
                    if j < 2:
                        silu_gate(i, j, L, KF, first + j)
                    if j == 1 and type(i) is int and i == 10:
                        first_rounds(1, L, 2 * G["ffn1_out"])

            ffn1_turn(0, q1)
            with act.Fori(0, 4) as i:
                for t in range(2):
                    ffn1_turn(2 * i + 1 + t, q1 + 4 + 4 * t)
            for t in (9, 10):
                ffn1_turn(t, q1 + 4 * t)
            ffn_out(1, G["ffn1_out"], L, "second")
            units_act(act, link, LAT_UNITS)
            act.wait_ge(s_ucp, LAT_UNITS[-1]["c"] + 1)
            norm_act(act, link, "lat")
            units_act(act, link, GATE_UNITS)
            exp_and_ln()
            units_act(act, link, MLA_UNITS)
            att_act(act, link, ATT["mla"])
            units_act(act, link, NA_GATE_UNITS)
            exp_and_ln()
            units_act(act, link, NA_UNITS)
            att_act(act, link, ATT["na"])
            round_next(act, 2 * G["out2"], 16)
            act.wait_ge(s_top, 1)
            nc.scalar.activation(big[:, 0:512], ps[:, 0, :], ACT.Copy).then_inc(s_fo, 1)
            act.wait_ge(used, 2 * G["end"])
            nc.scalar.activation(big[:, D:D + 512], ps[:, 2, :], ACT.Copy).then_inc(s_fo, 1)

        @block.vector
        def _(dve):
            def link(ins):
                v_count[0] += 1
                ins.then_inc(v_ch, 1)
                dve.wait_ge(v_ch, v_count[0])

            def mark(ins):
                v_count[0] += 1
                ins.then_inc(v_ch, 1)
                return v_count[0]

            link(nc.vector.memset(eps_c[:, :], EPS))
            dve.wait_ge(s_turn, 1)
            nc.vector.tensor_copy(par[:, :], ps[:, 0, 0:N_ADA + N_PAR]).then_inc(s_turn_v, 1)
            dve.wait_ge(s_turn_v, 1)
            nc.vector.tensor_tensor(sml[:, 0:1], par_of("lam_a"), par_of("lam_b"), ALU.mult)\
                .then_inc(s_turn_v, 1)
            link(nc.vector.tensor_scalar(subg[:, :], par_of("subln"), 1.0 - LAM_INIT, None, ALU.mult))
            for gain, scale in (("dq", ATT["diff"]["scale"]), ("qn", ATT["mla"]["scale"]),
                                ("qpe", ATT["mla"]["scale"]), ("naq", ATT["na"]["scale"])):
                link(nc.vector.tensor_scalar(par_of(gain), par_of(gain), scale, None, ALU.mult))
            dve.wait_ge(s_cond, 1)
            nc.vector.tensor_tensor(condr[:, :, 2:4], cond[:, :].rearrange("p (c k) -> p k c", c=2),
                                    condr[:, :, 0:2].bitcast(F32), ALU.subtract).then_inc(s_cond, 1)
            dve.wait_ge(s_mod, 1)
            link(nc.vector.tensor_tensor(sml[:, 4:5], sml[:, 3:4], sml[:, 2:3], ALU.subtract))
            link(nc.vector.tensor_scalar(sml[:, 5:6], sml[:, 4:5], -LAM_INIT, None, ALU.add))
            for q in range(AHEAD):
                split_low(dve, q, q)

            def ada_copy(p, q):
                dve.wait_ge(used, q + 1)
                positive(dve, s_adat, p)
                nc.vector.tensor_copy(ada_row[0:4, :], ps[0:4, 6, :]).then_inc(s_adac, 1)

            def ada_bias(p, slabs=None):
                if slabs is None:
                    dve.wait_ge(s_adat, p + 1)
                else:
                    dve.wait_ge(s_asum, slabs)
                bias_of = par[:, bass.ds(p * 4, 4)]
                for c in range(2):
                    ins = nc.vector.tensor_tensor(
                        ada_flat[:, bass.ds(p * 4, 4), c],
                        ps[:, 7, 0:8].rearrange("p (m c) -> p m c", m=4)[:, :, c], bias_of, ALU.add)
                ins.then_inc(s_adav, 1)

            def scaled_gain(layer, n):
                sec = 1 if n == 0 else 4
                for c in range(2):
                    link(nc.vector.scalar_tensor_tensor(
                        out=gsc[:, layer, n, :, c], in0=ada[:, layer, sec * KD:(sec + 1) * KD, c], scalar=1.0,
                        in1=par_of("norm_gain", (2 * layer + n) * KD, KD), op0=ALU.add, op1=ALU.mult))

            for p in range(4):
                if p == 1:
                    for k in range(KD):
                        dve.wait_ge(s_turn, 3 + k)
                        nc.vector.tensor_copy(x_lat[:, k, :], ps[:, k % 2, 0:L]).then_inc(s_turn_v, 1)
                    dve.wait_ge(s_turn, 3 + KD)
                    nc.vector.tensor_copy(x_meta[:, :, :], ps[:, 4, 0:KD * N_META]
                                          .rearrange("p (k n) -> p k n", k=KD)).then_inc(s_turn_v, 1)
                split_next(dve, 4 * p, 2)
                ada_copy(p, 4 * p + 3)
                split_next(dve, 4 * p + 2, 2)
                if p >= 1:
                    ada_bias(p - 1)
            ada_bias(3)
            dve.wait_ge(s_adav, 4)
            scaled_gain(0, 0)
            norm_dve(dve, "fnet")
            for i in range(8 + 1):
                if i < 8:
                    dve.wait_ge(s_f1, i + 1)
                    if i >= 2:
                        dve.wait_ge(s_f2, i - 1)
                    nc.vector.tensor_copy(uv[:, i % 2, 2:4, :].rearrange("p t c -> p (t c)"),
                                          ps[:, 2 * (i % 2) + 1, :]).then_inc(s_f1v, 1)
                    q = 16 + 4 * i
                    split_next(dve, q, 2)
                    ada_copy(4 + i, q + 3)
                    split_next(dve, q + 2, 2)
                if i >= 1:
                    dve.wait_ge(s_f2a, i)
                    nc.vector.tensor_tensor(hl[:, i - 1, 0:NT], ps[:, 4 + (i - 1) % 2, :],
                                            hh[:, i - 1, 0:NT].bitcast(F32), ALU.subtract).then_inc(s_f2v, 1)
                if i < 8:
                    ada_bias(4 + i)
            dve.wait_ge(s_adav, 12)
            scaled_gain(0, 1)

            def add_gated(src, layer, sec, m, width, off, x, c):
                return nc.vector.scalar_tensor_tensor(out=x[:, m, :], in0=src[:, off:off + width],
                                                      scalar=ada[:, layer, sec * KD + m, c:c + 1],
                                                      in1=x[:, m, :], op0=ALU.mult, op1=ALU.add)

            for m, q in enumerate(FNET_OUT_Q):
                dve.wait_ge(s_opa, m + 1)
                add_gated(ex[:, m % 2, 0, :], 0, 2, m, L, 0, x_lat, 0)
                add_gated(ex[:, m % 2, 0, :], 0, 2, m, LC, L, x_ctx, 1).then_inc(s_x, 1)
                split_next(dve, q)
                if m in (3, 5):
                    split_next(dve, q + 1, 2)
                if m == 5:
                    ada_copy(12, q + 2)
            ada_bias(12)

            def up_times_gate(i, j, n, tile, q):
                dve.wait_ge(used, q + 1)
                dve.wait_ge(s_silu, tile + 2 * i + j + 1)
                nc.vector.tensor_tensor(big[:, bass.ds(i * (2 * n) + j * n, n)], nrm[:, j, 0:n],
                                        ps[:, 2 + j, 0:n], ALU.mult).then_inc(s_act, 1)

            def act_split(layer, k, at, n, q0):
                dve.wait_ge(s_ar, k + (layer * KF + 1))
                nc.vector.tensor_tensor(al[:, at % 2, 0:n], big[:, bass.ds(k * n, n)],
                                        ah[:, at % 2, 0:n].bitcast(F32), ALU.subtract).then_inc(s_as, 1)

            def ffn_out(layer, g0, n, norm):
                q0 = 2 * g0
                if layer == 0:
                    ada_bias(23, 22)
                    dve.wait_ge(s_adav, 24)
                    scaled_gain(1, 0)
                    scaled_gain(1, 1)
                for k in range(2):
                    act_split(layer, k + 2, k, n, q0)
                    split_next(dve, q0 + k)
                with dve.Fori(0, 2) as i:
                    for j in range(8):
                        act_split(layer, i * 8 + (j + 4), j, n, q0)
                        split_low(dve, i * 8 + (q0 + 2 + j + AHEAD), q0 + 2 + j + AHEAD)
                for k in range(18, 20):
                    act_split(layer, k + 2, k, n, q0)
                    split_next(dve, q0 + k)
                for m in range(KD):
                    if m < KD - 1:
                        dve.wait_ge(s_fin, layer * (KD - 1) + m + 1)
                    else:
                        dve.wait_ge(used, q0 + KF)
                    ins = add_gated(ps[:, m, :], layer, 5, m, L, 0, x_lat, 0)
                    if layer == 0:
                        ins = add_gated(ps[:, m, :], layer, 5, m, LC, L, x_ctx, 1)
                    ins.then_inc(s_x, 1)
                split_next(dve, q0 + 20)
                dve.wait_ge(s_x, (X_FFN1 if layer else X_FFN0) + KD)
                norm_dve(dve, norm)
                split_next(dve, q0 + 21)

            norm_dve(dve, "ffn0")
            q = 2 * G["ffn0_in"]

            def ada_products(i, h):
                slab, half = divmod(h, 2)
                acc, base = ada_acc[slab], i * 32 + 16 * slab
                dve.wait_ge(s_adal[h], i * 16 + 16)
                for k in range(4 * half, 4 * half + 4):
                    for c in range(2):
                        w, a = ada_buf[slab][:, k * 256:(k + 1) * 256], acc[:, c * 256:(c + 1) * 256]
                        weight = cond[:, c * KD + k:c * KD + k + 1]
                        if k == 0:
                            positive(dve, s_asum, i * 2 + (slab - 1))
                            ins = nc.vector.tensor_scalar(a, w, weight, None, ALU.mult)
                        else:
                            dve.wait_ge(s_am, base + (2 * k + c - 1))
                            ins = nc.vector.scalar_tensor_tensor(out=a, in0=w, scalar=weight, in1=a,
                                                                 op0=ALU.mult, op1=ALU.add)
                        ins.then_inc(s_am, 1)

            def ffn0_turn(i, at):
                for j in range(4):
                    split_low(dve, i * 4 + (q + j + AHEAD), at + j + AHEAD)
                    if j >= 2:
                        up_times_gate(i, j - 2, NT, 0, i * 4 + (q + j))
                    if j == 1 and (type(i) is not int or i >= 1):
                        ada_bias(i + 12, i * 2)
                    if j == 2 and type(i) is int and i == 10:
                        for k in range(2):
                            act_split(0, k, k, NT, 0)
                    ada_products(i, j)

            ffn0_turn(0, q)
            with dve.Fori(0, 4) as i:
                for t in range(2):
                    ffn0_turn(2 * i + 1 + t, q + 4 + 4 * t)
            for t in (9, 10):
                ffn0_turn(t, q + 4 * t)
            ffn_out(0, G["ffn0_out"], NT, "diff")
            units_dve(dve, link, DIFF_UNITS)
            att_dve(dve, link, mark, ATT["diff"])
            for m in range(KD):
                q = 2 * G["diff_out"] + m
                dve.wait_ge(used, q + 1)
                add_gated(ps[:, m % 4, :], 1, 2, m, L, 0, x_lat, 0).then_inc(s_x, 1)
                split_next(dve, q)
            dve.wait_ge(s_x, X_DIFF + KD)
            norm_dve(dve, "ffn1")
            q1 = 2 * G["ffn1_in"]

            def ffn1_turn(i, at):
                first = i * 4 + q1
                for j in range(4):
                    split_low(dve, first + (j + AHEAD), at + j + AHEAD)
                    if j >= 2:
                        up_times_gate(i, j - 2, L, KF, first + j)
                    if j == 2 and type(i) is int and i == 10:
                        for k in range(2):
                            act_split(1, k, k, L, 0)

            ffn1_turn(0, q1)
            with dve.Fori(0, 4) as i:
                for t in range(2):
                    ffn1_turn(2 * i + 1 + t, q1 + 4 + 4 * t)
            for t in (9, 10):
                ffn1_turn(t, q1 + 4 * t)
            ffn_out(1, G["ffn1_out"], L, "second")
            units_dve(dve, link, LAT_UNITS)
            norm_dve(dve, "lat")
            units_dve(dve, link, GATE_UNITS)
            units_dve(dve, link, MLA_UNITS)
            att_dve(dve, link, mark, ATT["mla"])
            units_dve(dve, link, NA_GATE_UNITS)
            units_dve(dve, link, NA_UNITS)
            att_dve(dve, link, mark, ATT["na"])
            split_next(dve, 2 * G["out2"], 16)
            dve.wait_ge(s_top, 1)
            nc.vector.tensor_copy(big[:, 512:D], ps[:, 1, :]).then_inc(s_fov, 1)
            dve.wait_ge(used, 2 * G["end"])
            nc.vector.tensor_copy(big[:, D + 512:2 * D], ps[:, 3, :]).then_inc(s_fov, 1)

        @block.tensor
        def _(pe):
            pe.wait_ge(s_rows, 48)
            nc.tensor.transpose(ps[:, 0, 0:N_ADA], rows[0:N_ADA, 0:P], T["ident"][0:N_ADA, 0:N_ADA])
            nc.tensor.transpose(ps[:, 0, N_ADA:N_ADA + N_PAR], rows[0:N_PAR, P:2 * P],
                                T["ident"][0:N_PAR, 0:N_PAR]).then_inc(s_turn, 1)
            pe.wait_ge(s_turn_v, 2)
            for c in range(2):
                ins = nc.tensor.matmul(ps[:, 3 - 2 * c, c:c + 1], T["ones"][64 * c:64 * c + 64, :],
                                       sml[64 * c:64 * c + 64, 0:1], start=True, stop=True)
            ins.then_inc(s_turn, 1)
            def ada_slab(at, half, q):
                pe.wait_ge(split, q + 2)
                for k in range(KD):
                    for w in (wh, wl):
                        ins = nc.tensor.matmul(
                            ps[0:4, 6, half * 256:(half + 1) * 256].rearrange("p (h e) -> p h e", h=2),
                            condr[:, k, :], w[:, at % SPLIT_SLOTS:at % SPLIT_SLOTS + 2, k * P:(k + 1) * P],
                            start=(k == 0 and w is wh), stop=(k == KD - 1 and w is wl))
                ins.then_inc(used, 2)

            def ada_turn(p):
                pe.wait_ge(s_adac, p + 1)
                positive(pe, s_adav, p)
                for m in range(4):
                    ins = nc.tensor.matmul(ps[:, 7, 2 * m:2 * m + 2], ada_row[0:4, m * P:(m + 1) * P],
                                           T["fold"][0:4, :], start=True, stop=True)
                ins.then_inc(s_adat, 1)

            def ada_pair(at, q, p):
                positive(pe, s_adac, p)
                ada_slab(at, 0, q)
                ada_slab(at + 2, 1, q + 2)

            pe.wait_ge(s_cond, 2)

            def turn_x():
                pe.wait_ge(s_xin, 48)
                pe.wait_ge(s_mod, 1)
                for k in range(KD):
                    if k >= 2:
                        pe.wait_ge(s_turn_a, k - 1)
                        pe.wait_ge(s_turn_v, k + 1)
                    for t in range(4):
                        ins = nc.tensor.transpose(ps[:, 2 * (t // 2) + k % 2, t % 2 * P:(t % 2 + 1) * P],
                                                  xin[:, t, k * P:(k + 1) * P], T["ident"])
                    ins.then_inc(s_turn, 1)
                meta = h32[0:N_META, 0:2, :].rearrange("p a b -> p (a b)")
                for k in range(KD):
                    ins = nc.tensor.transpose(ps[:, 4, k * N_META:(k + 1) * N_META],
                                              meta[:, k * P:(k + 1) * P], T["ident"][0:N_META, 0:N_META])
                ins.then_inc(s_turn, 1)

            for p in range(4):
                ada_pair(4 * p, 4 * p, p)
                if p == 1:
                    turn_x()
                if p >= 1:
                    ada_turn(p - 1)
                if p >= 2:
                    for k in range(4 * p - 8, 4 * p - 4):
                        norm_sum(pe, "fnet", k)
            ada_turn(3)
            pe.wait_ge(s_turn_v, 3 + KD)

            def fnet_inner(i):
                if i == 0:
                    pe.wait_ge(s_tab, 32)
                pe.wait_ge(s_h, i + 1)
                if i >= 2:
                    pe.wait_ge(s_f1a, i - 1)
                    pe.wait_ge(s_f1v, i - 1)
                for t in range(4):
                    ins = nc.tensor.matmul(ps[:, 2 * (i % 2) + t // 2, t % 2 * L:(t % 2 + 1) * L],
                                           h32[:, i, t * P:(t + 1) * P], dft_g, start=True, stop=True)
                ins.then_inc(s_f1, 1)

            def fnet_outer(i):
                pe.wait_ge(s_f1a, i + 1)
                pe.wait_ge(s_f1v, i + 1)
                if i >= 2:
                    pe.wait_ge(s_f2v, i - 1)
                for s in range(2):
                    for t in range(2):
                        for c, tb in enumerate((cos_l, nsin_l)):
                            ins = nc.tensor.matmul(ps[:, 4 + i % 2, s * L:(s + 1) * L],
                                                   uv[:, i % 2, 2 * s + t, c * P:(c + 1) * P], tb[:, t, :],
                                                   start=(t == 0 and c == 0), stop=(t == 1 and c == 1))
                ins.then_inc(s_f2, 1)

            fnet_inner(0)
            for i in range(8):
                ada_pair(16 + 4 * i, 16 + 4 * i, 4 + i)
                if i < 7:
                    fnet_inner(i + 1)
                fnet_outer(i)
                ada_turn(4 + i)
            pe.wait_ge(s_adav, 12)

            def fnet_out_between(m, q):
                if m in (3, 5):
                    if m == 3:
                        pe.wait_ge(s_adac, 12)
                    ada_slab(q + 1, m // 4, q + 1)
                if m == 6:
                    ada_turn(12)

            outproj_pe(pe, FNET_OUT_Q, NT, X_FNET, "ffn0", lambda k: pe.wait_ge(s_f2v, k + 1),
                       fnet_out_between)

            def ada_sum(i, slab):
                pe.wait_ge(s_am, i * 32 + 16 * (slab + 1))
                if slab == 0:
                    pe.wait_ge(s_adav, i + 13)
                for m in range(2):
                    for c in range(2):
                        at = 4 * slab + 2 * m + c
                        ins = nc.tensor.matmul(ps[:, 7, at:at + 1],
                                               ada_acc[slab][:, c * 256 + m * P:c * 256 + (m + 1) * P],
                                               T["ones"][:, 0:1], start=True, stop=True)
                ins.then_inc(s_asum, 1)

            def half_ffn(q, at, n, bank, h_base=None):
                order = [(m, k) for m in range(2) for k in range(KD)] if h_base is None else \
                    [(m, k) for k in range(KD) for m in range(2)]
                for m, k in order:
                    if k == 0:
                        pe.wait_ge(split, q + (m + 1))
                    if h_base is not None and m == 0:
                        pe.wait_ge(s_h, h_base + k + 1)
                    ins = product(ps[:, bank + m, 0:n], tile_of(wh, at + m, KD, P)[:, k, :],
                                  tile_of(wl, at + m, KD, P)[:, k, :], hh[:, k, 0:n], hl[:, k, 0:n], k == 0,
                                  k == KD - 1)
                    if k == KD - 1:
                        ins.then_inc(used, 1)

            def ffn_out_half(layer, q, at, k, n, first, last):
                pe.wait_ge(split, q + 1)
                pe.wait_ge(s_as, k + (layer * KF + 1))
                whv, wlv = wh[:, at % SPLIT_SLOTS, :], wl[:, at % SPLIT_SLOTS, :]
                for m in (0, 1, 4, 5, 6, 2, 3, 7) if first else range(KD):
                    c = slice(m * P, (m + 1) * P)
                    if first and layer == 0 and m == 3:
                        ada_sum(10, 1)
                    if first and layer == 0 and m == 7:
                        pe.wait_ge(s_adav, 24)
                    if first and m == 2:
                        pe.wait_ge(s_act, (layer + 1) * KF)
                    ins = product(ps[:, m, 0:n], whv[:, c], wlv[:, c], ah[:, at % 2, 0:n], al[:, at % 2, 0:n],
                                  first, last)
                ins.then_inc(used, 1)

            def ffn_out(layer, g0, n, norm):
                q0 = 2 * g0
                pe.wait_ge(s_silu, (layer + 1) * KF)
                for k in range(2):
                    ffn_out_half(layer, q0 + k, q0 + k, k, n, k == 0, False)
                with pe.Fori(0, 2) as i:
                    for j in range(8):
                        ffn_out_half(layer, i * 8 + (q0 + 2 + j), q0 + 2 + j, i * 8 + (2 + j), n, False, False)
                for k in range(18, 20):
                    ffn_out_half(layer, q0 + k, q0 + k, k, n, False, False)
                pe.wait_ge(split, q0 + KF)
                pe.wait_ge(s_as, (layer + 1) * KF)
                for m in range(KD):
                    c = slice(m * P, (m + 1) * P)
                    for k in (20, 21):
                        at = (q0 + k) % SPLIT_SLOTS
                        ins = product(ps[:, m, 0:n], wh[:, at, c], wl[:, at, c], ah[:, k % 2, 0:n],
                                      al[:, k % 2, 0:n], False, k == 21)
                    if m < KD - 1:
                        ins.then_inc(s_fin, 1)
                    else:
                        ins.then_inc(used, 2)
                    if m >= 2:
                        norm_sum(pe, norm, m - 2)
                norm_sum(pe, norm, KD - 2)
                norm_sum(pe, norm, KD - 1)

            q = 2 * G["ffn0_in"]

            def ffn0_turn(i, at, h_base=None):
                first = i * 4 + q
                positive(pe, s_silu, i * 2)
                half_ffn(first, at, NT, 0, h_base)
                if h_base is None:
                    ada_sum(i - 1, 1)
                positive(pe, s_act, i * 2)
                half_ffn(first + 2, at + 2, NT, 2)
                ada_sum(i, 0)

            ffn0_turn(0, q, BASE["ffn0"])
            with pe.Fori(0, 5) as i:
                for t in range(2):
                    ffn0_turn(2 * i + 1 + t, q + 4 + 4 * t)
            ffn_out(0, G["ffn0_out"], NT, "diff")
            pe.wait_ge(s_x, X_FFN0 + KD)
            units_pe(pe, DIFF_UNITS, BASE["diff"])
            pe.wait_ge(s_urdy, 16)
            pe.wait_ge(s_ucp, 16)
            steps = ATT["diff"]["steps"]
            diff_out = [2 * G["diff_out"] + m for m in range(KD)]

            def head_split(k):
                pe.wait_ge(s_os, k + 1)

            def diff_tail(i):
                if i in (steps + 1, steps + 3):
                    pe.wait_ge(s_ex, ATT["diff"]["maps"] * steps)
                    for m in range(i - steps - 1, i - steps + 1):
                        outproj_part(pe, diff_out[m], m, range(5), L, head_split)

            att_pe(pe, ATT["diff"], diff_tail)
            outproj_pe(pe, diff_out, L, X_DIFF, "ffn1", head_split,
                       before=[(m, k) for m in range(4) for k in range(5)])
            q1 = 2 * G["ffn1_in"]

            def ffn1_turn(i, at, h_base=None):
                first = i * 4 + q1
                positive(pe, s_silu, i * 2 + KF)
                half_ffn(first, at, L, 0, h_base)
                positive(pe, s_act, i * 2 + KF)
                half_ffn(first + 2, at + 2, L, 2)

            ffn1_turn(0, q1, BASE["ffn1"])
            with pe.Fori(0, 5) as i:
                for t in range(2):
                    ffn1_turn(2 * i + 1 + t, q1 + 4 + 4 * t)
            ffn_out(1, G["ffn1_out"], L, "second")
            pe.wait_ge(s_x, X_FFN1 + KD)
            units_pe(pe, LAT_UNITS, BASE["second"])
            unit_start(pe, GATE_UNITS[0], True)
            for k in range(KD):
                unit_tile(GATE_UNITS[0], k)
            norm_pe(pe, "lat")
            units_pe(pe, GATE_UNITS, before=1)
            pe.wait_ge(s_h, BASE["lat"] + 2)
            units_pe(pe, MLA_UNITS)
            pe.wait_ge(s_urdy, ROPED[-1]["r"] + 1)
            pe.wait_ge(s_unrm, max(u["h"] for u in MLA_UNITS if u["kind"] == "head") + 1)
            pe.wait_ge(s_ucp, max(u["c"] for u in MLA_UNITS if "c" in u) + 1)

            def mla_tail(i):
                a = ATT["mla"]
                if a["steps"] <= i < a["steps"] + 3:
                    pe.wait_ge(s_ex, a["m0"] + a["steps"])
                    u = NA_GATE_UNITS[i - a["steps"]]
                    unit_start(pe, u, True)
                    for k in range(KD):
                        unit_tile(u, k)

            att_pe(pe, ATT["mla"], mla_tail)
            units_pe(pe, NA_GATE_UNITS, before=3)
            units_pe(pe, NA_UNITS)
            pe.wait_ge(s_unrm, max(u["h"] for u in NA_UNITS if u["kind"] == "head") + 1)
            pe.wait_ge(s_ucp, NA_GATE_UNITS[-1]["c"] + 1)

            def out_half(k):
                q = 2 * G["out2"] + k
                pe.wait_ge(split, q + 1)
                if k >= 8:
                    pe.wait_ge(s_os, 16 + k - 8 + 1)
                if k == 1:
                    for t in range(2):
                        for m in range(KD):
                            nc.tensor.matmul(ps[:, 2 * t + m // 4, m % 4 * P:(m % 4 + 1) * P],
                                             x_lat[:, m, t * P:(t + 1) * P], T["ident"], start=False,
                                             stop=False, skip_group_check=True)
                for t in range(2):
                    at = (L2 + t * P) if k < 8 else t * P
                    a_h, a_l = hh[:, k % 8, at:at + P], hl[:, k % 8, at:at + P]
                    for c in range(2):
                        o = ps[:, 2 * t + c, :]
                        n = slice(c * 512, (c + 1) * 512)
                        w_h, w_l = wh[:, q % SPLIT_SLOTS, n], wl[:, q % SPLIT_SLOTS, n]
                        nc.tensor.matmul(o, a_h, w_h, start=(k == 0), stop=False, skip_group_check=True)
                        nc.tensor.matmul(o, a_h, w_l, start=False, stop=False, skip_group_check=True)
                        ins = nc.tensor.matmul(o, a_l, w_h, start=False, stop=(k == 15), skip_group_check=True)
                    if k == 15 and t == 0:
                        ins.then_inc(s_top, 1)
                ins.then_inc(used, 1)

            def na_tail(i):
                if i == ATT["na"]["steps"] + 1:
                    pe.wait_ge(s_ex, map_base)
                    out_half(0)

            att_pe(pe, ATT["na"], na_tail)
            for k in range(1, 16):
                out_half(k)


def kernel(**inputs):
    import concourse.bacc as _bacc
    from concourse.bass_utils import run_bass_kernel_spmd as _run

    def flat(name, *shape):
        return np.ascontiguousarray(inputs[name]).reshape(*shape)

    twice = lambda name: np.concatenate([flat(name, 1, 64)] * 2, 1)
    lam = flat("diff_lambda", 4, 64)
    params = np.concatenate([
        flat("norm_gain", 4 * KD, P), flat("fnet_b_out", KD, P), flat("norm_w_2", KD, P),
        flat("q_lat_norm_w_2", 2, P), flat("kv_lat_norm_w_2", 2, P), flat("diff_subln_gain", 1, P),
        flat("diff_q_gain", 1, P), flat("diff_k_gain", 1, P), flat("mla_qn_w_2", 1, P), flat("mla_kn_w_2", 1, P),
        twice("mla_qpe_w_2"), twice("mla_kpe_w_2"), twice("na_q_norm_w_2"), twice("na_k_norm_w_2"),
        np.concatenate([lam[0:1], lam[2:3]], 1), np.concatenate([lam[1:2], lam[3:4]], 1),
        flat("c", KD, P), flat("c_ctx", KD, P)], 0)
    tables = shape_tables()
    names = list(TABLE_COLS)
    kept = np.concatenate([tables[n] for n in names[:N_KEPT]], 1).astype(np.float32)
    fourier = np.concatenate([tables[n] for n in names[N_KEPT:]], 1).astype(np.float32)
    arrays = {
        "tables": kept, "fourier": fourier, "params": params, "b_ada": flat("b_ada", N_ADA, P),
        "meta_bias": flat("na_meta_bias_2", NA_HEADS * N_META),
        "rel_bias_rev": flat("na_rel_bias_2", -1)[::-1],
    }
    for name in ("x", "ctx", "w_ada", "ffn_w_in", "ffn_w_out", "fnet_w_out", "diff_w_in", "diff_w_out",
                 "meta_tokens_2", "w_in_2", "w_uq_2", "w_ukv_2", "w_out_2"):
        arrays[name] = inputs[name]
    arrays = {f"in_{n}": np.ascontiguousarray(a) for n, a in arrays.items()}

    nc = _bacc.Bacc("TRN2", target_bir_lowering=False, num_devices=1)
    d = {n[3:]: nc.dram_tensor(n, a.shape, mybir.dt.from_np(a.dtype), kind="ExternalInput").ap()
         for n, a in arrays.items()}
    out = nc.dram_tensor("out_0", (1, L, D), F32, kind="ExternalOutput").ap()
    build(nc, d, out)
    r = _run(nc, [arrays], core_ids=[0])
    return r.results[0]["out_0"]
```
